# Optimizing a Trainium2 kernel written in Bass

```python
import jax, jax.numpy as jnp
from jax import lax
import numpy as np

D_MODEL = 1024
BATCH = 1
SEQ = 256
DEPTH = 2

N_MEM = 256
HEAD_DIM = 64
ROT_DIM = HEAD_DIM // 4
ROPE_THETA = 500000.0
MEM_HEADS = 4
MEM_WIDTH = MEM_HEADS * HEAD_DIM
MIX_WIDTH = D_MODEL
PRIMARY_WIDTH = MIX_WIDTH - MEM_WIDTH
NSA_HEADS = PRIMARY_WIDTH // HEAD_DIM
NSA_KV_GROUPS = 3
NSA_GROUP_SIZE = NSA_HEADS // NSA_KV_GROUPS
NSA_KV_WIDTH = NSA_KV_GROUPS * HEAD_DIM
CMP_BLOCK = 32
CMP_STRIDE = 16
CMP_HIDDEN = 256
SEL_BLOCK = 64
SEL_TOPK = 16
WINDOW = 512
Q_BLOCK = 64
NSA_IN = PRIMARY_WIDTH + 6 * NSA_KV_WIDTH + 3 * NSA_HEADS + MEM_WIDTH
RWKV_HEADS = PRIMARY_WIDTH // HEAD_DIM
DECAY_LORA = 64
AAA_LORA = 64
GATE_LORA = 128
RWKV_SHIFT_W = 3 * PRIMARY_WIDTH + DECAY_LORA + AAA_LORA + GATE_LORA
RWKV_IN = RWKV_SHIFT_W + MEM_WIDTH
RWKV_GN_EPS = HEAD_DIM * 1e-5
FFN_HIDDEN = ((8 * D_MODEL + 3 * 256 - 1) // (3 * 256)) * 256
NORM_EPS = 1e-6
NEG = -1e30
FORCE = 1e6

kernel_name = 'hybrid_nsa_rwkv7_memory_trunk'

def rmsnorm(x, g):
    xf = x.astype(jnp.float32)
    y = xf * lax.rsqrt(jnp.mean(xf * xf, axis=-1, keepdims=True) + NORM_EPS)
    return (y * g.astype(jnp.float32)).astype(x.dtype)

def masked_softmax(s, mask):
    s = jnp.where(mask, s.astype(jnp.float32), NEG)
    m = jnp.max(s, axis=-1, keepdims=True)
    e = jnp.where(mask, jnp.exp(s - m), 0.0)
    return e / jnp.maximum(jnp.sum(e, axis=-1, keepdims=True), 1e-30)

def rope_tables(positions):
    inv = ROPE_THETA ** (-jnp.arange(0, ROT_DIM, 2, dtype=jnp.float32) / ROT_DIM)
    ang = positions.astype(jnp.float32)[..., None] * inv
    return jnp.cos(ang), jnp.sin(ang)

def apply_rope(t, cos, sin):
    half = ROT_DIM // 2
    c = cos[:, :, None, :].astype(t.dtype)
    s = sin[:, :, None, :].astype(t.dtype)
    t1, t2, rest = t[..., :half], t[..., half:ROT_DIM], t[..., ROT_DIM:]
    return jnp.concatenate([t1 * c - t2 * s, t1 * s + t2 * c, rest], axis=-1)

def nsa_mixer(proj, cos, sin, gate_b, cmp_pos_k, cmp_pos_v, cmp_k_w1, cmp_k_w2, cmp_v_w1, cmp_v_w2):
    B, S, _ = proj.shape
    G, Hg, Dh = NSA_KV_GROUPS, NSA_GROUP_SIZE, HEAD_DIM
    offs = list(np.cumsum([PRIMARY_WIDTH] + [NSA_KV_WIDTH] * 6)[:])
    q, kc_raw, vc_raw, ks, vs, kw, vw, gl = jnp.split(proj, offs, axis=-1)
    q = apply_rope(q.reshape(B, S, NSA_HEADS, Dh), cos, sin).reshape(B, S, G, Hg, Dh)
    ks = apply_rope(ks.reshape(B, S, G, Dh), cos, sin)
    kw = apply_rope(kw.reshape(B, S, G, Dh), cos, sin)
    vs = vs.reshape(B, S, G, Dh)
    vw = vw.reshape(B, S, G, Dh)
    gates = jax.nn.sigmoid(gl + gate_b).reshape(B, S, G, Hg, 3)

    n_cmp = (S - CMP_BLOCK) // CMP_STRIDE + 1
    cmp_idx = jnp.arange(n_cmp)[:, None] * CMP_STRIDE + jnp.arange(CMP_BLOCK)[None, :]
    cmp_end = cmp_idx[:, -1]

    def compress(t, pos_emb, w1, w2):
        blocks = t.reshape(B, S, G, Dh)[:, cmp_idx] + pos_emb[None, None, :, None, :]
        h = jax.nn.gelu(jnp.einsum('bnlgd,ldh->bngh', blocks, w1.reshape(CMP_BLOCK, Dh, CMP_HIDDEN)))
        return jnp.einsum('bngh,he->bnge', h, w2)

    kc = compress(kc_raw, cmp_pos_k, cmp_k_w1, cmp_k_w2)
    kc = apply_rope(kc, cos[:, cmp_end], sin[:, cmp_end])
    vc = compress(vc_raw, cmp_pos_v, cmp_v_w1, cmp_v_w2)

    n_sel = S // SEL_BLOCK
    n_topk = min(SEL_TOPK, n_sel)
    ksb = ks.reshape(B, n_sel, SEL_BLOCK, G, Dh).transpose(0, 3, 1, 2, 4)
    vsb = vs.reshape(B, n_sel, SEL_BLOCK, G, Dh).transpose(0, 3, 1, 2, 4)
    ratio = SEL_BLOCK // CMP_STRIDE
    pad_l = (CMP_BLOCK - CMP_STRIDE) // CMP_STRIDE
    n_taps = ratio + CMP_BLOCK // CMP_STRIDE - 1
    tap_w = jnp.asarray(np.array([
        max(0, min((o - pad_l) * CMP_STRIDE + CMP_BLOCK, SEL_BLOCK) - max((o - pad_l) * CMP_STRIDE, 0)) / CMP_STRIDE
        for o in range(n_taps)], dtype=np.float32))
    pad_r = ratio * (n_sel - 1) + n_taps - n_cmp - pad_l
    tap_idx = ratio * jnp.arange(n_sel)[:, None] + jnp.arange(n_taps)[None, :]

    kw_pad = jnp.pad(kw, ((0, 0), (WINDOW, 0), (0, 0), (0, 0)))
    vw_pad = jnp.pad(vw, ((0, 0), (WINDOW, 0), (0, 0), (0, 0)))

    n_qb = S // Q_BLOCK
    qb_all = q.reshape(B, n_qb, Q_BLOCK, G, Hg, Dh).swapaxes(0, 1)
    gb_all = gates.reshape(B, n_qb, Q_BLOCK, G, Hg, 3).swapaxes(0, 1)
    scale = HEAD_DIM ** -0.5
    b_idx = jnp.arange(B)[:, None, None, None]
    g_idx = jnp.arange(G)[None, :, None, None]
    jj = jnp.arange(n_sel)

    def block(args):
        qb, gb, blk = args
        t0 = blk * Q_BLOCK
        tq = t0 + jnp.arange(Q_BLOCK)
        s_c = jnp.einsum('bqghd,bngd->bghqn', qb, kc) * scale
        p_c = masked_softmax(s_c, cmp_end[None, :] <= tq[:, None])
        o_c = jnp.einsum('bghqn,bngd->bqghd', p_c.astype(vc.dtype), vc)
        imp = jnp.pad(p_c.sum(axis=2), ((0, 0), (0, 0), (0, 0), (pad_l, pad_r)))
        imp = jnp.einsum('bgqjt,t->bgqj', imp[..., tap_idx], tap_w)
        cur = tq // SEL_BLOCK
        forced = (jj[None, :] == 0) | (jj[None, :] == cur[:, None]) | (jj[None, :] == cur[:, None] - 1)
        score = jnp.where(forced, FORCE, imp)
        score = jnp.where(jj[None, :] <= cur[:, None], score, -FORCE)
        _, top = lax.top_k(score, n_topk)
        k_sel = ksb[b_idx, g_idx, top]
        v_sel = vsb[b_idx, g_idx, top]
        tok = top[..., None] * SEL_BLOCK + jnp.arange(SEL_BLOCK)
        m_s = (tok <= tq[:, None, None]).reshape(B, G, 1, Q_BLOCK, n_topk * SEL_BLOCK)
        s_s = jnp.einsum('bqghd,bgqkld->bghqkl', qb, k_sel).reshape(B, G, Hg, Q_BLOCK, n_topk * SEL_BLOCK) * scale
        p_s = masked_softmax(s_s, m_s).reshape(B, G, Hg, Q_BLOCK, n_topk, SEL_BLOCK)
        o_s = jnp.einsum('bghqkl,bgqkld->bqghd', p_s.astype(v_sel.dtype), v_sel)
        kwb = lax.dynamic_slice_in_dim(kw_pad, t0, Q_BLOCK + WINDOW, axis=1)
        vwb = lax.dynamic_slice_in_dim(vw_pad, t0, Q_BLOCK + WINDOW, axis=1)
        tk = t0 - WINDOW + jnp.arange(Q_BLOCK + WINDOW)
        m_w = (tk[None, :] <= tq[:, None]) & (tq[:, None] - tk[None, :] < WINDOW) & (tk[None, :] >= 0)
        s_w = jnp.einsum('bqghd,bkgd->bghqk', qb, kwb) * scale
        p_w = masked_softmax(s_w, m_w)
        o_w = jnp.einsum('bghqk,bkgd->bqghd', p_w.astype(vwb.dtype), vwb)
        out = gb[..., 0:1] * o_c + gb[..., 1:2] * o_s + gb[..., 2:3] * o_w
        return out.reshape(B, Q_BLOCK, PRIMARY_WIDTH)

    out = lax.map(block, (qb_all, gb_all, jnp.arange(n_qb)))
    return out.swapaxes(0, 1).reshape(B, S, PRIMARY_WIDTH)

def rwkv7_time_mix(proj, mu, w0, w2, a0, a2, g2, k_k, k_a, r_k, ln_g, ln_b):
    B, S, _ = proj.shape
    H, N = RWKV_HEADS, HEAD_DIM
    prev = jnp.pad(proj, ((0, 0), (1, 0), (0, 0)))[:, :-1]
    xs = proj + (prev - proj) * mu
    offs = list(np.cumsum([PRIMARY_WIDTH] * 3 + [DECAY_LORA, AAA_LORA]))
    r, k, v, wl, al, gl = jnp.split(xs, offs, axis=-1)
    w = -jax.nn.softplus(-(w0 + jnp.tanh(wl) @ w2)) - 0.5
    decay = jnp.exp(-jnp.exp(w.astype(jnp.float32)))
    a = jax.nn.sigmoid(a0 + al @ a2)
    g = jax.nn.sigmoid(gl) @ g2
    kk = (k * k_k).reshape(B, S, H, N).astype(jnp.float32)
    kk = kk * lax.rsqrt(jnp.maximum(jnp.sum(kk * kk, axis=-1, keepdims=True), 1e-24))
    k = k * (1.0 + (a - 1.0) * k_a)
    heads = lambda t: t.reshape(B, S, H, N).astype(jnp.float32)
    rh, kh, vh, ah = heads(r), heads(k), heads(v), heads(a)
    wh = decay.reshape(B, S, H, N)
    tmaj = lambda t: jnp.moveaxis(t, 1, 0)

    def step(state, inp):
        r_t, w_t, k_t, v_t, a_t, b_t = inp
        sa = jnp.einsum('bhij,bhj->bhi', state, a_t)
        state = state * w_t[:, :, None, :] + sa[..., None] * b_t[:, :, None, :] + v_t[..., None] * k_t[:, :, None, :]
        return state, jnp.einsum('bhij,bhj->bhi', state, r_t)

    s0 = jnp.zeros((B, H, N, N), jnp.float32)
    _, y = lax.scan(step, s0, (tmaj(rh), tmaj(wh), tmaj(kh), tmaj(vh), tmaj(-kk), tmaj(kk * ah)))
    y = jnp.moveaxis(y, 0, 1)
    mean = jnp.mean(y, axis=-1, keepdims=True)
    var = jnp.mean(jnp.square(y - mean), axis=-1, keepdims=True)
    y = ((y - mean) * lax.rsqrt(var + RWKV_GN_EPS)).reshape(B, S, PRIMARY_WIDTH) * ln_g + ln_b
    bonus = jnp.sum(rh * kh * r_k, axis=-1, keepdims=True) * vh
    y = y + bonus.reshape(B, S, PRIMARY_WIDTH)
    return (y * g).astype(proj.dtype)

def memory_attention(q_mem, mem_k, mem_v):
    B, S, _ = q_mem.shape
    q = q_mem.reshape(B, S, MEM_HEADS, HEAD_DIM)
    s = jnp.einsum('bshd,bmhd->bhsm', q, mem_k).astype(jnp.float32) * (HEAD_DIM ** -0.5)
    p = jax.nn.softmax(s, axis=-1)
    return jnp.einsum('bhsm,bmhd->bshd', p.astype(mem_v.dtype), mem_v).reshape(B, S, MEM_WIDTH)

def setup_inputs(seed: int = 0) -> dict:
    key = jax.random.key(seed)
    keys = iter(jax.random.split(key, 48))
    nrm = lambda shape, scale: jax.random.normal(next(keys), shape, jnp.float32) * scale
    gain = lambda shape: 1.0 + nrm(shape, 0.05)
    n_nsa = (DEPTH + 1) // 2
    n_rwkv = DEPTH // 2
    D = D_MODEL
    x = nrm((BATCH, SEQ, D), 1.0)
    mem = nrm((BATCH, N_MEM, D), 1.0)
    positions = jax.random.randint(next(keys), (BATCH, 1), 0, 4096, dtype=jnp.int32) + jnp.arange(SEQ, dtype=jnp.int32)[None, :]
    return {
        'x': x,
        'mem': mem,
        'positions': positions,
        'mem_norm_g': gain((D,)),
        'w_mem_kv': nrm((D, 2 * MEM_WIDTH), D ** -0.5),
        'pre_mix_g': gain((DEPTH, D)),
        'post_mix_g': gain((DEPTH, D)),
        'pre_ffn_g': gain((DEPTH, D)),
        'post_ffn_g': gain((DEPTH, D)),
        'w_out': nrm((DEPTH, MIX_WIDTH, D), MIX_WIDTH ** -0.5),
        'w_ffn_in': nrm((DEPTH, D, 2 * FFN_HIDDEN), D ** -0.5),
        'w_ffn_out': nrm((DEPTH, FFN_HIDDEN, D), FFN_HIDDEN ** -0.5),
        'nsa_w_in': nrm((n_nsa, D, NSA_IN), D ** -0.5),
        'nsa_gate_b': nrm((n_nsa, 3 * NSA_HEADS), 0.1),
        'nsa_cmp_pos_k': nrm((n_nsa, CMP_BLOCK, HEAD_DIM), 0.02),
        'nsa_cmp_pos_v': nrm((n_nsa, CMP_BLOCK, HEAD_DIM), 0.02),
        'nsa_cmp_k_w1': nrm((n_nsa, CMP_BLOCK * HEAD_DIM, CMP_HIDDEN), (CMP_BLOCK * HEAD_DIM) ** -0.5),
        'nsa_cmp_k_w2': nrm((n_nsa, CMP_HIDDEN, HEAD_DIM), CMP_HIDDEN ** -0.5),
        'nsa_cmp_v_w1': nrm((n_nsa, CMP_BLOCK * HEAD_DIM, CMP_HIDDEN), (CMP_BLOCK * HEAD_DIM) ** -0.5),
        'nsa_cmp_v_w2': nrm((n_nsa, CMP_HIDDEN, HEAD_DIM), CMP_HIDDEN ** -0.5),
        'rwkv_w_in': nrm((n_rwkv, D, RWKV_IN), D ** -0.5),
        'rwkv_mu': jax.random.uniform(next(keys), (n_rwkv, RWKV_SHIFT_W), jnp.float32),
        'rwkv_w0': jax.random.uniform(next(keys), (n_rwkv, PRIMARY_WIDTH), jnp.float32, -5.0, -0.5),
        'rwkv_w2': nrm((n_rwkv, DECAY_LORA, PRIMARY_WIDTH), 0.5 * DECAY_LORA ** -0.5),
        'rwkv_a0': nrm((n_rwkv, PRIMARY_WIDTH), 0.5),
        'rwkv_a2': nrm((n_rwkv, AAA_LORA, PRIMARY_WIDTH), AAA_LORA ** -0.5),
        'rwkv_g2': nrm((n_rwkv, GATE_LORA, PRIMARY_WIDTH), GATE_LORA ** -0.5),
        'rwkv_k_k': 0.85 + nrm((n_rwkv, PRIMARY_WIDTH), 0.05),
        'rwkv_k_a': gain((n_rwkv, PRIMARY_WIDTH)),
        'rwkv_r_k': nrm((n_rwkv, RWKV_HEADS, HEAD_DIM), 0.1),
        'rwkv_ln_g': gain((n_rwkv, PRIMARY_WIDTH)),
        'rwkv_ln_b': nrm((n_rwkv, PRIMARY_WIDTH), 0.02),
    }

def reference(x, mem, positions, mem_norm_g, w_mem_kv, pre_mix_g, post_mix_g, pre_ffn_g, post_ffn_g,
              w_out, w_ffn_in, w_ffn_out, nsa_w_in, nsa_gate_b, nsa_cmp_pos_k, nsa_cmp_pos_v,
              nsa_cmp_k_w1, nsa_cmp_k_w2, nsa_cmp_v_w1, nsa_cmp_v_w2, rwkv_w_in, rwkv_mu, rwkv_w0,
              rwkv_w2, rwkv_a0, rwkv_a2, rwkv_g2, rwkv_k_k, rwkv_k_a, rwkv_r_k, rwkv_ln_g, rwkv_ln_b):
    B, S, _ = x.shape
    M = mem.shape[1]
    mkv = rmsnorm(mem, mem_norm_g) @ w_mem_kv
    mem_k = mkv[..., :MEM_WIDTH].reshape(B, M, MEM_HEADS, HEAD_DIM)
    mem_v = mkv[..., MEM_WIDTH:].reshape(B, M, MEM_HEADS, HEAD_DIM)
    cos, sin = rope_tables(positions)
    h = x
    for i in range(DEPTH):
        j = i // 2
        hn = rmsnorm(h, pre_mix_g[i])
        if i % 2 == 0:
            proj = hn @ nsa_w_in[j]
            prim = nsa_mixer(proj[..., :NSA_IN - MEM_WIDTH], cos, sin, nsa_gate_b[j], nsa_cmp_pos_k[j],
                             nsa_cmp_pos_v[j], nsa_cmp_k_w1[j], nsa_cmp_k_w2[j], nsa_cmp_v_w1[j], nsa_cmp_v_w2[j])
        else:
            proj = hn @ rwkv_w_in[j]
            prim = rwkv7_time_mix(proj[..., :RWKV_SHIFT_W], rwkv_mu[j], rwkv_w0[j], rwkv_w2[j], rwkv_a0[j],
                                  rwkv_a2[j], rwkv_g2[j], rwkv_k_k[j], rwkv_k_a[j], rwkv_r_k[j],
                                  rwkv_ln_g[j], rwkv_ln_b[j])
        mo = memory_attention(proj[..., -MEM_WIDTH:], mem_k, mem_v)
        mix = jnp.concatenate([prim, mo], axis=-1) @ w_out[i]
        h = h + rmsnorm(mix, post_mix_g[i])
        hn = rmsnorm(h, pre_ffn_g[i])
        gu = hn @ w_ffn_in[i]
        ff = (jax.nn.silu(gu[..., :FFN_HIDDEN]) * gu[..., FFN_HIDDEN:]) @ w_ffn_out[i]
        h = h + rmsnorm(ff, post_ffn_g[i])
    return h


_drawn_inputs = setup_inputs


def setup_inputs(seed=0):
    import zlib

    import numpy as np

    out = dict(_drawn_inputs(seed))
    spreads = {}
    factors = {'mem_norm_g': 2.876,
     'nsa_cmp_pos_k': 39.31,
     'rwkv_ln_b': 19.454,
     'nsa_gate_b': 3.31,
     'nsa_cmp_pos_v': 6.023,
     'rwkv_w2': 4.183,
     'rwkv_k_k': 19.789,
     'rwkv_k_a': 2.682,
     'rwkv_ln_g': 3.358}
    for name, (base, spread) in spreads.items():
        noise = np.random.default_rng([zlib.crc32(name.encode()), seed]).standard_normal(out[name].shape)
        drawn = base * np.exp(spread * noise) if base else spread * noise
        out[name] = __import__('jax').numpy.asarray(drawn.astype(out[name].dtype))
    for name, factor in factors.items():
        out[name] = (out[name] * factor).astype(out[name].dtype)
    return out
```

```python
from contextlib import ExitStack

import numpy as np

import concourse.bass as bass
from concourse import mybir

ALU = mybir.AluOpType
ACT = mybir.ActivationFunctionType
AX = mybir.AxisListType
F32 = mybir.dt.float32
F32R = mybir.dt.float32r
I32 = mybir.dt.int32

P = 128
D = 1024
SEQ = 256
TT = SEQ // P
KD = D // P
HD = 64
MEM_HEADS = 4
MEM_W = MEM_HEADS * HD
PRIM = D - MEM_W
HEADS = PRIM // HD
GROUPS = 3
KVW = GROUPS * HD
ROT = HD // 4
HALF = ROT // 2
ROPE_THETA = 500000.0
CMP_BLOCK = 32
CMP_STRIDE = 16
CMP_HIDDEN = 256
NCMP = (SEQ - CMP_BLOCK) // CMP_STRIDE + 1
CJ = CMP_BLOCK * HD // P
GATES = 3 * HEADS
LORA = 64
GLORA = 128
SHIFT_W = 3 * PRIM + 2 * LORA + GLORA
NSA_IN = PRIM + 6 * KVW + GATES + MEM_W
RWKV_IN = SHIFT_W + MEM_W
FFN = ((8 * D + 3 * 256 - 1) // (3 * 256)) * 256
FC = 256
NFC = FFN // FC
KF = FFN // P
FT = PRIM // P
EPS = 1e-6
GN_EPS = HD * 1e-5
NEG = -1e30
SCALE = float(HD) ** -0.5
KAPPA = float(np.exp(-0.5))
BLK = 16

O_KC, O_VC, O_KS, O_VS, O_KW, O_VW, O_G, O_MQ = (
    PRIM, PRIM + KVW, PRIM + 2 * KVW, PRIM + 3 * KVW, PRIM + 4 * KVW, PRIM + 5 * KVW,
    PRIM + 6 * KVW, PRIM + 6 * KVW + GATES)

A_MEMG, A_PREMIX, A_PREFFN, A_POSK, A_POSV = 0, 8, 24, 40, 56
NA = 72
B_MU, B_W0, B_A0, B_KK, B_KA, B_RK, B_LNG, B_LNB = 0, 20, 26, 32, 38, 44, 50, 56
NB = 62

N_VEC = 13
MAGIC = 12582912.0
TURN = [6.28125, 2029.0 / 2**20, 2 * np.pi - 6.28125 - 2029.0 / 2**20]

RAW, SPL = 5, 3
PIECE = 2048


def weight_pieces(w_mem_kv, nsa_w_in, w1k, w1v, w_out, w_ffn_in, w_ffn_out, rwkv_w_in):
    out, start = [], {}

    def kt_view(w):
        return w.rearrange("(k p) n -> p k n", p=P)

    start["mem"] = len(out)
    for hf in range(2):
        out.append(kt_view(w_mem_kv)[:, 4 * hf:4 * hf + 4, :])
    start["nsa"] = len(out)
    for c in range(0, NSA_IN, 512):
        for hf in range(2):
            out.append(kt_view(nsa_w_in)[:, 4 * hf:4 * hf + 4, c:min(c + 512, NSA_IN)])
    start["cmp"] = len(out)
    for w in (w1k, w1v):
        for hf in range(2):
            out.append(kt_view(w)[:, 8 * hf:8 * hf + 8, :])
    for layer in range(2):
        if layer == 1:
            start["rwkv"] = len(out)
            for c in RWKV_ORDER:
                out.append(kt_view(rwkv_w_in)[:, :, 256 * c:256 * c + 256])
        start["out", layer] = len(out)
        for k in range(0, KD, 2):
            out.append(kt_view(w_out[layer])[:, k:k + 2, :])
        start["up", layer] = len(out)
        for c in range(NFC):
            for hf in range(2):
                out.append((kt_view(w_ffn_in[layer][:, FC * c:FC * c + FC])[:, 4 * hf:4 * hf + 4, :],
                            kt_view(w_ffn_in[layer][:, FFN + FC * c:FFN + FC * c + FC])[:, 4 * hf:4 * hf + 4, :]))
        start["down", layer] = len(out)
        for k in range(0, KF, 2):
            out.append(kt_view(w_ffn_out[layer])[:, k:k + 2, :])
    return out, start


RWKV_ORDER = [9, 3, 4, 5, 0, 1, 2, 6, 7, 8, 10]


def trunk(nc, x, mem, positions, mem_norm_g, w_mem_kv, pre_mix_g, post_mix_g, pre_ffn_g, post_ffn_g,
          w_out, w_ffn_in, w_ffn_out, nsa_w_in, nsa_gate_b, nsa_cmp_pos_k, nsa_cmp_pos_v,
          nsa_cmp_k_w1, nsa_cmp_k_w2, nsa_cmp_v_w1, nsa_cmp_v_w2, rwkv_w_in, rwkv_mu, rwkv_w0,
          rwkv_w2, rwkv_a0, rwkv_a2, rwkv_g2, rwkv_k_k, rwkv_k_a, rwkv_r_k, rwkv_ln_g, rwkv_ln_b, out):
    pieces, first = weight_pieces(w_mem_kv, nsa_w_in[0], nsa_cmp_k_w1[0], nsa_cmp_v_w1[0], w_out,
                                  w_ffn_in, w_ffn_out, rwkv_w_in[0])
    NPIECES = len(pieces)

    with ExitStack() as ctx:
        ARENA = (nc.sbuf_base + 127) // 128 * 128
        ROOM = nc.sbuf_usable_end - ARENA
        base = [0]

        def at(offset, name, shape, dt=F32):
            n = 4 * int(np.prod(shape[1:]))
            assert offset + n <= ROOM, (name, offset, n)
            return nc.alloc_sbuf_tensor_at(name, shape, dt, offset=ARENA + offset)

        def put(name, shape, dt=F32):
            n = 4 * int(np.prod(shape[1:]))
            t = at(base[0], name, shape, dt)
            base[0] += (n + 31) // 32 * 32
            return t

        raw = put("w_raw", [P, RAW, PIECE])
        w_hi = put("w_hi", [P, SPL, PIECE], F32R)
        w_lo = put("w_lo", [P, SPL, PIECE], F32R)
        h = put("h", [P, TT, D])
        o_xh = base[0]
        xh = put("x_hi", [P, KD, SEQ], F32R)
        o_xl = base[0]
        xl = put("x_lo", [P, KD, SEQ], F32R)
        o_hn = base[0]
        hn = put("hn", [P, TT, D])
        gain = put("post_gain", [P, D])
        mkv = put("mem_kv", [P, TT, 2 * MEM_W])
        mkT = put("mem_kT", [P, 2, SEQ])
        mqT = put("mem_qT", [P, 2, SEQ])
        ident = put("ident", [P, P])
        cmask = put("causal_mask", [P, SEQ])
        bcmask = put("block_mask", [P, NCMP * TT])
        rowok = put("row_has_block", [P, TT])
        colA = put("cols_a", [P, NA])
        colB = put("cols_b", [P, NB])
        cst = put("consts", [P, 8])
        bones = put("head_blocks", [P, P])
        ssq = put("ssq", [P, 4])
        ss2 = put("ss2", [P, TT])
        rms = put("rms", [P, TT])
        rin = put("rinv", [P, TT])
        mx = put("row_max", [P, 2, 2])
        nbias = put("neg_max", [P, 2, 2])
        rsum = put("row_sum", [P, 2, 2])
        coef = put("row_coef", [P, 2, 2])
        PH = base[0]

        o = PH
        pr = at(o, "nsa_proj", [P, TT, NSA_IN])
        mh = at(o, "mem_hi", [P, KD, SEQ], F32R)
        ml = at(o + 8192, "mem_lo", [P, KD, SEQ], F32R)
        o += 4 * TT * NSA_IN
        dup = at(o, "kv_twice", [P, TT, 12, P])
        pcT = at(o, "block_probsT", [NCMP, TT, HEADS, P])
        o += 12288
        qT = at(o, "qT", [P, FT, SEQ])
        o_kT = o + 6144
        kT = at(o_kT, "kT", [P, 2 * GROUPS, SEQ])
        o += 12288
        KC = at(o, "cmp_inT", [P, 2 * GROUPS, SEQ])
        sc = at(o, "block_scores", [P, TT, HEADS, NCMP])
        o += 6144
        KB = CJ * GROUPS * NCMP
        kph = [at(b, f"cmp_blocks_hi{k}", [P, CJ, GROUPS * NCMP], F32R) for k, b in enumerate((o, o_kT))]
        kpl = [at(b + 4 * KB, f"cmp_blocks_lo{k}", [P, CJ, GROUPS * NCMP], F32R) for k, b in enumerate((o, o_kT))]
        sm = at(o, "scores", [P, 2, 2, SEQ])
        pT = at(o + 4096, "probsT", [P, 2, 4, P])
        o += 8192
        kpf = at(o_hn, "cmp_blocks", [P, CJ, GROUPS * NCMP])
        rowsA = at(o_kT, "rows_a", [NA, P])
        rowsB = at(o_kT + 512, "rows_b", [NB, P])
        oo = o
        w2k = at(oo, "cmp_k_w2", [P, 2, HD]); oo += 512
        w2v = at(oo, "cmp_v_w2", [P, 2, HD]); oo += 512
        hc = at(o_hn + 3072, "cmp_hidden", [GROUPS * NCMP, 2, CMP_HIDDEN])
        hcT = at(o_hn + 5120, "cmp_hiddenT", [P, 4, GROUPS * NCMP])
        kcs = at(o_hn + 5856, "kc_tok", [GROUPS * NCMP, HD])
        kcd = at(o_hn + 6112, "kc_twice", [GROUPS * NCMP, 2, HD])
        kcT = at(oo, "kcT", [P, GROUPS * NCMP]); oo += 192
        vcs = at(oo, "vc_tok", [NCMP, GROUPS, HD]); oo += 768
        gates = at(oo, "gates", [P, TT, GATES]); oo += 288
        gateb = at(oo, "gate_bias", [P, GATES]); oo += 160
        posi = at(oo, "pos_int", [P, 3], I32); oo += 32
        posf = at(oo, "pos", [P, 3]); oo += 32
        invf = at(oo, "inv_freq", [P, 2, HALF]); oo += 64
        ang = at(oo, "angle", [P, 3, 2, HALF]); oo += 192
        turns = at(oo, "turns", [P, 3, 2, HALF]); oo += 192
        trig = at(oo, "trig", [P, 3, 2, HALF]); oo += 192
        cmx = at(oo, "block_max", [P, HEADS]); oo += 64
        csum = at(oo, "block_sum", [P, HEADS]); oo += 64
        ccf = at(oo, "block_coef", [P, HEADS]); oo += 64
        rt = at(o_hn + 6656, "rope_tmp", [P, 4 * 48])
        rtq = at(PH + 4 * TT * NSA_IN + 12288, "rope_tmp_q", [P, 4, TT, HEADS, HALF])

        hh = at(PH, "hidden_hi", [P, KF, SEQ], F32R)
        hl = at(PH + 4 * KF * SEQ, "hidden_lo", [P, KF, SEQ], F32R)
        o = PH + 8 * KF * SEQ
        sg = at(o, "silu", [P, TT, FC])
        hid = at(o + 2048, "hidden", [P, TT, FC])

        A6 = 4 * FT * SEQ
        C6 = 4 * FT * TT * (P + 1) + 16
        rT, k_T, aT, kkT, gT = (at(PH + A6 * i, n, [P, FT, SEQ]) for i, n in enumerate(
            ("rT", "kT_rwkv", "aT", "kkT", "out_gateT")))
        y_tok = at(PH + 3 * A6, "y_tok", [P, TT, PRIM])
        o = PH + 5 * A6
        o_v = o
        vT = at(o, "vT", [P, FT, SEQ])
        eP = at(o + A6, "decay_from_mid", [P, FT, TT, P + 1])
        o += A6 + C6
        cs = at(o, "decay_sums", [P, FT, TT, P + 1])
        eN = at(o + C6, "decay_to_mid", [P, FT, TT, P])
        lwT = at(o + C6, "log_decay", [P, FT, SEQ])
        tk = at(o, "v_b_k_tok", [P, 4, PRIM])
        y_fin = at(o, "y_scaled", [P, FT, SEQ])
        o += A6 + C6
        eP_sq = at(o, "kk_squares", [P, FT, SEQ])
        art = at(o, "a_rT", [P, FT, TT, 2, P])
        o += 2 * A6
        shb = [at(o + 2080 * i, f"shift_in{i}", [P, 2, SEQ + 1]) for i in range(2)]
        dmask = at(o, "delta_masks", [P, 6, P])
        o += 2 * 2080
        st = at(o, "state_T", [P, FT, HD])
        mid = at(o + 1536, "mid_sums", [P, FT, TT])
        sfac = at(o + 1600, "state_scale", [P, FT])
        gst = [at(o + 1632 + 64 * i, f"gn_stat{i}", [P, HEADS]) for i in range(3)]
        lora = at(o_hn, "lora_w2_a2", [P, PRIM])
        wg = at(o_hn + 6144, "lora_in", [P, 2, SEQ])
        g2 = at(o_hn + 3072, "gate_w2", [P, PRIM])
        gsq = at(o_hn + 4096, "gn_squares", [P, PRIM])

        def pair_buffers(s):
            if s == 0:
                spots = [o_xh, o_xh + 2048, o_xh + 4096, o_xl, o_xl + 2048, o_xl + 4096, o_hn]
            else:
                spots = [o_v + 2048 * i for i in range(6)] + [o_hn + 2048]
            n = f"_{'ab'[s]}"
            half = spots[6]
            return dict(
                DA=at(spots[0], "D_Arb" + n, [P, 2, 2, P]), KR=at(spots[1], "Aak_Ark" + n, [P, 2, 2, P]),
                T=at(spots[2], "Dt_Et" + n, [P, 2, 2, P]), S2=at(spots[3], "pow2" + n, [P, 2, 2, P]),
                S4=at(spots[4], "pow4" + n, [P, 2, 2, P]), 
                R=at(spots[5], "R" + n, [P, 2, P]), S8=at(half, "pow8" + n, [P, 2, P]),
                U=[at(half + 1024 + 512 * i, f"U{i}" + n, [P, 2, HD]) for i in range(2)])

        PB = [pair_buffers(s) for s in range(2)]
        sm1 = at(o_xh, "scores_1", [P, 2, 2, SEQ])
        pT1 = at(o_xl, "probsT_1", [P, 2, 4, P])
        SM, PT = [sm, sm1], [pT, pT1]

        psum = ctx.enter_context(nc.psum_tensor("ps", [P, 8, 512], F32))

        def sem(name):
            return ctx.enter_context(nc.semaphore(name))

        landed = [sem(f"w_landed{i}") for i in range(RAW)]
        hi_done = sem("w_hi_done")
        lo_done = sem("w_lo_done")
        used = sem("w_used")
        in_x = sem("in_x")
        in_mem = sem("in_mem")
        in_vec = sem("in_vec")
        in_small = sem("in_small")
        in_gain = sem("in_gain")
        stored = sem("stored")
        consts = sem("consts_ready")
        s_pool = sem("pool_chain")
        s_dve = sem("dve_chain")
        s_act = sem("act_chain")
        n_sqA, n_sqD, n_rms, n_inv = sem("n_sqA"), sem("n_sqD"), sem("n_rms"), sem("n_inv")
        n_scA, n_scD, n_tp, n_hi, n_lo = sem("n_scA"), sem("n_scD"), sem("n_tp"), sem("n_hi"), sem("n_lo")
        vec_tp, vec_ev = sem("vec_tp"), sem("vec_ev")
        tok_mm, tok_evA, tok_evD = sem("tok_mm"), sem("tok_evA"), sem("tok_evD")
        trig_r, trig_s = sem("trig_arg"), sem("trig_done")
        dup_c, dup_k, roped_k, roped_q = sem("dup_cmp"), sem("dup_keys"), sem("roped_keys"), sem("roped_q")
        tp0, tp0A, tp0D = sem("turned"), sem("turned_A"), sem("turned_D")
        gl_s, gate_s = sem("gate_logits"), sem("gates_ready")
        kp_f, kp_hi, kp_lo = sem("kp_f"), sem("kp_hi"), sem("kp_lo")
        c_gelu, c_tp, c_ht, c_w2, c_kv, c_kd, c_kt, c_ktv = (
            sem("c_gelu"), sem("c_tp"), sem("c_ht"), sem("c_w2"), sem("c_kv"), sem("c_kd"), sem("c_kt"), sem("c_ktv"))
        b_sc, b_sub, b_exp, b_p, b_tp, b_pt = (
            sem("b_sc"), sem("b_sub"), sem("b_exp"), sem("b_p"), sem("b_tp"), sem("b_pt"))
        a_sc, a_max, a_exp, a_coef, a_p, a_tp, a_ptA, a_ptD, a_pv, a_hi, a_lo = (
            sem("a_sc"), sem("a_max"), sem("a_exp"), sem("a_coef"), sem("a_p"), sem("a_tp"), sem("a_ptA"),
            sem("a_ptD"), sem("a_pv"), sem("a_hi"), sem("a_lo"))
        p_sq, p_tmp, p_ss, p_rms, p_h = (
            sem("p_sq"), sem("p_tmp"), sem("p_ss"), sem("p_rms"), sem("p_h"))
        up_mm, up_silu, up_mul, up_tp, up_hi, up_lo = (
            sem("up_mm"), sem("up_silu"), sem("up_mul"), sem("up_tp"), sem("up_hi"), sem("up_lo"))

        in_lora, fm_out, shifted, shb_zero = sem("in_lora"), sem("fm_out"), sem("shifted"), sem("shift_zero")
        l_act, z_mm, a_mm, z_ev, a_ev = sem("lora_act"), sem("z_mm"), sem("a_mm"), sem("z_ev"), sem("a_ev")
        g_mm, g_ev, cs_ok, ex_ok = sem("g_mm"), sem("g_ev"), sem("sums_ok"), sem("exps_ok")
        kk_ok, sq_ok, ss_mm, ss_ev, ss_rt, kn_ok = (
            sem("kk_ok"), sem("sq_ok"), sem("ss_mm"), sem("ss_ev"), sem("ss_rt"), sem("kn_ok"))
        r_ok, rk_ok, bo_mm, bo_ev, bk_ok, ar_ok, tk_mm, tk_ev = (
            sem("rdecay_ok"), sem("rk_ok"), sem("bo_mm"), sem("bo_ev"), sem("bk_ok"), sem("ar_ok"), sem("tk_mm"), sem("tk_ev"))
        dm_ok, sf_ok = sem("delta_masks"), sem("scale_ok")
        pm = [sem("pair_pe_a"), sem("pair_pe_b")]
        pv = [sem("pair_dve_a"), sem("pair_dve_b")]
        pa = [sem("pair_act_a"), sem("pair_act_b")]
        pp = [sem("pair_pool_a"), sem("pair_pool_b")]
        gn_sub, gn_sq, gn_var, gn_rt, gn_ok = sem("gn_sub"), sem("gn_sq"), sem("gn_var"), sem("gn_rt"), sem("gn_ok")
        y_mm, y_sc, y_add, y_fin_ok, y_hi, y_lo = (
            sem("y_mm"), sem("y_sc"), sem("y_add"), sem("y_fin"), sem("y_hi"), sem("y_lo"))

        block = ctx.enter_context(nc.Block())

        def raw_view(i):
            src = pieces[i]
            if isinstance(src, tuple):
                return raw[:, i % RAW, :].rearrange("p (k c n) -> p k c n", k=4, c=2)
            return raw[:, i % RAW, 0:src.shape[1] * src.shape[2]].rearrange("p (k n) -> p k n", k=src.shape[1])

        def size(i):
            src = pieces[i]
            return PIECE if isinstance(src, tuple) else src.shape[1] * src.shape[2]

        def kt_of(buf, i, k):
            src = pieces[i]
            n = 512 if isinstance(src, tuple) else src.shape[2]
            return buf[:, i % SPL, k * n:(k + 1) * n]

        land_value, count = [], [0] * RAW
        for i in range(NPIECES):
            count[i % RAW] += 32 if isinstance(pieces[i], tuple) else 16
            land_value.append(count[i % RAW])

        GEMM_ACC = [2, 3, 6, 7]
        NORM_COL = [A_MEMG, A_PREMIX, A_PREFFN, A_PREMIX + 8, A_PREFFN + 8]

        @block.sync
        def _(sp):
            def load_piece(i):
                if i >= RAW:
                    sp.wait_ge(lo_done, i - RAW + 1)
                src = pieces[i]
                if isinstance(src, tuple):
                    for c in range(2):
                        sp.dma_start(raw_view(i)[:, :, c, :], src[c]).then_inc(landed[i % RAW], 16)
                else:
                    sp.dma_start(raw_view(i), src).then_inc(landed[i % RAW], 16)

            sp.dma_start(hn[:], mem[0].rearrange("(t p) d -> p t d", p=P)).then_inc(in_mem, 16)
            sp.dma_start(h[:], x[0].rearrange("(t p) d -> p t d", p=P)).then_inc(in_x, 16)
            for i in range(NPIECES):
                load_piece(i)
            for t in range(TT):
                sp.wait_ge(p_h, 2 * 3 + t + 1)
                sp.dma_start(out[0, t * P:(t + 1) * P, :], h[:, t, :]).then_inc(stored, 16)
            sp.wait_ge(stored, 16 * TT)


        def rows_of(head):
            return slice(HD * (head % 2), HD * (head % 2) + HD)

        nsa_units = [(f, e, t, "nsa") for f in range(FT) for e in range(2) for t in range(TT)]
        mem_units = [(f, e, t, "mem") for f in range(FT, KD) for e in range(2) for t in range(TT)]
        UNITS = [nsa_units + mem_units, mem_units]
        UBASE = [0, len(nsa_units + mem_units)]
        FBASE = [0, KD - FT]
        LAG_T, LAG_V = 2, 3

        def branches(unit):
            return (2, unit[2] + 1) if unit[3] == "nsa" else (1, TT)

        TURNS = ([("dup", j) for j in range(6)] + [("q", f) for f in range(FT)]
                 + [("dup", j) for j in range(6, 12)] + [("mq", 0), ("mq", 1), ("mk", 0), ("mk", 1)])
        NTURN = len(TURNS) // 2

        PE_STEPS = ["gram", "sq2", "r2", "sq4", "r3", "sq8", "j", "f", "z", "f2", "uj", "f4", "uf", "uf2", "uf4", "y", "s"]
        DVE_STEPS = ["Dt", "D", "Et", "K", "R2", "R3", "J", "Z", "U1", "U2", "U3", "U"]
        ACT_STEPS = ["S2", "S4", "S8", "F", "F2", "F4", "Y", "S"]
        NPAIR = FT // 2
        ROUNDS = TT * NPAIR

        def step(steps, d, name):
            last = 1 if steps[-1] in ("s", "S") else 0
            return len(steps) * d - last * max(0, d - NPAIR) + steps.index(name) + 1

        @block.gpsimd
        def _(pool):
            chain = [0]

            def link(ins):
                chain[0] += 1
                ins.then_inc(s_pool, 1)
                pool.wait_ge(s_pool, chain[0])

            def rows(dst, r, src):
                n = int(np.prod(src.shape)) // P
                pat = {1: "(r p) -> r p", 2: "a b -> (a b)"}
                v = src if len(src.shape) == 1 else src.rearrange(pat[2])
                pool.dma_start(dst[r:r + n, :], v.rearrange(pat[1], p=P)).then_inc(in_vec, 16)

            loads = [(rowsA, A_MEMG, mem_norm_g), (rowsA, A_PREMIX, pre_mix_g), (rowsA, A_PREFFN, pre_ffn_g),
                     (rowsA, A_POSK, nsa_cmp_pos_k[0]), (rowsA, A_POSV, nsa_cmp_pos_v[0]),
                     (rowsB, B_MU, rwkv_mu[0]), (rowsB, B_W0, rwkv_w0[0]), (rowsB, B_A0, rwkv_a0[0]),
                     (rowsB, B_KK, rwkv_k_k[0]), (rowsB, B_KA, rwkv_k_a[0]), (rowsB, B_RK, rwkv_r_k[0]),
                     (rowsB, B_LNG, rwkv_ln_g[0]), (rowsB, B_LNB, rwkv_ln_b[0])]
            for item in loads:
                rows(*item)
            assert len(loads) == N_VEC

            link(pool.memset(posi[:], 0))
            pool.dma_start(posi[:, 0:TT], positions[0].rearrange("(t p) -> p t", p=P),
                           allow_slow_non_contiguous=True).then_inc(in_small, 16)
            for g in range(GROUPS):
                pool.dma_start(posi[g * NCMP:(g + 1) * NCMP, TT:TT + 1],
                               positions[:, CMP_BLOCK - 1:SEQ:CMP_STRIDE].rearrange("a n -> n a"),
                               allow_slow_non_contiguous=True).then_inc(in_small, 16)
            pool.dma_start(gateb[:], nsa_gate_b.to_broadcast([P, GATES])).then_inc(in_small, 16)
            for dst, src in ((w2k, nsa_cmp_k_w2), (w2v, nsa_cmp_v_w2)):
                pool.dma_start(dst[:], src[0].rearrange("(k p) n -> p k n", p=P)).then_inc(in_small, 16)

            link(pool.memset(ident[:], 0.0))
            pool.affine_select(ident[:], ident[:], [[-1, P]], ALU.not_equal, 1.0, base=0,
                               channel_multiplier=1).then_inc(consts, 1)
            pool.memset(cst[:, 0:1], EPS).then_inc(consts, 1)
            pool.memset(cst[:, 1:2], GN_EPS).then_inc(consts, 1)
            for i in range(HALF):
                pool.memset(invf[:, :, i:i + 1], float(np.float32(ROPE_THETA) ** np.float32(-i / HALF))).then_inc(consts, 1)
            link(pool.memset(cmask[:], 0.0))
            pool.affine_select(cmask[:, P:], cmask[:, P:], [[-1, P]], ALU.is_ge, NEG, base=0,
                               channel_multiplier=1).then_inc(consts, 1)
            link(pool.memset(bcmask[:], 0.0))
            bc = bcmask[:].rearrange("p (t n) -> p t n", t=TT)
            pool.affine_select(bc, bc, [[P, TT], [-CMP_STRIDE, NCMP]], ALU.is_ge, NEG,
                               base=1 - CMP_BLOCK, channel_multiplier=1).then_inc(consts, 1)
            link(pool.memset(rowok[:], 1.0))
            pool.affine_select(rowok[:], rowok[:], [[P, TT]], ALU.is_ge, 0.0, base=1 - CMP_BLOCK,
                               channel_multiplier=1).then_inc(consts, 1)

            def load_gain(m):
                if m:
                    pool.wait_ge(p_tmp, 4 * m)
                g = (post_mix_g, post_ffn_g)[m % 2]
                pool.dma_start(gain[:], g[m // 2:m // 2 + 1, :].to_broadcast([P, D])).then_inc(in_gain, 16)

            link(pool.memset(bones[:], 1.0))
            v = bones[:].rearrange("p (b c) -> p b c", c=HD)
            link(pool.affine_select(v, v, [[-HD, 2], [0, HD]], ALU.is_ge, 0.0, base=0, channel_multiplier=1))
            pool.affine_select(v, v, [[HD, 2], [0, HD]], ALU.is_ge, 0.0, base=HD - 1, channel_multiplier=-1).then_inc(consts, 1)
            pool.memset(cst[:, 2:3], 1.0).then_inc(consts, 1)
            load_gain(0)

            pool.wait_ge(tok_evA, 4)
            pool.wait_ge(tok_evD, 4)
            for t in range(TT):
                for c in range(2):
                    pool.tensor_copy(dup[:, t, 0:6, HD * c:HD * c + HD],
                                     pr[:, t, O_KC:O_KS].rearrange("p (j d) -> p j d", d=HD)).then_inc(dup_c, 1)
            pool.wait_ge(roped_k, 2)
            for b, col in enumerate((O_KS, O_KW)):
                for t in range(TT):
                    for c in range(2):
                        pool.tensor_copy(dup[:, t, 6 + 3 * b:9 + 3 * b, HD * c:HD * c + HD],
                                         pr[:, t, col:col + KVW].rearrange("p (j d) -> p j d", d=HD)).then_inc(dup_k, 1)

            def scale_probs(layer):
                for i, unit in enumerate(UNITS[layer]):
                    u = UBASE[layer] + i
                    nbr, nk = branches(unit)
                    pool.wait_ge(a_coef, u + 1)
                    for b in range(nbr):
                        v = SM[layer][:, u % 2, b, 0:nk * P]
                        ins = pool.tensor_scalar(v, v, coef[:, u % 2, b:b + 1], None, ALU.mult)
                    ins.then_inc(a_p, 1)

            scale_probs(0)
            load_gain(1)
            pool.wait_ge(n_tp, 16)
            pool.dma_start(lora[0:LORA, :], rwkv_w2[0]).then_inc(in_lora, 16)
            pool.dma_start(lora[LORA:P, :], rwkv_a2[0]).then_inc(in_lora, 16)
            pool.dma_start(g2[:], rwkv_g2[0]).then_inc(in_lora, 16)
            load_gain(2)
            pool.wait_ge(p_h, 4)
            for i in range(2):
                pool.memset(shb[i][:, :, 0:1], 0.0).then_inc(shb_zero, 1)
            pool.memset(cs[:, :, :, 0:1], 0.0).then_inc(shb_zero, 1)
            pool.wait_ge(kk_ok, 1)
            pool.tensor_tensor(eP_sq[:], kkT[:], kkT[:], ALU.mult).then_inc(sq_ok, 1)
            scale_probs(1)
            pool.wait_ge(shifted, 10)
            link(pool.memset(dmask[:], 1.0))
            up = [[1, P]]
            m = [dmask[:, i, :] for i in range(6)]
            for i in (0, 2):
                ins = pool.affine_select(m[i], m[i], up, ALU.is_ge, 0.0, base=-1, channel_multiplier=-1)
            for i in (1, 3):
                pool.affine_select(m[i], m[i], up, ALU.is_ge, 0.0, base=0, channel_multiplier=-1)
            for i in (4, 5):
                ins = pool.affine_select(m[i], m[i], [[-1, P]], ALU.is_ge, 0.0, base=-1, channel_multiplier=1)
            link(ins)
            for i in (0, 4):
                v = m[i].rearrange("p (b c) -> p b c", c=BLK)
                link(pool.affine_select(v, v, [[-BLK, P // BLK], [0, BLK]], ALU.is_ge, 0.0, base=0, channel_multiplier=1))
                link(pool.affine_select(v, v, [[BLK, P // BLK], [0, BLK]], ALU.is_ge, 0.0, base=BLK - 1, channel_multiplier=-1))
            pool.tensor_tensor(m[5], m[5], m[4], ALU.subtract).then_inc(dm_ok, 1)
            for d in range(ROUNDS):
                for s in range(2):
                    b = PB[s]
                    pool.wait_ge(pv[s], step(DVE_STEPS, d, "D"))
                    pool.tensor_tensor(b["R"][:], b["DA"][:, :, 0, :], ident[:].unsqueeze(1).to_broadcast([P, 2, P]),
                                       ALU.add).then_inc(pp[s], 1)
            for j in range(FT // 2):
                pool.wait_ge(y_sc, j + 1)
                pool.tensor_tensor(y_fin[:, 2 * j:2 * j + 2, :], y_fin[:, 2 * j:2 * j + 2, :], rT[:, 2 * j:2 * j + 2, :],
                                   ALU.add).then_inc(y_add, 1)
            load_gain(3)

        @block.tensor
        def _(pe):
            def three(dst, ah, al, bh, bl, start, stop):
                pe.matmul(dst, ah, bh, start=start, stop=False)
                pe.matmul(dst, ah, bl, start=False, stop=False)
                return pe.matmul(dst, al, bh, start=False, stop=stop)

            def norm(n):
                pe.wait_ge(n_scA, n + 1)
                pe.wait_ge(n_scD, n + 1)
                for b in range(KD // 2):
                    for j in range(2):
                        for t in range(TT):
                            k = 2 * b + j
                            ins = pe.transpose(psum[:, b, j * SEQ + t * P:j * SEQ + (t + 1) * P],
                                               hn[:, t, k * P:(k + 1) * P], ident[:])
                    ins.then_inc(n_tp, 1)

            def token_gemm(g, ah, al):
                i0 = first["mem"] if g == 0 else first["nsa"] + 2 * (g - 1)
                n = pieces[i0].shape[2]
                for hf in range(2):
                    pe.wait_ge(lo_done, i0 + hf + 1)
                    for t in range(TT):
                        if hf == 0 and g >= 2:
                            pe.wait_ge((tok_evA, tok_evD)[t], g - 1)
                        for k in range(4):
                            kk = 4 * hf + k
                            ins = three(psum[:, 4 + 2 * (g % 2) + t, 0:n], ah[:, kk, t * P:(t + 1) * P],
                                        al[:, kk, t * P:(t + 1) * P], kt_of(w_hi, i0 + hf, k), kt_of(w_lo, i0 + hf, k),
                                        start=kk == 0, stop=kk == KD - 1)
                        if hf == 1 and t == 0:
                            ins.then_inc(tok_mm, 1)
                    ins.then_inc(used, 1)

            def turn(k):
                if k >= 4:
                    pe.wait_ge((tp0A, tp0D)[k % 2], (k - 4) // 2 + 1)
                for j in range(2):
                    kind, n = TURNS[2 * k + j]
                    for t in range(TT):
                        src = {"dup": lambda: dup[:, t, n, :], "q": lambda: pr[:, t, n * P:(n + 1) * P],
                               "mq": lambda: pr[:, t, O_MQ + n * P:O_MQ + (n + 1) * P],
                               "mk": lambda: mkv[:, t, n * P:(n + 1) * P]}[kind]()
                        ins = pe.transpose(psum[:, k % 4, j * SEQ + t * P:j * SEQ + (t + 1) * P], src, ident[:])
                ins.then_inc(tp0, 1)

            def cmp_gemm():
                for kv in range(2):
                    pe.wait_ge(kp_hi, kv + 1)
                    pe.wait_ge(kp_lo, kv + 1)
                    for hf in range(2):
                        i = first["cmp"] + 2 * kv + hf
                        pe.wait_ge(lo_done, i + 1)
                        for j in range(CJ // 2):
                            jj = CJ // 2 * hf + j
                            ins = three(psum[0:GROUPS * NCMP, 4 + kv, 0:CMP_HIDDEN], kph[kv][:, jj, :], kpl[kv][:, jj, :],
                                        kt_of(w_hi, i, j), kt_of(w_lo, i, j), start=jj == 0, stop=jj == CJ - 1)
                        ins.then_inc(used, 1)

            def scores(layer, i):
                unit = UNITS[layer][i]
                u = UBASE[layer] + i
                f, e, t, kind = unit
                nbr, nk = branches(unit)
                if u >= 2:
                    pe.wait_ge(a_max, u - 1)
                r = rows_of(e)
                for b in range(nbr):
                    if kind == "nsa":
                        lhs, rhs = qT[r, f, t * P:(t + 1) * P], kT[r, 3 * b + f // 2, 0:nk * P]
                    else:
                        lhs, rhs = mqT[r, f - FT, t * P:(t + 1) * P], mkT[r, f - FT, :]
                    ins = pe.matmul(psum[:, u % 2, b * SEQ:b * SEQ + nk * P], lhs, rhs, start=True, stop=True)
                ins.then_inc(a_sc, 1)

            def probs_turn(layer, i):
                unit = UNITS[layer][i]
                u = UBASE[layer] + i
                nbr, nk = branches(unit)
                pe.wait_ge(a_p, u + 1)
                if u >= 2:
                    pe.wait_ge((a_ptA, a_ptD)[u % 2], (u - 2) // 2 + 1)
                for b in range(nbr):
                    for k in range(nk):
                        ins = pe.transpose(psum[:, 2 + u % 2, (b * nk + k) * P:(b * nk + k + 1) * P],
                                           SM[layer][:, u % 2, b, k * P:(k + 1) * P], ident[:])
                ins.then_inc(a_tp, 1)

            def values(layer, i):
                unit = UNITS[layer][i]
                u = UBASE[layer] + i
                f, e, t, kind = unit
                nbr, nk = branches(unit)
                head = 2 * f + e
                pe.wait_ge((a_ptA, a_ptD)[u % 2], u // 2 + 1)
                fi = f + FBASE[layer]
                if e == 0 and t == 0 and (f >= 2 or layer):
                    pe.wait_ge(a_lo, fi - 1)
                dst = psum[rows_of(e), 6 + f % 2, t * P:(t + 1) * P]
                todo = []
                for b in range(nbr):
                    for k in range(nk):
                        if kind == "nsa":
                            c = (O_VS, O_VW)[b] + HD * (f // 2)
                            lhs = pr[:, k, c:c + HD]
                        else:
                            c = MEM_W + HD * (head - HEADS)
                            lhs = mkv[:, k, c:c + HD]
                        todo.append((lhs, PT[layer][:, u % 2, b * nk + k, :]))
                if kind == "nsa":
                    todo.append((vcs[:, f // 2, :], pcT[:, t, head, :]))
                for n, (lhs, rhs) in enumerate(todo):
                    ins = pe.matmul(dst, lhs, rhs, start=n == 0, stop=n == len(todo) - 1)
                ins.then_inc(a_pv, 1)

            def attention(layer):
                n = len(UNITS[layer])
                for s in range(n + LAG_V):
                    if s < n:
                        scores(layer, s)
                    if 0 <= s - LAG_T < n:
                        probs_turn(layer, s - LAG_T)
                    if 0 <= s - LAG_V < n:
                        values(layer, s - LAG_V)

            def full_gemm(i0, kt_n, ah, al):
                for j in range(kt_n // 2):
                    pe.wait_ge(lo_done, i0 + j + 1)
                    for t in range(TT):
                        for nh in range(2):
                            for k in range(2):
                                kk = 2 * j + k
                                c = slice(512 * nh, 512 * nh + 512)
                                ins = three(psum[:, GEMM_ACC[2 * t + nh], :], ah[:, kk, t * P:(t + 1) * P],
                                            al[:, kk, t * P:(t + 1) * P], kt_of(w_hi, i0 + j, k)[:, c],
                                            kt_of(w_lo, i0 + j, k)[:, c], start=kk == 0, stop=kk == kt_n - 1)
                    ins.then_inc(used, 1)

            def ffn(layer):
                up0, tp0_ = 2 * NFC * layer, NFC * layer

                def hidden_turn(c):
                    pe.wait_ge(up_mul, up0 + 2 * c + 2)
                    if c >= 2:
                        pe.wait_ge(up_lo, tp0_ + c - 1)
                    for j in range(2):
                        for t in range(TT):
                            ins = pe.transpose(psum[:, 4 + c % 2, j * SEQ + t * P:j * SEQ + (t + 1) * P],
                                               hid[:, t, j * P:(j + 1) * P], ident[:])
                    ins.then_inc(up_tp, 1)

                for c in range(NFC):
                    for hf in range(2):
                        i = first["up", layer] + 2 * c + hf
                        pe.wait_ge(lo_done, i + 1)
                        for t in range(TT):
                            if hf == 0 and c >= 2:
                                pe.wait_ge(up_mul, up0 + 2 * (c - 2) + t + 1)
                            for k in range(4):
                                kk = 4 * hf + k
                                ins = three(psum[:, 2 * (c % 2) + t, :], xh[:, kk, t * P:(t + 1) * P],
                                            xl[:, kk, t * P:(t + 1) * P], kt_of(w_hi, i, k), kt_of(w_lo, i, k),
                                            start=kk == 0, stop=kk == KD - 1)
                            if hf == 1 and t == 0:
                                ins.then_inc(up_mm, 1)
                        ins.then_inc(used, 1)
                        if hf == 0 and c:
                            hidden_turn(c - 1)
                hidden_turn(NFC - 1)
                full_gemm(first["down", layer], KF, hh, hl)

            pe.wait_ge(consts, 1)
            pe.wait_ge(in_vec, 16 * N_VEC)
            pe.transpose(psum[:, 7, 0:NA], rowsA[:], ident[0:NA, 0:NA])
            pe.transpose(psum[:, 7, P:P + NB], rowsB[:], ident[0:NB, 0:NB]).then_inc(vec_tp, 1)
            norm(0)
            pe.wait_ge(n_hi, 4)
            pe.wait_ge(n_lo, 4)
            token_gemm(0, mh, ml)
            norm(1)
            pe.wait_ge(n_lo, 8)
            for g in range(1, 5):
                token_gemm(g, xh, xl)
            pe.wait_ge(dup_c, 4)
            for k in range(3):
                turn(k)
            token_gemm(5, xh, xl)
            cmp_gemm()
            pe.wait_ge(roped_q, 1)
            for k in range(3, 5):
                turn(k)
            pe.wait_ge(c_gelu, 2)
            pe.wait_ge(tok_evA, 6)
            n = GROUPS * NCMP
            for kv in range(2):
                for k in range(2):
                    ins = pe.transpose(psum[:, 6, (2 * kv + k) * n:(2 * kv + k + 1) * n],
                                       hc[:, kv, k * P:(k + 1) * P], ident[0:n, 0:n])
            ins.then_inc(c_tp, 1)
            turn(5)
            pe.wait_ge(dup_k, 8)
            turn(6)
            pe.wait_ge(c_ht, 1)
            pe.wait_ge(tok_evD, 6)
            pe.wait_ge(in_small, 16 * 7)
            for k in range(2):
                pe.matmul(psum[0:n, 7, 0:HD], hcT[:, k, :], w2k[:, k, :], start=k == 0, stop=k == 1)
            for g in range(GROUPS):
                for k in range(2):
                    ins = pe.matmul(psum[0:NCMP, 7, HD * (g + 1):HD * (g + 2)], hcT[:, 2 + k, NCMP * g:NCMP * (g + 1)],
                                    w2v[:, k, :], start=k == 0, stop=k == 1)
            ins.then_inc(c_w2, 1)
            for k in range(7, NTURN):
                turn(k)
            pe.wait_ge(c_kd, 1)
            pe.transpose(psum[:, 7, 256:256 + n], kcd[:].rearrange("p c d -> p (c d)"), ident[0:n, 0:n]).then_inc(c_kt, 1)
            pe.wait_ge(c_ktv, 1)
            pe.wait_ge(tp0A, (NTURN + 1) // 2)
            pe.wait_ge(tp0D, NTURN // 2)
            for t in range(TT):
                for head in range(HEADS):
                    r = rows_of(head)
                    g = head // (HEADS // GROUPS)
                    ins = pe.matmul(psum[:, 4 + 2 * t + head % 2, head // 2 * NCMP:(head // 2 + 1) * NCMP], qT[r, head // 2, t * P:(t + 1) * P],
                                    kcT[r, g * NCMP:(g + 1) * NCMP], start=True, stop=True)
                ins.then_inc(b_sc, 1)
            for t in range(TT):
                pe.wait_ge(b_p, TT)
                for q in range(3):
                    for i in range(4):
                        head = 4 * q + i
                        ins = pe.transpose(psum[0:NCMP, 3 * t + q, i * P:(i + 1) * P], sc[:, t, head, :], ident[:])
                    ins.then_inc(b_tp, 1)
            pe.wait_ge(b_pt, 6)
            attention(0)
            pe.wait_ge(a_lo, KD)
            full_gemm(first["out", 0], KD, xh, xl)
            norm(2)
            pe.wait_ge(n_lo, 12)
            ffn(0)

            norm(3)
            pe.wait_ge(n_lo, 16)

            def strip(q):
                i = first["rwkv"] + q
                pe.wait_ge(lo_done, i + 1)
                if q >= 2:
                    pe.wait_ge(fm_out, q - 1)
                for j in range(2):
                    for k in range(KD):
                        c = slice(P * j, P * j + P)
                        ins = three(psum[:, 4 + q % 2, j * SEQ:(j + 1) * SEQ], kt_of(w_hi, i, k)[:, c],
                                    kt_of(w_lo, i, k)[:, c], xh[:, k, :], xl[:, k, :], start=k == 0, stop=k == KD - 1)
                ins.then_inc(used, 1)

            strip(0)
            strip(1)
            pe.wait_ge(in_lora, 48)
            pe.wait_ge(l_act, 2)
            pe.wait_ge(shifted, 1)
            pe.wait_ge(a_lo, KD)
            for j in range(FT // 2):
                if j:
                    pe.wait_ge(z_ev, j)
                for i in range(2):
                    f = 2 * j + i
                    ins = pe.matmul(psum[:, 6, i * SEQ:(i + 1) * SEQ], lora[0:LORA, f * P:(f + 1) * P], wg[0:LORA, 0, :],
                                    start=True, stop=True)
                ins.then_inc(z_mm, 1)
                if j:
                    pe.wait_ge(a_ev, j)
                for i in range(2):
                    f = 2 * j + i
                    ins = pe.matmul(psum[:, 7, i * SEQ:(i + 1) * SEQ], lora[LORA:P, f * P:(f + 1) * P], wg[LORA:P, 0, :],
                                    start=True, stop=True)
                ins.then_inc(a_mm, 1)
            strip(2)
            for j in range(FT // 2):
                for i in range(2):
                    f = 2 * j + i
                    ins = pe.matmul(psum[:, j, i * SEQ:(i + 1) * SEQ], g2[:, f * P:(f + 1) * P], wg[:, 1, :], start=True, stop=True)
                ins.then_inc(g_mm, 1)
            strip(3)
            strip(4)
            pe.wait_ge(sq_ok, 1)
            pe.wait_ge(g_ev, 3)
            for j in range(FT // 2):
                for i in range(2):
                    ins = pe.matmul(psum[:, j, i * SEQ:(i + 1) * SEQ], bones[:], eP_sq[:, 2 * j + i, :], start=True, stop=True)
                ins.then_inc(ss_mm, 1)
            for q in range(5, 9):
                strip(q)
            pe.wait_ge(rk_ok, 1)
            pe.wait_ge(ss_ev, 3)
            for j in range(FT // 2):
                for i in range(2):
                    ins = pe.matmul(psum[:, j, i * SEQ:(i + 1) * SEQ], bones[:], rT[:, 2 * j + i, :], start=True, stop=True)
                ins.then_inc(bo_mm, 1)
            strip(9)
            strip(10)
            pe.wait_ge(bk_ok, 1)
            pe.wait_ge(shifted, 10)
            pe.wait_ge(bo_ev, 3)
            for f in range(FT):
                if f >= 2:
                    pe.wait_ge(tk_ev, f - 1)
                for i, src in enumerate((vT[:, f, 0:P], vT[:, f, P:SEQ], aT[:, f, 0:P], k_T[:, f, 0:P])):
                    ins = pe.transpose(psum[:, 3 * (f % 2), i * P:(i + 1) * P], src, ident[:])
                ins.then_inc(tk_mm, 1)
            pe.wait_ge(tk_ev, 6)
            pe.wait_ge(fm_out, 11)
            attention(1)

            def gemm2(s, bank, pairs):
                for kind, (lhs, rhs) in enumerate(pairs):
                    for e in range(2):
                        ins = pe.matmul(psum[:, bank, (2 * kind + e) * P:(2 * kind + e + 1) * P], lhs(e), rhs(e), start=True, stop=True)
                ins.then_inc(pm[s], 1)

            def applied(s, bank, lhs, rhs):
                for e in range(2):
                    ins = pe.matmul(psum[:, bank, e * HD:(e + 1) * HD], lhs(e), rhs(e), start=True, stop=True)
                ins.then_inc(pm[s], 1)

            pe.wait_ge(a_lo, KD + KD - FT)
            pe.wait_ge(ar_ok, 1)
            for d in range(ROUNDS):
                t = d // NPAIR

                def V(s, n):
                    pe.wait_ge(pv[s], step(DVE_STEPS, d, n))

                def A(s, n):
                    pe.wait_ge(pa[s], step(ACT_STEPS, d, n))

                for name in PE_STEPS[:len(PE_STEPS) - t]:
                    for s in range(2):
                        b, B0 = PB[s], 4 * s
                        f = 2 * (d % NPAIR) + s
                        D, Arb = (lambda e: b["DA"][:, e, 0, :]), (lambda e: b["DA"][:, e, 1, :])
                        Aak, Ark = (lambda e: b["KR"][:, e, 0, :]), (lambda e: b["KR"][:, e, 1, :])
                        Dt, Et = (lambda e: b["T"][:, 0, e, :]), (lambda e: b["T"][:, 1, e, :])
                        p2, p2t = (lambda e: b["S2"][:, 0, e, :]), (lambda e: b["S2"][:, 1, e, :])
                        p4, p4t = (lambda e: b["S4"][:, 0, e, :]), (lambda e: b["S4"][:, 1, e, :])
                        p8, R = (lambda e: b["S8"][:, e, :]), (lambda e: b["R"][:, e, :])
                        U0, U1 = (lambda e: b["U"][0][:, e, :]), (lambda e: b["U"][1][:, e, :])
                        vv = lambda e: tk[:, t, f * P + e * HD:f * P + (e + 1) * HD]
                        if name == "gram":
                            if d:
                                pe.wait_ge(pv[s], step(DVE_STEPS, d - 1, "U"))
                                pe.wait_ge(pa[s], step(ACT_STEPS, d - 1, "S" if d <= NPAIR else "Y"))
                            for e in range(2):
                                r = rows_of(e)
                                tok = slice(t * P, (t + 1) * P)
                                ar = art[r, f, t, :, :].rearrange("p c n -> p (c n)")
                                pe.matmul(psum[:, B0 + e, 0:2 * P], aT[r, f, tok], ar, start=True, stop=True)
                                pe.matmul(psum[:, B0 + e, 2 * P:4 * P], k_T[r, f, tok], ar, start=True, stop=True)
                                ins = pe.matmul(psum[:, B0 + 2 + e, 0:P], art[r, f, t, 0, :], aT[r, f, tok], start=True, stop=True)
                            ins.then_inc(pm[s], 1)
                        elif name == "sq2":
                            V(s, "Et")
                            gemm2(s, B0 + 2, [(Dt, D), (D, Dt)])
                        elif name == "r2":
                            A(s, "S2")
                            pe.wait_ge(pp[s], d + 1)
                            gemm2(s, B0 + 3, [(p2t, R)])
                        elif name == "sq4":
                            V(s, "K")
                            gemm2(s, B0, [(p2t, p2), (p2, p2t)])
                        elif name == "r3":
                            A(s, "S4")
                            V(s, "R2")
                            gemm2(s, B0 + 1, [(p4t, R)])
                        elif name == "sq8":
                            gemm2(s, B0 + 2, [(p4, p4t)])
                        elif name == "j":
                            A(s, "S8")
                            V(s, "R3")
                            gemm2(s, B0 + 3, [(p8, R)])
                        elif name == "f":
                            V(s, "J")
                            gemm2(s, B0, [(Et, R), (R, Et)])
                        elif name == "z":
                            for e in range(2):
                                ins = pe.matmul(psum[:, B0 + 2 + e, 0:HD], Aak(e), vv(e), start=True, stop=t == 0)
                            if t:
                                for e in range(2):
                                    ins = pe.matmul(psum[:, B0 + 2 + e, 0:HD], art[rows_of(e), f, t, 0, :], st[rows_of(e), f, :],
                                                    start=False, stop=True)
                            ins.then_inc(pm[s], 1)
                        elif name == "f2":
                            A(s, "F")
                            gemm2(s, B0 + 1, [(p2t, p2), (p2, p2t)])
                        elif name == "uj":
                            V(s, "Z")
                            applied(s, B0 + 3, R, U0)
                        elif name == "f4":
                            A(s, "F2")
                            gemm2(s, B0 + 2, [(p4t, p4)])
                        elif name == "uf":
                            V(s, "U1")
                            applied(s, B0, p2, U1)
                        elif name == "uf2":
                            V(s, "U2")
                            applied(s, B0 + 1, p4, U0)
                        elif name == "uf4":
                            V(s, "U3")
                            A(s, "F4")
                            applied(s, B0 + 3, p8, U1)
                        elif name == "y":
                            V(s, "U")
                            for e in range(2):
                                dst = psum[:, B0 + e, 0:HD]
                                pe.matmul(dst, Arb(e), U0(e), start=True, stop=False)
                                ins = pe.matmul(dst, Ark(e), vv(e), start=False, stop=t == 0)
                            if t:
                                for e in range(2):
                                    ins = pe.matmul(psum[:, B0 + e, 0:HD], art[rows_of(e), f, t, 1, :], st[rows_of(e), f, :],
                                                    start=False, stop=True)
                            ins.then_inc(pm[s], 1)
                        else:
                            for e in range(2):
                                dst = psum[rows_of(e), B0 + 2, 0:HD]
                                c = slice(f * P + e * HD, f * P + (e + 1) * HD)
                                pe.matmul(dst, tk[:, 2, c], U0(e), start=True, stop=False)
                                ins = pe.matmul(dst, tk[:, 3, c], vv(e), start=False, stop=True)
                            ins.then_inc(pm[s], 1)
            pe.wait_ge(gn_ok, TT)
            for j in range(FT // 2):
                for i in range(2):
                    for t in range(TT):
                        f = 2 * j + i
                        ins = pe.transpose(psum[:, j, i * SEQ + t * P:i * SEQ + (t + 1) * P], y_tok[:, t, f * P:(f + 1) * P], ident[:])
                ins.then_inc(y_mm, 1)
            pe.wait_ge(y_lo, FT // 2)
            full_gemm(first["out", 1], KD, xh, xl)
            norm(4)
            pe.wait_ge(n_lo, 20)
            ffn(1)

        @block.scalar
        def _(act):
            split = [0]

            def split_to(n):
                for i in range(split[0], min(n, NPIECES)):
                    act.wait_ge(landed[i % RAW], land_value[i])
                    if i >= SPL:
                        act.wait_ge(used, i - SPL + 1)
                    act.activation(w_hi[:, i % SPL, 0:size(i)], raw[:, i % RAW, 0:size(i)], ACT.Copy).then_inc(hi_done, 1)
                split[0] = max(split[0], min(n, NPIECES))

            def norm(n):
                src = hn if n == 0 else h
                dh = mh if n == 0 else xh
                if n == 0:
                    act.wait_ge(in_mem, 16)
                elif n == 1:
                    act.wait_ge(in_x, 16)
                    act.wait_ge(n_lo, 4)
                    act.wait_ge(n_tp, 4)
                else:
                    act.wait_ge(p_h, 2 * (n - 1))
                act.activation(psum[:, 0:2, :], src[:, 0, :].rearrange("p (b n) -> p b n", b=2), ACT.Square,
                               accum_out=ssq[:, 0:1]).then_inc(n_sqA, 1)
                act.wait_ge(n_sqA, n + 1)
                act.wait_ge(n_sqD, n + 1)
                if n == 0:
                    act.wait_ge(consts, 2)
                act.activation(rms[:], ssq[:, 0:2], ACT.Sqrt, bias=cst[:, 0:1], scale=1.0 / D).then_inc(n_rms, 1)
                act.wait_ge(n_inv, n + 1)
                act.activation(hn[:, 0, :], src[:, 0, :], ACT.Copy, scale=rin[:, 0:1]).then_inc(n_scA, 1)
                if n == 0:
                    act.wait_ge(vec_ev, 1)
                for b in range(KD // 2):
                    act.wait_ge(n_tp, 4 * n + b + 1)
                    for j in range(2):
                        k = 2 * b + j
                        ins = act.activation(dh[:, k, :], psum[:, b, j * SEQ:(j + 1) * SEQ], ACT.Copy,
                                             scale=colA[:, NORM_COL[n] + k:NORM_COL[n] + k + 1])
                    ins.then_inc(n_hi, 1)

            def token_out(g):
                act.wait_ge(tok_mm, g + 1)
                dst = mkv[:, 0, :] if g == 0 else pr[:, 0, 512 * (g - 1):min(512 * g, NSA_IN)]
                act.activation(dst, psum[:, 4 + 2 * (g % 2), 0:dst.shape[1]], ACT.Copy).then_inc(tok_evA, 1)

            def turn_out(k):
                act.wait_ge(tp0, k + 1)
                src = psum[:, k % 4, :].rearrange("p (j n) -> p j n", j=2)
                kind, n = TURNS[2 * k]
                if k < 3:
                    act.activation(KC[0:HD, n:n + 2, :], src[0:HD], ACT.Copy)
                    act.activation(KC[HD:P, n:n + 2, 0:SEQ - 1], src[HD:P, :, 1:SEQ], ACT.Copy).then_inc(tp0A, 1)
                else:
                    dst = {"dup": kT, "q": qT, "mq": mqT, "mk": mkT}[kind]
                    n = n - 6 if kind == "dup" else n
                    act.activation(dst[:, n:n + 2, :], src, ACT.Copy).then_inc(tp0A, 1)

            def attention(layer):
                n = len(UNITS[layer])
                for s in range(n + LAG_V + 1):
                    if s < n:
                        u = UBASE[layer] + s
                        nbr, nk = branches(UNITS[layer][s])
                        act.wait_ge(a_max, u + 1)
                        for b in range(nbr):
                            v = SM[layer][:, u % 2, b, 0:nk * P]
                            ins = act.activation(v, v, ACT.Exp, bias=nbias[:, u % 2, b:b + 1], scale=SCALE,
                                                 accum_out=rsum[:, u % 2, b:b + 1])
                        ins.then_inc(a_exp, 1)
                    i = s - LAG_T
                    if 0 <= i < n and (UBASE[layer] + i) % 2 == 0:
                        u = UBASE[layer] + i
                        nbr, nk = branches(UNITS[layer][i])
                        act.wait_ge(a_tp, u + 1)
                        if u >= 2:
                            act.wait_ge(a_pv, u - 1)
                        act.activation(PT[layer][:, u % 2, 0:nbr * nk, :],
                                       psum[:, 2 + u % 2, 0:nbr * nk * P].rearrange("p (k n) -> p k n", n=P),
                                       ACT.Copy).then_inc(a_ptA, 1)
                    i = s - LAG_V
                    if 0 <= i < n and i % 4 == 3:
                        f = UNITS[layer][i][0]
                        act.wait_ge(a_pv, UBASE[layer] + i + 1)
                        act.activation(xh[:, f, :], psum[:, 6 + f % 2, 0:SEQ], ACT.Copy).then_inc(a_hi, 1)

            def post(m, last_piece):
                act.wait_ge(used, last_piece)
                for b in range(4):
                    act.activation(psum[:, (0, 1, 4, 5)[b], :], psum[:, GEMM_ACC[b], :], ACT.Square,
                                   accum_out=ssq[:, b:b + 1]).then_inc(p_sq, 1)
                act.wait_ge(p_ss, m + 1)
                act.activation(rms[:], ss2[:], ACT.Sqrt, bias=cst[:, 0:1], scale=1.0 / D).then_inc(p_rms, 1)

            def ffn(layer):
                up0, t0 = 2 * NFC * layer, NFC * layer

                def hidden_hi(c):
                    act.wait_ge(up_tp, t0 + c + 1)
                    act.activation(hh[:, 2 * c:2 * c + 2, :], psum[:, 4 + c % 2, :].rearrange("p (j n) -> p j n", j=2),
                                   ACT.Copy).then_inc(up_hi, 1)

                for c in range(NFC):
                    i = first["up", layer] + 2 * c
                    split_to(i + 3)
                    if c:
                        hidden_hi(c - 1)
                    split_to(i + 4)
                    for t in range(TT):
                        if t == 0:
                            act.wait_ge(up_mm, t0 + c + 1)
                        else:
                            act.wait_ge(used, i + 2)
                        if c:
                            act.wait_ge(up_mul, up0 + 2 * (c - 1) + t + 1)
                        act.activation(sg[:, t, :], psum[:, 2 * (c % 2) + t, 0:FC], ACT.Silu).then_inc(up_silu, 1)
                hidden_hi(NFC - 1)
                i0 = first["down", layer]
                for j in range(KF // 2):
                    split_to(i0 + j + 3)

            norm(0)
            split_to(3)
            norm(1)
            token_out(0)
            split_to(4)
            act.wait_ge(trig_r, 1)
            act.activation(trig[:], ang[:], ACT.Sin).then_inc(trig_s, 1)
            for g in range(1, 6):
                i = first["nsa"] + 2 * (g - 1)
                split_to(i + 3)
                split_to(i + 4)
                token_out(g)
                if g == 4:
                    split_to(i + 5)
                    turn_out(0)
                    turn_out(2)
                    act.wait_ge(kp_f, 1)
                    act.activation(kph[0][:], kpf[:], ACT.Copy).then_inc(kp_hi, 1)
                    act.wait_ge(kp_f, 2)
                    act.activation(kph[1][:], kpf[:], ACT.Copy).then_inc(kp_hi, 1)
            i = first["cmp"]
            split_to(i + 3)
            act.wait_ge(gl_s, 1)
            act.activation(gates[:], gates[:], ACT.Sigmoid).then_inc(gate_s, 1)
            split_to(i + 4)
            for kv in range(2):
                act.wait_ge(used, i + 2 * kv + 2)
                if kv == 0:
                    act.wait_ge(kp_lo, 2)
                act.activation(hc[:, kv, :], psum[0:GROUPS * NCMP, 4 + kv, 0:CMP_HIDDEN], ACT.Gelu_apprx_tanh).then_inc(c_gelu, 1)
            turn_out(4)
            act.wait_ge(c_tp, 1)
            act.activation(hcT[:], psum[:, 6, 0:4 * GROUPS * NCMP].rearrange("p (k n) -> p k n", k=4), ACT.Copy).then_inc(c_ht, 1)
            for k in range(6, NTURN, 2):
                turn_out(k)
            act.wait_ge(c_kt, 1)
            act.activation(kcT[:], psum[:, 7, 256:256 + GROUPS * NCMP], ACT.Copy).then_inc(c_ktv, 1)
            split_to(i + 7)
            for t in range(TT):
                act.wait_ge(b_sub, t + 1)
                v = sc[:, t].rearrange("p h n -> p (h n)")
                act.activation(v, v, ACT.Exp, scale=SCALE).then_inc(b_exp, 1)
            for t in range(TT):
                for q in range(3):
                    act.wait_ge(b_tp, 3 * t + q + 1)
                    act.activation(pcT[:, t, 4 * q:4 * q + 4, :],
                                   psum[0:NCMP, 3 * t + q, :].rearrange("p (h n) -> p h n", h=4), ACT.Copy).then_inc(b_pt, 1)
            attention(0)
            i = first["out", 0]
            for j in range(KD // 2):
                split_to(i + j + 3)
            post(0, i + KD // 2)
            split_to(first["up", 0] + 3)
            norm(2)
            ffn(0)
            post(1, first["down", 0] + KF // 2)

            split_to(first["rwkv"] + 3)
            norm(3)

            def strip_out(q):
                act.wait_ge(used, first["rwkv"] + q + 1)
                src = psum[:, 4 + q % 2, :].rearrange("p (j n) -> p j n", j=2)
                if q == 10:
                    act.activation(mqT[:], src, ACT.Copy).then_inc(fm_out, 1)
                    return
                if q == 0:
                    act.wait_ge(shb_zero, 3)
                if q >= 2:
                    act.wait_ge(shifted, q - 1)
                act.activation(shb[q % 2][:, :, 1:SEQ + 1], src, ACT.Copy).then_inc(fm_out, 1)

            def col(base, f):
                return colB[:, base + f:base + f + 1]

            for q in range(11):
                split_to(first["rwkv"] + q + 3)
                strip_out(q)
                if q == 0:
                    act.wait_ge(shifted, 1)
                    act.activation(wg[0:LORA, 0, :], wg[0:LORA, 0, :], ACT.Tanh).then_inc(l_act, 1)
                    act.activation(wg[:, 1, :], wg[:, 1, :], ACT.Sigmoid).then_inc(l_act, 1)
                if q == 1:
                    for j in range(FT // 2):
                        act.wait_ge(z_mm, j + 1)
                        for i in range(2):
                            f = 2 * j + i
                            ins = act.activation(lwT[:, f, :], psum[:, 6, i * SEQ:(i + 1) * SEQ], ACT.Sigmoid, bias=col(B_W0, f))
                        ins.then_inc(z_ev, 1)
                        act.wait_ge(a_mm, j + 1)
                        for i in range(2):
                            f = 2 * j + i
                            ins = act.activation(aT[:, f, :], psum[:, 7, i * SEQ:(i + 1) * SEQ], ACT.Sigmoid, bias=col(B_A0, f))
                        ins.then_inc(a_ev, 1)
                if q == 2:
                    for j in range(FT // 2):
                        act.wait_ge(g_mm, j + 1)
                        act.activation(gT[:, 2 * j:2 * j + 2, :], psum[:, j, :].rearrange("p (j n) -> p j n", j=2), ACT.Copy).then_inc(g_ev, 1)
                if q == 3:
                    act.wait_ge(cs_ok, 1)
                    act.activation(eP[:], cs[:], ACT.Exp, scale=-KAPPA).then_inc(ex_ok, 1)
                    act.activation(eN[:].rearrange("p f t n -> p (f t) n"),
                                   cs[:].rearrange("p f t n -> p (f t) n")[:, :, 1:], ACT.Exp, scale=KAPPA).then_inc(ex_ok, 1)
                if q == 5:
                    for j in range(FT // 2):
                        act.wait_ge(ss_ev, j + 1)
                        v = eP_sq[:, 2 * j:2 * j + 2, :]
                        act.activation(v, v, ACT.Sqrt).then_inc(ss_rt, 1)
            for f in range(FT):
                act.wait_ge(tk_mm, f + 1)
                act.activation(tk[:, :, f * P:(f + 1) * P], psum[:, 3 * (f % 2), :].rearrange("p (k n) -> p k n", k=4),
                               ACT.Copy).then_inc(tk_ev, 1)
            attention(1)
            split_to(first["rwkv"] + 11 + 3)
            act.wait_ge(sf_ok, 1)
            act.activation(sfac[:], sfac[:], ACT.Exp, scale=-KAPPA).then_inc(s_act, 1)
            act.wait_ge(s_act, 1)
            for d in range(ROUNDS):
                t = d // NPAIR
                for name, bank, key, after in (("S2", 2, "S2", "sq2"), ("S4", 0, "S4", "sq4"), ("S8", 2, "S8", "sq8"),
                                               ("F", 0, "S2", "f"), ("F2", 1, "S4", "f2"), ("F4", 2, "S8", "f4"),
                                               ("Y", None, None, "y"), ("S", 2, None, "s")):
                    if name == "S" and t:
                        continue
                    for s in range(2):
                        f = 2 * (d % NPAIR) + s
                        act.wait_ge(pm[s], step(PE_STEPS, d, after))
                        if name == "Y":
                            src = psum[:, 4 * s:4 * s + 2, 0:HD]
                            dst = y_tok[:, t, f * P:(f + 1) * P].rearrange("p (e n) -> p e n", e=2)
                            act.activation(dst, src, ACT.Copy).then_inc(pa[s], 1)
                        elif name == "S":
                            act.activation(st[:, f, :], psum[:, 4 * s + 2, 0:HD], ACT.Copy, scale=sfac[:, f:f + 1]).then_inc(pa[s], 1)
                        else:
                            dst = PB[s][key]
                            n = 4 if len(dst.shape) == 4 else 2
                            pat = "p a b n -> p (a b) n" if n == 4 else "p a n -> p a n"
                            act.activation(dst[:].rearrange(pat), psum[:, 4 * s + bank, 0:n * P].rearrange("p (k n) -> p k n", n=P),
                                           ACT.Copy).then_inc(pa[s], 1)
            for t in range(TT):
                act.wait_ge(gn_sub, t + 1)
                act.activation(gsq[:], y_tok[:, t, :], ACT.Square).then_inc(gn_sq, 1)
                act.wait_ge(gn_var, t + 1)
                act.activation(gst[1][:], gst[1][:], ACT.Sqrt, bias=cst[:, 1:2], scale=1.0 / HD).then_inc(gn_rt, 1)
            for j in range(FT // 2):
                act.wait_ge(y_mm, j + 1)
                for i in range(2):
                    f = 2 * j + i
                    ins = act.activation(y_fin[:, f, :], psum[:, j, i * SEQ:(i + 1) * SEQ], ACT.Identity,
                                         scale=col(B_LNG, f), bias=col(B_LNB, f))
                ins.then_inc(y_sc, 1)
            for j in range(FT // 2):
                act.wait_ge(y_fin_ok, j + 1)
                act.activation(xh[:, 2 * j:2 * j + 2, :], y_fin[:, 2 * j:2 * j + 2, :], ACT.Copy).then_inc(y_hi, 1)
            i = first["out", 1]
            for j in range(KD // 2):
                split_to(i + j + 3)
            post(2, i + KD // 2)
            split_to(first["up", 1] + 3)
            norm(4)
            ffn(1)
            post(3, first["down", 1] + KF // 2)

        @block.vector
        def _(dve):
            chain = [0]

            def link(ins):
                chain[0] += 1
                ins.then_inc(s_dve, 1)
                dve.wait_ge(s_dve, chain[0])

            split = [0]

            def split_to(n):
                for i in range(split[0], min(n, NPIECES)):
                    dve.wait_ge(hi_done, i + 1)
                    dve.tensor_tensor(w_lo[:, i % SPL, 0:size(i)], raw[:, i % RAW, 0:size(i)], w_hi[:, i % SPL, 0:size(i)],
                                      ALU.subtract).then_inc(lo_done, 1)
                split[0] = max(split[0], min(n, NPIECES))

            def norm_start(n):
                src = hn if n == 0 else h
                if n == 0:
                    dve.wait_ge(in_mem, 16)
                elif n == 1:
                    dve.wait_ge(in_x, 16)
                    dve.wait_ge(n_tp, 4)
                if n >= 2:
                    dve.wait_ge(p_h, 2 * (n - 1))
                if n:
                    dve.wait_ge(n_lo, 4 * n)
                dve.tensor_tensor_reduce(psum[:, 2:4, :].rearrange("p b n -> p (b n)"), src[:, 1, :], src[:, 1, :], 1.0, 0.0,
                                         ALU.mult, ALU.add, ssq[:, 1:2]).then_inc(n_sqD, 1)

            def norm(n):
                src = hn if n == 0 else h
                norm_start(n)
                dl, dh = (ml, mh) if n == 0 else (xl, xh)
                dve.wait_ge(n_rms, n + 1)
                dve.reciprocal(rin[:], rms[:]).then_inc(n_inv, 1)
                dve.wait_ge(n_inv, n + 1)
                dve.tensor_scalar(hn[:, 1, :], src[:, 1, :], rin[:, 1:2], None, ALU.mult).then_inc(n_scD, 1)
                return dl, dh

            def norm_lo(n):
                dl, dh = (ml, mh) if n == 0 else (xl, xh)
                for b in range(KD // 2):
                    dve.wait_ge(n_hi, 4 * n + b + 1)
                    for j in range(2):
                        k = 2 * b + j
                        c = NORM_COL[n] + k
                        ins = dve.scalar_tensor_tensor(dl[:, k, :], psum[:, b, j * SEQ:(j + 1) * SEQ], colA[:, c:c + 1],
                                                       dh[:, k, :], ALU.mult, ALU.subtract)
                    ins.then_inc(n_lo, 1)

            def token_out(g):
                i0 = first["mem"] if g == 0 else first["nsa"] + 2 * (g - 1)
                dve.wait_ge(used, i0 + 2)
                dst = mkv[:, 1, :] if g == 0 else pr[:, 1, 512 * (g - 1):min(512 * g, NSA_IN)]
                dve.tensor_copy(dst, psum[:, 5 + 2 * (g % 2), 0:dst.shape[1]]).then_inc(tok_evD, 1)

            def turn_out(k):
                dve.wait_ge(tp0, k + 1)
                src = psum[:, k % 4, :].rearrange("p (j n) -> p j n", j=2)
                kind, n = TURNS[2 * k]
                if k < 3:
                    dve.tensor_copy(KC[0:HD, n:n + 2, :], src[0:HD])
                    dve.tensor_copy(KC[HD:P, n:n + 2, 0:SEQ - 1], src[HD:P, :, 1:SEQ]).then_inc(tp0D, 1)
                else:
                    dst = {"dup": kT, "q": qT, "mq": mqT, "mk": mkT}[kind]
                    n = n - 6 if kind == "dup" else n
                    dve.tensor_copy(dst[:, n:n + 2, :], src).then_inc(tp0D, 1)

            def rope(a, b, cos, sin, tmp, done=None):
                dve.tensor_tensor(tmp[0], a, cos, ALU.mult)
                dve.tensor_tensor(tmp[1], b, sin, ALU.mult)
                dve.tensor_tensor(tmp[2], a, sin, ALU.mult)
                link(dve.tensor_tensor(tmp[3], b, cos, ALU.mult))
                dve.tensor_tensor(a, tmp[0], tmp[1], ALU.subtract)
                ins = dve.tensor_tensor(b, tmp[2], tmp[3], ALU.add)
                if done is None:
                    link(ins)
                else:
                    ins.then_inc(done, 1)

            def rope_heads(col, heads, tmp, done):
                v = pr[:, :, col:col + heads * HD].rearrange("p t (h d) -> p t h d", d=HD)
                tr = trig[:, 0:TT]
                cos, sin = (tr[:, :, i, :].unsqueeze(2).to_broadcast([P, TT, heads, HALF]) for i in (1, 0))
                rope(v[:, :, :, 0:HALF], v[:, :, :, HALF:ROT], cos, sin, tmp, done)

            def attention(layer):
                n = len(UNITS[layer])
                for s in range(n + LAG_V + 1):
                    if s < n:
                        u = UBASE[layer] + s
                        f, e, t, kind = UNITS[layer][s]
                        nbr, nk = branches(UNITS[layer][s])
                        dve.wait_ge(a_sc, u + 1)
                        if u >= 2:
                            dve.wait_ge(a_tp, u - 1)
                        for b in range(nbr):
                            if kind == "nsa":
                                mask = cmask[:, (TT - 1 - t) * P:SEQ]
                            else:
                                mask = cmask[:, 0:1].to_broadcast([P, SEQ])
                            ins = dve.tensor_tensor_reduce(SM[layer][:, u % 2, b, 0:nk * P], psum[:, u % 2, b * SEQ:b * SEQ + nk * P],
                                                           mask, 1.0, NEG, ALU.add, ALU.max, mx[:, u % 2, b:b + 1])
                        link(ins)
                        dve.tensor_scalar(nbias[:, u % 2, 0:nbr], mx[:, u % 2, 0:nbr], -SCALE, None, ALU.mult).then_inc(a_max, 1)
                    i = s - 1
                    if 0 <= i < n:
                        u = UBASE[layer] + i
                        f, e, t, kind = UNITS[layer][i]
                        nbr, nk = branches(UNITS[layer][i])
                        dve.wait_ge(a_exp, u + 1)
                        ins = dve.reciprocal(coef[:, u % 2, 0:nbr], rsum[:, u % 2, 0:nbr])
                        if kind == "nsa":
                            link(ins)
                            g = 3 * (2 * f + e) + 1
                            ins = dve.tensor_tensor(coef[:, u % 2, :], coef[:, u % 2, :], gates[:, t, g:g + 2], ALU.mult)
                        ins.then_inc(a_coef, 1)
                    i = s - LAG_T
                    if 0 <= i < n and (UBASE[layer] + i) % 2 == 1:
                        u = UBASE[layer] + i
                        nbr, nk = branches(UNITS[layer][i])
                        dve.wait_ge(a_tp, u + 1)
                        if u >= 2:
                            dve.wait_ge(a_pv, u - 1)
                        dve.tensor_copy(PT[layer][:, u % 2, 0:nbr * nk, :],
                                        psum[:, 2 + u % 2, 0:nbr * nk * P].rearrange("p (k n) -> p k n", n=P)).then_inc(a_ptD, 1)
                    i = s - LAG_V
                    if 0 <= i < n and i % 4 == 3:
                        f = UNITS[layer][i][0]
                        dve.wait_ge(a_hi, f + FBASE[layer] + 1)
                        dve.tensor_tensor(xl[:, f, :], psum[:, 6 + f % 2, 0:SEQ], xh[:, f, :], ALU.subtract).then_inc(a_lo, 1)

            def post(m):
                dve.wait_ge(in_gain, 16 * (m + 1))
                for b in range(4):
                    dve.wait_ge(p_sq, 4 * m + b + 1)
                    c = slice(512 * (b % 2), 512 * (b % 2) + 512)
                    dve.tensor_tensor(hn[:, b // 2, c], psum[:, GEMM_ACC[b], :], gain[:, c], ALU.mult).then_inc(p_tmp, 1)
                q = ssq[:].rearrange("p (t n) -> p t n", n=2)
                dve.tensor_tensor(ss2[:], q[:, :, 0], q[:, :, 1], ALU.add).then_inc(p_ss, 1)
                dve.wait_ge(p_rms, m + 1)
                dve.wait_ge(p_tmp, 4 * m + 4)
                link(dve.reciprocal(rin[:], rms[:]))
                for t in range(TT):
                    dve.scalar_tensor_tensor(h[:, t, :], hn[:, t, :], rin[:, t:t + 1], h[:, t, :],
                                             ALU.mult, ALU.add).then_inc(p_h, 1)

            def ffn(layer):
                up0, t0 = 2 * NFC * layer, NFC * layer

                def hidden_lo(c):
                    dve.wait_ge(up_hi, t0 + c + 1)
                    dve.tensor_tensor(hl[:, 2 * c:2 * c + 2, :], psum[:, 4 + c % 2, :].rearrange("p (j n) -> p j n", j=2),
                                      hh[:, 2 * c:2 * c + 2, :], ALU.subtract).then_inc(up_lo, 1)

                for c in range(NFC):
                    i = first["up", layer] + 2 * c
                    split_to(i + 3)
                    if c:
                        hidden_lo(c - 1)
                    split_to(i + 4)
                    for t in range(TT):
                        dve.wait_ge(up_silu, up0 + 2 * c + t + 1)
                        if c:
                            dve.wait_ge(up_tp, t0 + c)
                        dve.tensor_tensor(hid[:, t, :], sg[:, t, :], psum[:, 2 * (c % 2) + t, FC:2 * FC],
                                          ALU.mult).then_inc(up_mul, 1)
                hidden_lo(NFC - 1)
                i0 = first["down", layer]
                for j in range(KF // 2):
                    split_to(i0 + j + 3)

            norm(0)
            dve.wait_ge(vec_tp, 1)
            dve.tensor_copy(colA[:], psum[:, 7, 0:NA])
            link(dve.tensor_copy(colB[:], psum[:, 7, P:P + NB]))
            dve.nop().then_inc(vec_ev, 1)
            norm_lo(0)
            split_to(3)
            norm(1)
            norm_lo(1)
            token_out(0)
            split_to(4)
            dve.wait_ge(in_small, 16 * 7)
            dve.wait_ge(consts, 3 + HALF)
            link(dve.tensor_copy(posf[:], posi[:]))
            shape = [P, 3, 2, HALF]
            for c in range(3):
                ins = dve.tensor_scalar(ang[:, c], invf[:], posf[:, c:c + 1], None, ALU.mult)
            link(ins)
            dve.tensor_scalar(turns[:, :, 0, :], ang[:, :, 0, :], 1.0 / (2 * np.pi), None, ALU.mult)
            link(dve.tensor_scalar(turns[:, :, 1, :], ang[:, :, 1, :], 1.0 / (2 * np.pi), 0.25, ALU.mult, ALU.add))
            link(dve.tensor_scalar(turns[:], turns[:], MAGIC, None, ALU.add))
            link(dve.tensor_scalar(turns[:], turns[:], -MAGIC, None, ALU.add))
            for part in TURN:
                link(dve.scalar_tensor_tensor(ang[:], turns[:], -float(part), ang[:], ALU.mult, ALU.add))
            link(dve.tensor_scalar(ang[:, :, 1, :], ang[:, :, 1, :], float(np.pi / 2), None, ALU.add))
            PI = float(np.nextafter(np.float32(np.pi), np.float32(0)))
            dve.tensor_scalar(ang[:], ang[:], PI, -PI, ALU.min, ALU.max).then_inc(trig_r, 1)
            for g in range(1, 6):
                i = first["nsa"] + 2 * (g - 1)
                split_to(i + 3)
                split_to(i + 4)
                token_out(g)
                if g == 4:
                    split_to(i + 5)
                    turn_out(1)
                    dve.wait_ge(tp0A, 2)
                    dve.wait_ge(tp0D, 1)
                    for kv in range(2):
                        if kv:
                            dve.wait_ge(kp_hi, 1)
                            dve.wait_ge(kp_lo, 1)
                        dst = kpf[:].rearrange("p j (g n) -> p j g n", g=GROUPS)
                        for half in range(2):
                            src = KC[:, 3 * kv:3 * kv + 3, CMP_STRIDE * half:CMP_STRIDE * (half + NCMP)].rearrange(
                                "p g (n j w) -> p j g n w", j=8, w=2)[:, :, :, :, 0]
                            col = (A_POSK, A_POSV)[kv] + 8 * half
                            ins = None
                            for gg in range(GROUPS):
                                pos = colA[:, col:col + 8].unsqueeze(2).to_broadcast([P, 8, NCMP])
                                ins = dve.tensor_tensor(dst[:, 8 * half:8 * half + 8, gg, :], src[:, :, gg, :], pos, ALU.add)
                        ins.then_inc(kp_f, 1)
                        dve.wait_ge(kp_hi, kv + 1)
                        dve.tensor_tensor(kpl[kv][:], kpf[:], kph[kv][:], ALU.subtract).then_inc(kp_lo, 1)
            i = first["cmp"]
            split_to(i + 3)
            dve.wait_ge(tok_evA, 6)
            dve.wait_ge(tok_evD, 6)
            dve.tensor_tensor(gates[:], pr[:, :, O_G:O_G + GATES], gateb[:].unsqueeze(1).to_broadcast([P, TT, GATES]),
                              ALU.add).then_inc(gl_s, 1)
            dve.wait_ge(trig_s, 1)
            small = [rt[:, 48 * k:48 * k + 48].rearrange("p (t h d) -> p t h d", t=TT, d=HALF) for k in range(4)]
            rope_heads(O_KS, GROUPS, small, roped_k)
            dve.wait_ge(roped_k, 1)
            rope_heads(O_KW, GROUPS, small, roped_k)
            split_to(i + 4)
            rope_heads(0, HEADS, [rtq[:, k] for k in range(4)], roped_q)
            turn_out(3)
            turn_out(5)
            dve.wait_ge(c_w2, 1)
            n = GROUPS * NCMP
            dve.tensor_copy(kcs[:], psum[0:n, 7, 0:HD])
            link(dve.tensor_copy(vcs[:], psum[0:NCMP, 7, HD:HD + KVW].rearrange("p (g d) -> p g d", d=HD)))
            rope(kcs[:, 0:HALF], kcs[:, HALF:ROT], trig[0:n, TT, 1, :], trig[0:n, TT, 0, :],
                 [rt[0:n, 8 * k:8 * k + 8] for k in range(4)])
            for c in range(2):
                ins = dve.tensor_copy(kcd[:, c, :], kcs[:])
            ins.then_inc(c_kd, 1)
            for k in range(7, NTURN, 2):
                turn_out(k)
            split_to(i + 7)
            for t in range(TT):
                dve.wait_ge(b_sc, t + 1)
                v = sc[:, t]
                mask = bcmask[:, t * NCMP:(t + 1) * NCMP].unsqueeze(1).to_broadcast([P, FT, NCMP])
                for e in range(2):
                    ins = dve.tensor_tensor(v.rearrange("p (f e) n -> p e f n", e=2)[:, e],
                                            psum[:, 4 + 2 * t + e, 0:FT * NCMP].rearrange("p (h n) -> p h n", n=NCMP), mask, ALU.add)
                link(ins)
                link(dve.tensor_reduce(cmx[:], v, AX.X, ALU.max))
                dve.tensor_tensor(v, v, cmx[:].unsqueeze(2).to_broadcast([P, HEADS, NCMP]), ALU.subtract).then_inc(b_sub, 1)
            dve.wait_ge(gate_s, 1)
            for t in range(TT):
                dve.wait_ge(b_exp, t + 1)
                v = sc[:, t]
                link(dve.tensor_reduce(csum[:], v, AX.X, ALU.add))
                link(dve.tensor_scalar(csum[:], csum[:], 1e-30, None, ALU.max))
                link(dve.reciprocal(csum[:], csum[:]))
                link(dve.scalar_tensor_tensor(ccf[:], csum[:], rowok[:, t:t + 1],
                                              gates[:, t, :].rearrange("p (h g) -> p h g", g=3)[:, :, 0], ALU.mult, ALU.mult))
                dve.tensor_tensor(v, v, ccf[:].unsqueeze(2).to_broadcast([P, HEADS, NCMP]), ALU.mult).then_inc(b_p, 1)
            attention(0)
            i = first["out", 0]
            for j in range(KD // 2):
                split_to(i + j + 3)
            post(0)
            split_to(first["up", 0] + 3)
            norm(2)
            norm_lo(2)
            ffn(0)
            post(1)

            split_to(first["rwkv"] + 3)
            norm(3)
            norm_lo(3)

            def col(base, f):
                return colB[:, base + f:base + f + 1]

            def shift(q):
                dve.wait_ge(fm_out, q + 1)
                f0 = 2 * RWKV_ORDER[q]
                dst = wg if q == 0 else (rT, k_T, vT)[f0 // FT]
                j0 = 0 if q == 0 else f0 % FT
                link(dve.tensor_tensor(dst[:, j0:j0 + 2, :], shb[q % 2][:, :, 0:SEQ], shb[q % 2][:, :, 1:SEQ + 1], ALU.subtract))
                for i in range(2):
                    ins = dve.scalar_tensor_tensor(dst[:, j0 + i, :], dst[:, j0 + i, :], col(B_MU, f0 + i),
                                                   shb[q % 2][:, i, 1:SEQ + 1], ALU.mult, ALU.add)
                ins.then_inc(shifted, 1)

            flat = "p f n -> p (f n)"
            ftn = "p f (t n) -> p (f t) n"
            for q in range(10):
                split_to(first["rwkv"] + q + 3)
                shift(q)
                if q == 1:
                    dve.wait_ge(z_ev, 3)
                    for f in range(FT):
                        for t in range(TT):
                            ins = dve.tensor_tensor_scan(cs[:, f, t, 1:], cst[:, 2:3].to_broadcast([P, P]), lwT[:, f, t * P:(t + 1) * P],
                                                         0.0, ALU.mult, ALU.add)
                    link(ins)
                    link(dve.tensor_copy(mid[:], cs[:, :, :, P // 2]))
                    v = cs[:].rearrange("p f t n -> p (f t) n")
                    dve.tensor_tensor(v, v, mid[:].rearrange("p f t -> p (f t)").unsqueeze(2).to_broadcast([P, FT * TT, P + 1]),
                                      ALU.subtract).then_inc(cs_ok, 1)
                    dve.wait_ge(cs_ok, 1)
                    dve.tensor_tensor(sfac[:], cs[:, :, 0, P], mid[:, :, 1], ALU.add).then_inc(sf_ok, 1)
                if q == 3:
                    dve.wait_ge(shifted, 4)
                    for f in range(FT):
                        ins = dve.tensor_scalar(kkT[:, f, :], k_T[:, f, :], col(B_KK, f), None, ALU.mult)
                    ins.then_inc(kk_ok, 1)
                    dve.wait_ge(a_ev, 3)
                    for f in range(FT):
                        ins = dve.tensor_scalar(vT[:, f, :], aT[:, f, :], -1.0, col(B_KA, f), ALU.add, ALU.mult)
                    link(ins)
                    link(dve.scalar_tensor_tensor(k_T[:].rearrange(flat), vT[:].rearrange(flat), 1.0, k_T[:].rearrange(flat),
                                                  ALU.add, ALU.mult))
                if q == 4:
                    for j in range(FT // 2):
                        dve.wait_ge(ss_mm, j + 1)
                        dve.tensor_scalar(eP_sq[:, 2 * j:2 * j + 2, :], psum[:, j, :].rearrange("p (j n) -> p j n", j=2), 1e-24, None,
                                          ALU.max).then_inc(ss_ev, 1)
                if q == 5:
                    dve.wait_ge(ss_rt, 3)
                    link(dve.reciprocal(eP_sq[:], eP_sq[:]))
                    link(dve.tensor_tensor(kkT[:], kkT[:], eP_sq[:], ALU.mult))
                    link(dve.tensor_tensor(aT[:], aT[:], kkT[:], ALU.mult))
                if q == 6:
                    dve.wait_ge(ex_ok, 2)
                    dve.wait_ge(shifted, 7)
                    e3 = eP[:].rearrange("p f t n -> p (f t) n")
                    for f in range(FT):
                        dve.scalar_tensor_tensor(art[:, f, :, 0, :], kkT[:, f, :].rearrange("p (t n) -> p t n", t=TT), -1.0,
                                                 eP[:, f, :, 0:P], ALU.mult, ALU.mult)
                        ins = dve.tensor_tensor(art[:, f, :, 1, :], rT[:, f, :].rearrange("p (t n) -> p t n", t=TT),
                                                eP[:, f, :, 1:], ALU.mult)
                    ins.then_inc(ar_ok, 1)
                    dve.wait_ge(ar_ok, 1)
                    for f in range(FT):
                        ins = dve.scalar_tensor_tensor(rT[:, f, :], rT[:, f, :], col(B_RK, f), k_T[:, f, :], ALU.mult, ALU.mult)
                    ins.then_inc(rk_ok, 1)
                    dve.wait_ge(rk_ok, 1)
                    en = eN[:].rearrange("p f t n -> p (f t n)")
                    dve.tensor_tensor(aT[:].rearrange(flat), aT[:].rearrange(flat), en, ALU.mult)
                    dve.tensor_tensor(k_T[:].rearrange(flat), k_T[:].rearrange(flat), en, ALU.mult).then_inc(bk_ok, 1)
            for j in range(FT // 2):
                dve.wait_ge(bo_mm, j + 1)
                dve.wait_ge(shifted, 10)
                dve.tensor_tensor(rT[:, 2 * j:2 * j + 2, :], psum[:, j, :].rearrange("p (j n) -> p j n", j=2),
                                  vT[:, 2 * j:2 * j + 2, :], ALU.mult).then_inc(bo_ev, 1)
            split_to(first["rwkv"] + 11 + 2)
            attention(1)
            split_to(first["rwkv"] + 11 + 3)
            dve.wait_ge(dm_ok, 1)

            def mask(i, n=1):
                return dmask[:, i:i + n, :].rearrange("p k n -> p (k n)").unsqueeze(1).to_broadcast([P, 2, n * P])

            for d in range(ROUNDS):
                t = d // NPAIR
                for name in DVE_STEPS:
                    for s in range(2):
                        b, B0 = PB[s], 4 * s

                        def M(n):
                            dve.wait_ge(pm[s], step(PE_STEPS, d, n))

                        def own(n):
                            dve.wait_ge(pv[s], step(DVE_STEPS, d, n))

                        def uu(bank):
                            return psum[:, B0 + bank, 0:2 * HD].rearrange("p (e n) -> p e n", e=2)

                        R = b["R"][:].rearrange("p e n -> p (e n)")
                        if name in ("Dt", "Et"):
                            M("gram")
                            ins = dve.tensor_tensor(b["T"][:, "DE".index(name[0]), :, :], psum[:, B0 + 2:B0 + 4, 0:P],
                                                    mask(4 if name == "Dt" else 5), ALU.mult)
                        elif name == "D":
                            ins = dve.tensor_tensor(b["DA"][:].rearrange("p e k n -> p e (k n)"), psum[:, B0:B0 + 2, 0:2 * P], mask(0, 2), ALU.mult)
                        elif name == "K":
                            ins = dve.tensor_tensor(b["KR"][:].rearrange("p e k n -> p e (k n)"), psum[:, B0:B0 + 2, 2 * P:4 * P],
                                                    mask(2, 2), ALU.mult)
                        elif name in ("R2", "R3", "J"):
                            M({"R2": "r2", "R3": "r3", "J": "j"}[name])
                            if name == "R2":
                                dve.wait_ge(pp[s], d + 1)
                            else:
                                own({"R3": "R2", "J": "R3"}[name])
                            bank = {"R2": 3, "R3": 1, "J": 3}[name]
                            ins = dve.tensor_tensor(R, psum[:, B0 + bank, 0:2 * P], R, ALU.add)
                        elif name == "Z":
                            M("z")
                            ins = dve.tensor_copy(b["U"][0][:], psum[:, B0 + 2:B0 + 4, 0:HD])
                        elif name == "U1":
                            M("uj")
                            ins = dve.tensor_copy(b["U"][1][:], uu(3))
                        else:
                            after, before, bank, i, o_ = {"U2": ("uf", "U1", 0, 1, 0), "U3": ("uf2", "U2", 1, 0, 1), "U": ("uf4", "U3", 3, 1, 0)}[name]
                            M(after)
                            own(before)
                            ins = dve.tensor_tensor(b["U"][o_][:], uu(bank), b["U"][i][:], ALU.add)
                        ins.then_inc(pv[s], 1)
            for t in range(TT):
                for s in range(2):
                    dve.wait_ge(pa[s], step(ACT_STEPS, ROUNDS - 1, "Y"))
                y3 = y_tok[:, t, :].rearrange("p (h n) -> p h n", n=HD)
                if t:
                    dve.wait_ge(gn_ok, t)
                link(dve.tensor_reduce(gst[0][:], y3, AX.X, ALU.add))
                link(dve.tensor_scalar(gst[0][:], gst[0][:], 1.0 / HD, None, ALU.mult))
                dve.tensor_tensor(y3, y3, gst[0][:].unsqueeze(2).to_broadcast([P, HEADS, HD]), ALU.subtract).then_inc(gn_sub, 1)
                dve.wait_ge(gn_sq, t + 1)
                dve.tensor_reduce(gst[1][:], gsq[:].rearrange("p (h n) -> p h n", n=HD), AX.X, ALU.add).then_inc(gn_var, 1)
                dve.wait_ge(gn_rt, t + 1)
                link(dve.reciprocal(gst[2][:], gst[1][:]))
                dve.tensor_tensor(y3, y3, gst[2][:].unsqueeze(2).to_broadcast([P, HEADS, HD]), ALU.mult).then_inc(gn_ok, 1)
            for j in range(FT // 2):
                dve.wait_ge(y_add, j + 1)
                v = y_fin[:, 2 * j:2 * j + 2, :]
                dve.tensor_tensor(v, v, gT[:, 2 * j:2 * j + 2, :], ALU.mult).then_inc(y_fin_ok, 1)
            for j in range(FT // 2):
                dve.wait_ge(y_hi, j + 1)
                dve.tensor_tensor(xl[:, 2 * j:2 * j + 2, :], y_fin[:, 2 * j:2 * j + 2, :], xh[:, 2 * j:2 * j + 2, :],
                                  ALU.subtract).then_inc(y_lo, 1)
            i = first["out", 1]
            for j in range(KD // 2):
                split_to(i + j + 3)
            post(2)
            split_to(first["up", 1] + 3)
            norm(4)
            norm_lo(4)
            ffn(1)
            post(3)


_NAMES = ["x", "mem", "positions", "mem_norm_g", "w_mem_kv", "pre_mix_g", "post_mix_g", "pre_ffn_g", "post_ffn_g",
          "w_out", "w_ffn_in", "w_ffn_out", "nsa_w_in", "nsa_gate_b", "nsa_cmp_pos_k", "nsa_cmp_pos_v",
          "nsa_cmp_k_w1", "nsa_cmp_k_w2", "nsa_cmp_v_w1", "nsa_cmp_v_w2", "rwkv_w_in", "rwkv_mu", "rwkv_w0",
          "rwkv_w2", "rwkv_a0", "rwkv_a2", "rwkv_g2", "rwkv_k_k", "rwkv_k_a", "rwkv_r_k", "rwkv_ln_g", "rwkv_ln_b"]


def kernel(**inputs):
    import concourse.bacc as bacc
    from concourse.bass_utils import run_bass_kernel_spmd

    nc = bacc.Bacc("TRN2", target_bir_lowering=False, num_devices=1)
    arrays, args = {}, []
    for name in _NAMES:
        a = np.ascontiguousarray(inputs[name])
        arrays[name] = a
        args.append(nc.dram_tensor(name, a.shape, mybir.dt.from_np(a.dtype), kind="ExternalInput").ap())
    out = nc.dram_tensor("out", (1, SEQ, D), F32, kind="ExternalOutput").ap()
    trunk(nc, *args, out)
    r = run_bass_kernel_spmd(nc, [arrays], core_ids=[0])
    return r.results[0]["out"]
```

```python
from contextlib import ExitStack

import numpy as np

import concourse.bass as bass
from concourse import mybir

ALU = mybir.AluOpType
ACT = mybir.ActivationFunctionType
AX = mybir.AxisListType
F32 = mybir.dt.float32
F32R = mybir.dt.float32r
I32 = mybir.dt.int32

P = 128
D = 1024
SEQ = 256
TT = SEQ // P
KD = D // P
HD = 64
MEM_HEADS = 4
MEM_W = MEM_HEADS * HD
PRIM = D - MEM_W
HEADS = PRIM // HD
GROUPS = 3
KVW = GROUPS * HD
ROT = HD // 4
HALF = ROT // 2
ROPE_THETA = 500000.0
CMP_BLOCK = 32
CMP_STRIDE = 16
CMP_HIDDEN = 256
NCMP = (SEQ - CMP_BLOCK) // CMP_STRIDE + 1
CJ = CMP_BLOCK * HD // P
GATES = 3 * HEADS
LORA = 64
GLORA = 128
SHIFT_W = 3 * PRIM + 2 * LORA + GLORA
NSA_IN = PRIM + 6 * KVW + GATES + MEM_W
RWKV_IN = SHIFT_W + MEM_W
FFN = ((8 * D + 3 * 256 - 1) // (3 * 256)) * 256
FC = 256
NFC = FFN // FC
KF = FFN // P
FT = PRIM // P
EPS = 1e-6
GN_EPS = HD * 1e-5
NEG = -1e30
SCALE = float(HD) ** -0.5
KAPPA = float(np.exp(-0.5))
BLK = 16

O_KC, O_VC, O_KS, O_VS, O_KW, O_VW, O_G, O_MQ = (
    PRIM, PRIM + KVW, PRIM + 2 * KVW, PRIM + 3 * KVW, PRIM + 4 * KVW, PRIM + 5 * KVW,
    PRIM + 6 * KVW, PRIM + 6 * KVW + GATES)

A_MEMG, A_PREMIX, A_PREFFN, A_POSK, A_POSV = 0, 8, 24, 40, 56
NA = 72
B_MU, B_W0, B_A0, B_KK, B_KA, B_RK, B_LNG, B_LNB = 0, 20, 26, 32, 38, 44, 50, 56
NB = 62

MAGIC = 12582912.0
TURN = [6.28125, 2029.0 / 2**20, 2 * np.pi - 6.28125 - 2029.0 / 2**20]

RAW, SPL = 5, 3
SLOTS = 3
PIECE = 2048


def weight_pieces(w_mem_kv, nsa_w_in, w1k, w1v, w_out, w_ffn_in, w_ffn_out, rwkv_w_in):
    out, start = [], {}

    def kt_view(w):
        return w.rearrange("(k p) n -> p k n", p=P)

    start["mem"] = len(out)
    for hf in range(2):
        out.append(kt_view(w_mem_kv)[:, 4 * hf:4 * hf + 4, :])
    start["nsa"] = len(out)
    for c in range(0, NSA_IN, 512):
        for hf in range(2):
            out.append(kt_view(nsa_w_in)[:, 4 * hf:4 * hf + 4, c:min(c + 512, NSA_IN)])
    start["cmp"] = len(out)
    for w in (w1k, w1v):
        for hf in range(2):
            out.append(kt_view(w)[:, 8 * hf:8 * hf + 8, :])
    for layer in range(2):
        if layer == 1:
            start["rwkv"] = len(out)
            for c in RWKV_ORDER:
                out.append(kt_view(rwkv_w_in)[:, :, 256 * c:256 * c + 256])
        start["out", layer] = len(out)
        for k in range(0, KD, 2):
            out.append(kt_view(w_out[layer])[:, k:k + 2, :])
        start["up", layer] = len(out)
        for c in range(NFC):
            for part in range(2):
                out.append(kt_view(w_ffn_in[layer])[:, :, FFN * part + FC * c:FFN * part + FC * c + FC])
        start["down", layer] = len(out)
        for k in range(0, KF, 2):
            out.append(kt_view(w_ffn_out[layer])[:, k:k + 2, :])
    return out, start


RWKV_ORDER = [9, 3, 4, 5, 0, 1, 2, 6, 7, 8, 10]


def trunk(nc, x, mem, positions, mem_norm_g, w_mem_kv, pre_mix_g, post_mix_g, pre_ffn_g, post_ffn_g,
          w_out, w_ffn_in, w_ffn_out, nsa_w_in, nsa_gate_b, nsa_cmp_pos_k, nsa_cmp_pos_v,
          nsa_cmp_k_w1, nsa_cmp_k_w2, nsa_cmp_v_w1, nsa_cmp_v_w2, rwkv_w_in, rwkv_mu, rwkv_w0,
          rwkv_w2, rwkv_a0, rwkv_a2, rwkv_g2, rwkv_k_k, rwkv_k_a, rwkv_r_k, rwkv_ln_g, rwkv_ln_b, out):
    pieces, first = weight_pieces(w_mem_kv, nsa_w_in[0], nsa_cmp_k_w1[0], nsa_cmp_v_w1[0], w_out,
                                  w_ffn_in, w_ffn_out, rwkv_w_in[0])
    NPIECES = len(pieces)

    with ExitStack() as ctx:
        ARENA = (nc.sbuf_base + 127) // 128 * 128
        ROOM = nc.sbuf_usable_end - ARENA
        base = [0]

        def at(offset, name, shape, dt=F32):
            n = 4 * int(np.prod(shape[1:]))
            assert offset + n <= ROOM, (name, offset, n)
            return nc.alloc_sbuf_tensor_at(name, shape, dt, offset=ARENA + offset)

        def put(name, shape, dt=F32):
            n = 4 * int(np.prod(shape[1:]))
            t = at(base[0], name, shape, dt)
            base[0] += (n + 31) // 32 * 32
            return t

        raw = put("w_raw", [P, RAW, PIECE])
        w_hi = put("w_hi", [P, SPL, PIECE], F32R)
        w_lo = put("w_lo", [P, SPL, PIECE], F32R)
        h = put("h", [P, TT, D])
        o_xh = base[0]
        xh = put("x_hi", [P, KD, SEQ], F32R)
        o_xl = base[0]
        xl = put("x_lo", [P, KD, SEQ], F32R)
        o_hn = base[0]
        hn = put("hn", [P, TT, D])
        gain = put("post_gain", [P, D])
        mkv = put("mem_kv", [P, TT, 2 * MEM_W])
        mkT = put("mem_kT", [P, 2, SEQ])
        mqT = put("mem_qT", [P, 2, SEQ])
        ident = put("ident", [P, P])
        cmask = put("causal_mask", [P, SEQ])
        bcmask = put("block_mask", [P, NCMP * TT])
        rowok = put("row_has_block", [P, TT])
        colA = put("cols_a", [P, NA])
        colB = put("cols_b", [P, NB])
        cst = put("consts", [P, 8])
        bones = put("head_blocks", [P, P])
        ssq = put("ssq", [P, 4])
        post_rms = put("post_rms", [P, TT])
        post_rin = put("post_rinv", [P, TT])
        rms = put("rms", [P, TT])
        rin = put("rinv", [P, TT])
        mx = put("row_max", [P, SLOTS, 2])
        nbias = put("neg_max", [P, SLOTS, 2])
        rsum = put("row_sum", [P, SLOTS, 2])
        coef = put("row_coef", [P, SLOTS, 2])
        PH = base[0]

        o = PH
        pr = at(o, "nsa_proj", [P, TT, NSA_IN])
        mh = at(o, "mem_hi", [P, KD, SEQ], F32R)
        ml = at(o + 8192, "mem_lo", [P, KD, SEQ], F32R)
        o += 4 * TT * NSA_IN
        dup = at(o, "kv_twice", [P, TT, 12, P])
        pcT = at(o, "block_probsT", [NCMP, TT, HEADS, P])
        o += 12288
        qT = at(o, "qT", [P, FT, SEQ])
        o_kT = o + 6144
        kT = at(o_kT, "kT", [P, 2 * GROUPS, SEQ])
        o += 12288
        KC = at(o, "cmp_inT", [P, 2 * GROUPS, SEQ])
        sc = at(o, "block_scores", [P, TT, HEADS, NCMP])
        o += 6144
        KB = CJ * GROUPS * NCMP
        kph = [at(b, f"cmp_blocks_hi{k}", [P, CJ, GROUPS * NCMP], F32R) for k, b in enumerate((o, o_kT))]
        kpl = [at(b + 4 * KB, f"cmp_blocks_lo{k}", [P, CJ, GROUPS * NCMP], F32R) for k, b in enumerate((o, o_kT))]
        sm = at(o_hn, "scores", [P, SLOTS, 2, SEQ])
        pT = at(o, "probsT", [P, SLOTS, 4, P])
        o += 8192
        kpf = at(o_hn, "cmp_blocks", [P, CJ, GROUPS * NCMP])
        rowsA = at(o_kT, "rows_a", [NA, P])
        rowsB = at(o_kT + 512, "rows_b", [NB, P])
        oo = o
        w2k = at(oo, "cmp_k_w2", [P, 2, HD]); oo += 512
        w2v = at(oo, "cmp_v_w2", [P, 2, HD]); oo += 512
        hc = at(o_hn + 3072, "cmp_hidden", [GROUPS * NCMP, 2, CMP_HIDDEN])
        hcT = at(o_hn + 5120, "cmp_hiddenT", [P, 4, GROUPS * NCMP])
        kcs = at(o_hn + 5856, "kc_tok", [GROUPS * NCMP, HD])
        kcd = at(o_hn + 6112, "kc_twice", [GROUPS * NCMP, 2, HD])
        kcT = at(oo, "kcT", [P, GROUPS * NCMP]); oo += 192
        vcs = at(oo, "vc_tok", [NCMP, GROUPS, HD]); oo += 768
        gates = at(oo, "gates", [P, TT, GATES]); oo += 288
        gateb = at(oo, "gate_bias", [P, GATES]); oo += 160
        posi = at(oo, "pos_int", [P, 3], I32); oo += 32
        posf = at(oo, "pos", [P, 3]); oo += 32
        invf = at(oo, "inv_freq", [P, 2, HALF]); oo += 64
        ang = at(oo, "angle", [P, 3, 2, HALF]); oo += 192
        turns = at(oo, "turns", [P, 3, 2, HALF]); oo += 192
        trig = at(oo, "trig", [P, 3, 2, HALF]); oo += 192
        cmx = at(oo, "block_max", [P, HEADS]); oo += 64
        csum = at(oo, "block_sum", [P, HEADS]); oo += 64
        ccf = at(oo, "block_coef", [P, HEADS]); oo += 64
        rt = at(o_hn + 6656, "rope_tmp", [P, 4 * 48])
        rtq = at(PH + 4 * TT * NSA_IN + 12288, "rope_tmp_q", [P, 4, TT, HEADS, HALF])

        hh = at(PH, "hidden_hi", [P, KF, SEQ], F32R)
        hl = at(PH + 4 * KF * SEQ, "hidden_lo", [P, KF, SEQ], F32R)
        o = PH + 8 * KF * SEQ
        sg = at(o, "silu", [P, 2, SEQ])
        hid = at(o + 2048, "hidden", [P, 2, SEQ])

        A6 = 4 * FT * SEQ
        C6 = 4 * FT * TT * (P + 1) + 16
        rT, k_T, aT, kkT, gT = (at(PH + A6 * i, n, [P, FT, SEQ]) for i, n in enumerate(
            ("rT", "kT_rwkv", "aT", "kkT", "out_gateT")))
        y_tok = at(PH + 3 * A6, "y_tok", [P, TT, PRIM])
        o = PH + 5 * A6
        o_v = o
        vT = at(o, "vT", [P, FT, SEQ])
        eP = at(o + A6, "decay_from_mid", [P, FT, TT, P + 1])
        o += A6 + C6
        cs = at(o, "decay_sums", [P, FT, TT, P + 1])
        eN = at(o + C6, "decay_to_mid", [P, FT, TT, P])
        lwT = at(o + C6, "log_decay", [P, FT, SEQ])
        tk = at(o, "v_b_k_tok", [P, 4, PRIM])
        y_fin = at(o, "y_scaled", [P, FT, SEQ])
        o += A6 + C6
        eP_sq = at(o, "kk_squares", [P, FT, SEQ])
        art = at(o, "a_rT", [P, FT, TT, 2, P])
        o += 2 * A6
        shb = [at(o + 2080 * i, f"shift_in{i}", [P, 2, SEQ + 1]) for i in range(2)]
        dmask = at(o, "delta_masks", [P, 6, P])
        o += 2 * 2080
        st = at(o, "state_T", [P, FT, HD])
        mid = at(o + 1536, "mid_sums", [P, FT, TT])
        sfac = at(o + 1600, "state_scale", [P, FT])
        gst = [at(o + 1632 + 64 * i, f"gn_stat{i}", [P, HEADS]) for i in range(3)]
        lora = at(o_hn, "lora_w2_a2", [P, PRIM])
        wg = at(o_hn + 6144, "lora_in", [P, 2, SEQ])
        g2 = at(o_hn + 3072, "gate_w2", [P, PRIM])
        gsq = at(o_hn + 4096, "gn_squares", [P, PRIM])

        def pair_buffers(s):
            if s == 0:
                spots = [o_xh, o_xh + 2048, o_xh + 4096, o_xl, o_xl + 2048, o_xl + 4096, o_hn]
            else:
                spots = [o_v + 2048 * i for i in range(6)] + [o_hn + 2048]
            n = f"_{'ab'[s]}"
            half = spots[6]
            return dict(
                DA=at(spots[0], "D_Arb" + n, [P, 2, 2, P]), KR=at(spots[1], "Aak_Ark" + n, [P, 2, 2, P]),
                T=at(spots[2], "Dt_Et" + n, [P, 2, 2, P]), S2=at(spots[3], "pow2" + n, [P, 2, 2, P]),
                S4=at(spots[4], "pow4" + n, [P, 2, 2, P]), 
                R=at(spots[5], "R" + n, [P, 2, P]), S8=at(half, "pow8" + n, [P, 2, P]),
                U=[at(half + 1024 + 512 * i, f"U{i}" + n, [P, 2, HD]) for i in range(2)])

        PB = [pair_buffers(s) for s in range(2)]
        sm1 = at(o_hn, "scores_1", [P, SLOTS, 2, SEQ])
        pT1 = at(o_xl, "probsT_1", [P, SLOTS, 4, P])
        SM, PT = [sm, sm1], [pT, pT1]

        psum = ctx.enter_context(nc.psum_tensor("ps", [P, 8, 512], F32))

        def sem(name):
            return ctx.enter_context(nc.semaphore(name))

        landed = [sem(f"w_landed{i}") for i in range(RAW)]
        hi_done = sem("w_hi_done")
        lo_done = sem("w_lo_done")
        used = sem("w_used")
        in_x = sem("in_x")
        in_mem = sem("in_mem")
        in_vec = sem("in_vec")
        in_small = sem("in_small")
        in_gain = sem("in_gain")
        stored = sem("stored")
        consts = sem("consts_ready")
        s_pool = sem("pool_chain")
        s_dve = sem("dve_chain")
        s_act = sem("act_chain")
        n_sqA, n_sqD, n_rms, n_inv = sem("n_sqA"), sem("n_sqD"), sem("n_rms"), sem("n_inv")
        n_scA, n_scD, n_tp, n_hi, n_lo = sem("n_scA"), sem("n_scD"), sem("n_tp"), sem("n_hi"), sem("n_lo")
        vec_tp, vec_ev = sem("vec_tp"), sem("vec_ev")
        tok_mm, tok_evA, tok_evD = sem("tok_mm"), sem("tok_evA"), sem("tok_evD")
        trig_r, trig_s = sem("trig_arg"), sem("trig_done")
        dup_c, dup_k, roped_k, roped_q = sem("dup_cmp"), sem("dup_keys"), sem("roped_keys"), sem("roped_q")
        tp0, tp0A, tp0D = sem("turned"), sem("turned_A"), sem("turned_D")
        gl_s, gate_s = sem("gate_logits"), sem("gates_ready")
        kp_f, kp_hi, kp_lo = sem("kp_f"), sem("kp_hi"), sem("kp_lo")
        c_gelu, c_tp, c_ht, c_w2, c_kv, c_kd, c_kt, c_ktv = (
            sem("c_gelu"), sem("c_tp"), sem("c_ht"), sem("c_w2"), sem("c_kv"), sem("c_kd"), sem("c_kt"), sem("c_ktv"))
        b_sc, b_sub, b_exp, b_p, b_tp, b_pt = (
            sem("b_sc"), sem("b_sub"), sem("b_exp"), sem("b_p"), sem("b_tp"), sem("b_pt"))
        a_sc, a_max, a_exp, a_coef, a_p, a_tp, a_ptA, a_ptD, a_pv, a_hi, a_lo = (
            sem("a_sc"), sem("a_max"), sem("a_exp"), sem("a_coef"), sem("a_p"), sem("a_tp"), sem("a_ptA"),
            sem("a_ptD"), sem("a_pv"), sem("a_hi"), sem("a_lo"))
        p_acc, p_sq, p_tmp, p_rms, p_h = (
            sem("p_acc"), sem("p_sq"), sem("p_tmp"), sem("p_rms"), sem("p_h"))
        up_silu, up_mul, up_hi, up_lo = (
            sem("up_silu"), sem("up_mul"), sem("up_hi"), sem("up_lo"))

        in_lora, fm_out, shifted, shb_zero = sem("in_lora"), sem("fm_out"), sem("shifted"), sem("shift_zero")
        l_act, z_mm, a_mm, z_ev, a_ev = sem("lora_act"), sem("z_mm"), sem("a_mm"), sem("z_ev"), sem("a_ev")
        g_mm, g_ev, cs_ok, ex_ok = sem("g_mm"), sem("g_ev"), sem("sums_ok"), sem("exps_ok")
        kk_ok, sq_ok, ss_mm, ss_ev, ss_rt, kn_ok = (
            sem("kk_ok"), sem("sq_ok"), sem("ss_mm"), sem("ss_ev"), sem("ss_rt"), sem("kn_ok"))
        r_ok, rk_ok, bo_mm, bo_ev, bk_ok, ar_ok, tk_mm, tk_ev = (
            sem("rdecay_ok"), sem("rk_ok"), sem("bo_mm"), sem("bo_ev"), sem("bk_ok"), sem("ar_ok"), sem("tk_mm"), sem("tk_ev"))
        dm_ok, sf_ok = sem("delta_masks"), sem("scale_ok")
        pm = [sem("pair_pe_a"), sem("pair_pe_b")]
        pv = [sem("pair_dve_a"), sem("pair_dve_b")]
        pa = [sem("pair_act_a"), sem("pair_act_b")]
        pp = [sem("pair_pool_a"), sem("pair_pool_b")]
        gn_sub, gn_sq, gn_var, gn_rt, gn_ok = sem("gn_sub"), sem("gn_sq"), sem("gn_var"), sem("gn_rt"), sem("gn_ok")
        y_mm, y_sc, y_add, y_fin_ok, y_hi, y_lo = (
            sem("y_mm"), sem("y_sc"), sem("y_add"), sem("y_fin"), sem("y_hi"), sem("y_lo"))

        block = ctx.enter_context(nc.Block())

        def raw_view(i):
            src = pieces[i]
            return raw[:, i % RAW, 0:src.shape[1] * src.shape[2]].rearrange("p (k n) -> p k n", k=src.shape[1])

        def size(i):
            src = pieces[i]
            return src.shape[1] * src.shape[2]

        def kt_of(buf, i, k):
            src = pieces[i]
            n = src.shape[2]
            return buf[:, i % SPL, k * n:(k + 1) * n]

        land_value, count = [], [0] * RAW
        for i in range(NPIECES):
            count[i % RAW] += 16
            land_value.append(count[i % RAW])

        GEMM_ACC = [2, 3, 6, 7]
        NORM_COL = [A_MEMG, A_PREMIX, A_PREFFN, A_PREMIX + 8, A_PREFFN + 8]

        def rows(queue, dst, r, src):
            n = int(np.prod(src.shape)) // P
            v = src if len(src.shape) == 1 else src.rearrange("a b -> (a b)")
            queue.dma_start(dst[r:r + n, :], v.rearrange("(r p) -> r p", p=P)).then_inc(in_vec, 16)

        LOADS_A = [(rowsA, A_MEMG, mem_norm_g), (rowsA, A_PREMIX, pre_mix_g), (rowsA, A_PREFFN, pre_ffn_g),
                   (rowsA, A_POSK, nsa_cmp_pos_k[0]), (rowsA, A_POSV, nsa_cmp_pos_v[0])]
        LOADS_B = [(rowsB, B_MU, rwkv_mu[0]), (rowsB, B_W0, rwkv_w0[0]), (rowsB, B_A0, rwkv_a0[0]),
                   (rowsB, B_KK, rwkv_k_k[0]), (rowsB, B_KA, rwkv_k_a[0]), (rowsB, B_RK, rwkv_r_k[0]),
                   (rowsB, B_LNG, rwkv_ln_g[0]), (rowsB, B_LNB, rwkv_ln_b[0])]
        N_VEC = len(LOADS_A) + len(LOADS_B)

        @block.sync
        def _(sp):
            def load_piece(i):
                if i >= RAW:
                    sp.wait_ge(lo_done, i - RAW + 1)
                sp.dma_start(raw_view(i), pieces[i]).then_inc(landed[i % RAW], 16)

            sp.dma_start(hn[:], mem[0].rearrange("(t p) d -> p t d", p=P)).then_inc(in_mem, 16)
            for item in LOADS_B:
                rows(sp, *item)
            load_piece(0)
            load_piece(1)
            sp.dma_start(h[:], x[0].rearrange("(t p) d -> p t d", p=P)).then_inc(in_x, 16)
            for i in range(2, NPIECES):
                load_piece(i)
            for t in range(TT):
                sp.wait_ge(p_h, 2 * 3 + t + 1)
                sp.dma_start(out[0, t * P:(t + 1) * P, :], h[:, t, :]).then_inc(stored, 16)
            sp.wait_ge(stored, 16 * TT)


        def rows_of(head):
            return slice(HD * (head % 2), HD * (head % 2) + HD)

        nsa_units = [(f, e, t, "nsa") for f in range(FT) for e in range(2) for t in range(TT)]
        mem_units = [(f, e, t, "mem") for f in range(FT, KD) for e in range(2) for t in range(TT)]
        UNITS = [nsa_units + mem_units, mem_units]
        UBASE = [0, len(nsa_units + mem_units)]
        FBASE = [0, KD - FT]
        SC_BANK, PT_BANK = (0, 1, 4), (2, 3, 5)
        LAG_T, LAG_V = 3, 5

        def branches(unit):
            return (2, unit[2] + 1) if unit[3] == "nsa" else (1, TT)

        TURNS = ([("dup", j) for j in range(6)] + [("q", f) for f in range(FT)]
                 + [("dup", j) for j in range(6, 12)] + [("mq", 0), ("mq", 1), ("mk", 0), ("mk", 1)])
        NTURN = len(TURNS) // 2

        PE_STEPS = ["gram", "sq2", "r2", "sq4", "r3", "sq8", "j", "f", "z", "f2", "uj", "f4", "uf", "uf2", "uf4", "y", "s"]
        DVE_STEPS = ["Dt", "D", "Et", "K", "R2", "R3", "J", "Z", "U1", "U2", "U3", "U"]
        ACT_STEPS = ["S2", "S4", "S8", "F", "F2", "F4", "Y", "S"]
        NPAIR = FT // 2
        Y_BANK = (0, 1, 4)
        ROUNDS = TT * NPAIR

        DVE_AFTER = dict(zip(DVE_STEPS, ["gram"] * 4 + ["r2", "r3", "j", "z", "uj", "uf", "uf2", "uf4"]))
        ACT_AFTER = dict(zip(ACT_STEPS, ["sq2", "sq4", "sq8", "f", "f2", "f4", "y", "s"]))
        PE_AFTER = dict(zip(PE_STEPS, PE_STEPS))
        STAGGER = 0

        def in_turn(after):
            todo = [(len(PE_STEPS) * d + PE_STEPS.index(pe_step) + STAGGER * s, s, i, d, name)
                    for d in range(ROUNDS) for s in range(2) for i, (name, pe_step) in enumerate(after.items())
                    if d < NPAIR or pe_step != "s"]
            return [(d, s, name) for _, s, _, d, name in sorted(todo)]

        def normed_heads(d):
            t, c, k = d // NPAIR, 2 * P * (d % NPAIR), 4 * (d % NPAIR)
            return (y_tok[:, t, c:c + 2 * P].rearrange("p (h n) -> p h n", n=HD),
                    gsq[:, c:c + 2 * P].rearrange("p (h n) -> p h n", n=HD), [g[:, k:k + 4] for g in gst])

        def step(steps, d, name):
            last = 1 if steps[-1] in ("s", "S") else 0
            return len(steps) * d - last * max(0, d - NPAIR) + steps.index(name) + 1

        @block.gpsimd
        def _(pool):
            chain = [0]

            def link(ins):
                chain[0] += 1
                ins.then_inc(s_pool, 1)
                pool.wait_ge(s_pool, chain[0])

            link(pool.memset(ident[:], 0.0))
            pool.affine_select(ident[:], ident[:], [[-1, P]], ALU.not_equal, 1.0, base=0,
                               channel_multiplier=1).then_inc(consts, 1)
            pool.memset(cst[:, 0:1], EPS).then_inc(consts, 1)
            pool.memset(cst[:, 1:2], GN_EPS).then_inc(consts, 1)
            link(pool.memset(posi[:], 0))
            pool.dma_start(posi[:, 0:TT], positions[0].rearrange("(t p) -> p t", p=P),
                           allow_slow_non_contiguous=True).then_inc(in_small, 16)
            for g in range(GROUPS):
                pool.dma_start(posi[g * NCMP:(g + 1) * NCMP, TT:TT + 1],
                               positions[:, CMP_BLOCK - 1:SEQ:CMP_STRIDE].rearrange("a n -> n a"),
                               allow_slow_non_contiguous=True).then_inc(in_small, 16)
            pool.dma_start(gateb[:], nsa_gate_b.to_broadcast([P, GATES])).then_inc(in_small, 16)
            for dst, src in ((w2k, nsa_cmp_k_w2), (w2v, nsa_cmp_v_w2)):
                pool.dma_start(dst[:], src[0].rearrange("(k p) n -> p k n", p=P)).then_inc(in_small, 16)

            for i in range(HALF):
                pool.memset(invf[:, :, i:i + 1], float(np.float32(ROPE_THETA) ** np.float32(-i / HALF))).then_inc(consts, 1)
            link(pool.memset(cmask[:], 0.0))
            pool.affine_select(cmask[:, P:], cmask[:, P:], [[-1, P]], ALU.is_ge, NEG, base=0,
                               channel_multiplier=1).then_inc(consts, 1)
            link(pool.memset(bcmask[:], 0.0))
            bc = bcmask[:].rearrange("p (t n) -> p t n", t=TT)
            pool.affine_select(bc, bc, [[P, TT], [-CMP_STRIDE, NCMP]], ALU.is_ge, NEG,
                               base=1 - CMP_BLOCK, channel_multiplier=1).then_inc(consts, 1)
            link(pool.memset(rowok[:], 1.0))
            pool.affine_select(rowok[:], rowok[:], [[P, TT]], ALU.is_ge, 0.0, base=1 - CMP_BLOCK,
                               channel_multiplier=1).then_inc(consts, 1)

            def load_gain(m):
                if m:
                    pool.wait_ge(p_tmp, TT * m)
                g = (post_mix_g, post_ffn_g)[m % 2]
                pool.dma_start(gain[:], g[m // 2:m // 2 + 1, :].to_broadcast([P, D])).then_inc(in_gain, 16)

            link(pool.memset(bones[:], 1.0))
            v = bones[:].rearrange("p (b c) -> p b c", c=HD)
            link(pool.affine_select(v, v, [[-HD, 2], [0, HD]], ALU.is_ge, 0.0, base=0, channel_multiplier=1))
            pool.affine_select(v, v, [[HD, 2], [0, HD]], ALU.is_ge, 0.0, base=HD - 1, channel_multiplier=-1).then_inc(consts, 1)
            pool.memset(cst[:, 2:3], 1.0).then_inc(consts, 1)
            load_gain(0)

            pool.wait_ge(tok_evA, 4)
            pool.wait_ge(tok_evD, 4)
            for t in range(TT):
                for c in range(2):
                    pool.tensor_copy(dup[:, t, 0:6, HD * c:HD * c + HD],
                                     pr[:, t, O_KC:O_KS].rearrange("p (j d) -> p j d", d=HD)).then_inc(dup_c, 1)
            pool.wait_ge(roped_k, 2)
            for b, col in enumerate((O_KS, O_KW)):
                for t in range(TT):
                    for c in range(2):
                        pool.tensor_copy(dup[:, t, 6 + 3 * b:9 + 3 * b, HD * c:HD * c + HD],
                                         pr[:, t, col:col + KVW].rearrange("p (j d) -> p j d", d=HD)).then_inc(dup_k, 1)

            def scale_probs(layer):
                for i, unit in enumerate(UNITS[layer]):
                    u = UBASE[layer] + i
                    nbr, nk = branches(unit)
                    pool.wait_ge(a_coef, u + 1)
                    for b in range(nbr):
                        v = SM[layer][:, u % SLOTS, b, 0:nk * P]
                        ins = pool.tensor_scalar(v, v, coef[:, u % SLOTS, b:b + 1], None, ALU.mult)
                    ins.then_inc(a_p, 1)

            scale_probs(0)
            load_gain(1)
            pool.wait_ge(n_tp, 16)
            pool.dma_start(lora[0:LORA, :], rwkv_w2[0]).then_inc(in_lora, 16)
            pool.dma_start(lora[LORA:P, :], rwkv_a2[0]).then_inc(in_lora, 16)
            pool.dma_start(g2[:], rwkv_g2[0]).then_inc(in_lora, 16)
            load_gain(2)
            pool.wait_ge(p_h, 4)
            for i in range(2):
                pool.memset(shb[i][:, :, 0:1], 0.0).then_inc(shb_zero, 1)
            pool.memset(cs[:, :, :, 0:1], 0.0).then_inc(shb_zero, 1)
            pool.wait_ge(kk_ok, 1)
            pool.tensor_tensor(eP_sq[:], kkT[:], kkT[:], ALU.mult).then_inc(sq_ok, 1)
            scale_probs(1)
            pool.wait_ge(shifted, 10)
            link(pool.memset(dmask[:], 1.0))
            up = [[1, P]]
            m = [dmask[:, i, :] for i in range(6)]
            for i in (0, 2):
                ins = pool.affine_select(m[i], m[i], up, ALU.is_ge, 0.0, base=-1, channel_multiplier=-1)
            for i in (1, 3):
                pool.affine_select(m[i], m[i], up, ALU.is_ge, 0.0, base=0, channel_multiplier=-1)
            for i in (4, 5):
                ins = pool.affine_select(m[i], m[i], [[-1, P]], ALU.is_ge, 0.0, base=-1, channel_multiplier=1)
            link(ins)
            for i in (0, 4):
                v = m[i].rearrange("p (b c) -> p b c", c=BLK)
                link(pool.affine_select(v, v, [[-BLK, P // BLK], [0, BLK]], ALU.is_ge, 0.0, base=0, channel_multiplier=1))
                link(pool.affine_select(v, v, [[BLK, P // BLK], [0, BLK]], ALU.is_ge, 0.0, base=BLK - 1, channel_multiplier=-1))
            pool.tensor_tensor(m[5], m[5], m[4], ALU.subtract).then_inc(dm_ok, 1)
            def gn_square(d):
                pool.wait_ge(gn_sub, d + 1)
                y3, q3, _ = normed_heads(d)
                pool.tensor_tensor(q3, y3, y3, ALU.mult).then_inc(gn_sq, 1)

            for d, s, _ in in_turn({"R": "gram"}):
                b = PB[s]
                pool.wait_ge(pv[s], step(DVE_STEPS, d, "D"))
                pool.tensor_tensor(b["R"][:], b["DA"][:, :, 0, :], ident[:].unsqueeze(1).to_broadcast([P, 2, P]),
                                   ALU.add).then_inc(pp[s], 1)
                if d and s:
                    gn_square(d - 1)
            gn_square(ROUNDS - 1)
            for j in range(FT // 2):
                pool.wait_ge(y_sc, j + 1)
                pool.tensor_tensor(y_fin[:, 2 * j:2 * j + 2, :], y_fin[:, 2 * j:2 * j + 2, :], rT[:, 2 * j:2 * j + 2, :],
                                   ALU.add).then_inc(y_add, 1)
            load_gain(3)

        @block.tensor
        def _(pe):
            def three(dst, ah, al, bh, bl, start, stop):
                pe.matmul(dst, ah, bh, start=start, stop=False)
                pe.matmul(dst, ah, bl, start=False, stop=False)
                return pe.matmul(dst, al, bh, start=False, stop=stop)

            def norm(n):
                for t in range(TT):
                    pe.wait_ge((n_scA, n_scD)[t], n + 1)
                    for b in range(KD // 2):
                        for j in range(2):
                            k = 2 * b + j
                            ins = pe.transpose(psum[:, b, j * SEQ + t * P:j * SEQ + (t + 1) * P],
                                               hn[:, t, k * P:(k + 1) * P], ident[:])
                        if t:
                            ins.then_inc(n_tp, 1)

            def normed(n, kk):
                if kk % 2 == 0:
                    pe.wait_ge(n_lo, 4 * n + kk // 2 + 1)

            def token_gemm(g, ah, al):
                i0 = first["mem"] if g == 0 else first["nsa"] + 2 * (g - 1)
                n = pieces[i0].shape[2]
                for hf in range(2):
                    pe.wait_ge(lo_done, i0 + hf + 1)
                    for t in range(TT):
                        if hf == 0 and g >= 2:
                            pe.wait_ge((tok_evA, tok_evD)[t], g - 1)
                        for k in range(4):
                            kk = 4 * hf + k
                            if g < 2 and t == 0:
                                normed(g, kk)
                            ins = three(psum[:, 4 + 2 * (g % 2) + t, 0:n], ah[:, kk, t * P:(t + 1) * P],
                                        al[:, kk, t * P:(t + 1) * P], kt_of(w_hi, i0 + hf, k), kt_of(w_lo, i0 + hf, k),
                                        start=kk == 0, stop=kk == KD - 1)
                        if hf == 1 and t == 0:
                            ins.then_inc(tok_mm, 1)
                            if g == 0:
                                norm(1)
                    ins.then_inc(used, 1)

            def turn(k):
                if k >= 4:
                    pe.wait_ge((tp0A, tp0D)[k % 2], (k - 4) // 2 + 1)
                for j in range(2):
                    kind, n = TURNS[2 * k + j]
                    for t in range(TT):
                        src = {"dup": lambda: dup[:, t, n, :], "q": lambda: pr[:, t, n * P:(n + 1) * P],
                               "mq": lambda: pr[:, t, O_MQ + n * P:O_MQ + (n + 1) * P],
                               "mk": lambda: mkv[:, t, n * P:(n + 1) * P]}[kind]()
                        ins = pe.transpose(psum[:, k % 4, j * SEQ + t * P:j * SEQ + (t + 1) * P], src, ident[:])
                ins.then_inc(tp0, 1)

            def cmp_gemm():
                for kv in range(2):
                    pe.wait_ge(kp_hi, kv + 1)
                    pe.wait_ge(kp_lo, kv + 1)
                    for hf in range(2):
                        i = first["cmp"] + 2 * kv + hf
                        pe.wait_ge(lo_done, i + 1)
                        for j in range(CJ // 2):
                            jj = CJ // 2 * hf + j
                            ins = three(psum[0:GROUPS * NCMP, 4 + kv, 0:CMP_HIDDEN], kph[kv][:, jj, :], kpl[kv][:, jj, :],
                                        kt_of(w_hi, i, j), kt_of(w_lo, i, j), start=jj == 0, stop=jj == CJ - 1)
                        ins.then_inc(used, 1)

            def scores(layer, i):
                unit = UNITS[layer][i]
                u = UBASE[layer] + i
                f, e, t, kind = unit
                nbr, nk = branches(unit)
                if u >= SLOTS:
                    pe.wait_ge(a_max, u - SLOTS + 1)
                r = rows_of(e)
                for b in range(nbr):
                    if kind == "nsa":
                        lhs, rhs = qT[r, f, t * P:(t + 1) * P], kT[r, 3 * b + f // 2, 0:nk * P]
                    else:
                        lhs, rhs = mqT[r, f - FT, t * P:(t + 1) * P], mkT[r, f - FT, :]
                    ins = pe.matmul(psum[:, SC_BANK[u % SLOTS], b * SEQ:b * SEQ + nk * P], lhs, rhs, start=True, stop=True)
                ins.then_inc(a_sc, 1)

            def probs_turn(layer, i):
                unit = UNITS[layer][i]
                u = UBASE[layer] + i
                nbr, nk = branches(unit)
                pe.wait_ge(a_p, u + 1)
                if u >= SLOTS:
                    pe.wait_ge((a_ptA, a_ptD)[(u - SLOTS) % 2], (u - SLOTS) // 2 + 1)
                for b in range(nbr):
                    for k in range(nk):
                        ins = pe.transpose(psum[:, PT_BANK[u % SLOTS], (b * nk + k) * P:(b * nk + k + 1) * P],
                                           SM[layer][:, u % SLOTS, b, k * P:(k + 1) * P], ident[:])
                ins.then_inc(a_tp, 1)

            def values(layer, i):
                unit = UNITS[layer][i]
                u = UBASE[layer] + i
                f, e, t, kind = unit
                nbr, nk = branches(unit)
                head = 2 * f + e
                pe.wait_ge((a_ptA, a_ptD)[u % 2], u // 2 + 1)
                fi = f + FBASE[layer]
                if e == 0 and t == 0 and (f >= 2 or layer):
                    pe.wait_ge(a_lo, fi - 1)
                dst = psum[rows_of(e), 6 + f % 2, t * P:(t + 1) * P]
                todo = []
                for b in range(nbr):
                    for k in range(nk):
                        if kind == "nsa":
                            c = (O_VS, O_VW)[b] + HD * (f // 2)
                            lhs = pr[:, k, c:c + HD]
                        else:
                            c = MEM_W + HD * (head - HEADS)
                            lhs = mkv[:, k, c:c + HD]
                        todo.append((lhs, PT[layer][:, u % SLOTS, b * nk + k, :]))
                if kind == "nsa":
                    todo.append((vcs[:, f // 2, :], pcT[:, t, head, :]))
                for n, (lhs, rhs) in enumerate(todo):
                    ins = pe.matmul(dst, lhs, rhs, start=n == 0, stop=n == len(todo) - 1)
                ins.then_inc(a_pv, 1)

            def attention(layer):
                n = len(UNITS[layer])
                for s in range(n + LAG_V):
                    if s < n:
                        scores(layer, s)
                    if 0 <= s - LAG_T < n:
                        probs_turn(layer, s - LAG_T)
                    if 0 <= s - LAG_V < n:
                        values(layer, s - LAG_V)

            def full_gemm(i0, kt_n, ah, al, ready=None, base=0, n_ready=0):
                for j in range(kt_n // 2):
                    pe.wait_ge(lo_done, i0 + j + 1)
                    if j < n_ready:
                        pe.wait_ge(ready, base + j + 1)
                    for t in range(TT):
                        for nh in range(2):
                            for k in range(2):
                                kk = 2 * j + k
                                c = slice(512 * nh, 512 * nh + 512)
                                ins = three(psum[:, GEMM_ACC[2 * t + nh], :], ah[:, kk, t * P:(t + 1) * P],
                                            al[:, kk, t * P:(t + 1) * P], kt_of(w_hi, i0 + j, k)[:, c],
                                            kt_of(w_lo, i0 + j, k)[:, c], start=kk == 0, stop=kk == kt_n - 1)
                        if t == 0 and j == kt_n // 2 - 1:
                            ins.then_inc(p_acc, 1)
                    ins.then_inc(used, 1)

            def feature_strip(i, bank, norm_step=None):
                pe.wait_ge(lo_done, i + 1)
                for j in range(2):
                    c = slice(P * j, P * j + P)
                    for k in range(KD):
                        if norm_step is not None and j == 0:
                            normed(norm_step, k)
                        ins = three(psum[:, bank, j * SEQ:(j + 1) * SEQ], kt_of(w_hi, i, k)[:, c],
                                    kt_of(w_lo, i, k)[:, c], xh[:, k, :], xl[:, k, :], start=k == 0, stop=k == KD - 1)
                ins.then_inc(used, 1)

            def ffn(layer):
                for c in range(NFC):
                    if c >= 2:
                        pe.wait_ge(up_mul, NFC * layer + c - 1)
                    for part in range(2):
                        feature_strip(first["up", layer] + 2 * c + part, 2 * (c % 2) + part,
                                      2 + 2 * layer if c == 0 and part == 0 else None)
                pe.wait_ge(up_mul, NFC * layer + NFC - 1)
                full_gemm(first["down", layer], KF, hh, hl, up_lo, NFC * layer, NFC)

            pe.wait_ge(consts, 1)
            pe.wait_ge(in_vec, 16 * N_VEC)
            pe.transpose(psum[:, 7, 0:NA], rowsA[:], ident[0:NA, 0:NA])
            pe.transpose(psum[:, 7, P:P + NB], rowsB[:], ident[0:NB, 0:NB]).then_inc(vec_tp, 1)
            norm(0)
            token_gemm(0, mh, ml)
            for g in range(1, 5):
                token_gemm(g, xh, xl)
            pe.wait_ge(dup_c, 4)
            for k in range(3):
                turn(k)
            token_gemm(5, xh, xl)
            cmp_gemm()
            pe.wait_ge(roped_q, 1)
            for k in range(3, 5):
                turn(k)
            pe.wait_ge(c_gelu, 2)
            pe.wait_ge(tok_evA, 6)
            n = GROUPS * NCMP
            for kv in range(2):
                for k in range(2):
                    ins = pe.transpose(psum[:, 6, (2 * kv + k) * n:(2 * kv + k + 1) * n],
                                       hc[:, kv, k * P:(k + 1) * P], ident[0:n, 0:n])
            ins.then_inc(c_tp, 1)
            turn(5)
            pe.wait_ge(dup_k, 8)
            turn(6)
            pe.wait_ge(c_ht, 1)
            pe.wait_ge(tok_evD, 6)
            pe.wait_ge(in_small, 16 * 7)
            for k in range(2):
                pe.matmul(psum[0:n, 7, 0:HD], hcT[:, k, :], w2k[:, k, :], start=k == 0, stop=k == 1)
            for g in range(GROUPS):
                for k in range(2):
                    ins = pe.matmul(psum[0:NCMP, 7, HD * (g + 1):HD * (g + 2)], hcT[:, 2 + k, NCMP * g:NCMP * (g + 1)],
                                    w2v[:, k, :], start=k == 0, stop=k == 1)
            ins.then_inc(c_w2, 1)
            for k in range(7, NTURN):
                turn(k)
            pe.wait_ge(c_kd, 1)
            pe.transpose(psum[:, 7, 256:256 + n], kcd[:].rearrange("p c d -> p (c d)"), ident[0:n, 0:n]).then_inc(c_kt, 1)
            pe.wait_ge(c_ktv, 1)
            pe.wait_ge(tp0A, (NTURN + 1) // 2)
            pe.wait_ge(tp0D, NTURN // 2)
            for t in range(TT):
                for head in range(HEADS):
                    r = rows_of(head)
                    g = head // (HEADS // GROUPS)
                    ins = pe.matmul(psum[:, 4 + 2 * t + head % 2, head // 2 * NCMP:(head // 2 + 1) * NCMP], qT[r, head // 2, t * P:(t + 1) * P],
                                    kcT[r, g * NCMP:(g + 1) * NCMP], start=True, stop=True)
                ins.then_inc(b_sc, 1)
            for t in range(TT):
                pe.wait_ge(b_p, TT)
                for q in range(3):
                    for i in range(4):
                        head = 4 * q + i
                        ins = pe.transpose(psum[0:NCMP, 3 * t + q, i * P:(i + 1) * P], sc[:, t, head, :], ident[:])
                    ins.then_inc(b_tp, 1)
            pe.wait_ge(b_pt, 6)
            attention(0)
            pe.wait_ge(a_lo, KD)
            full_gemm(first["out", 0], KD, xh, xl)
            norm(2)
            ffn(0)

            norm(3)

            def strip(q):
                if q >= 2:
                    pe.wait_ge(fm_out, q - 1)
                feature_strip(first["rwkv"] + q, 4 + q % 2, 3 if q == 0 else None)

            strip(0)
            strip(1)
            pe.wait_ge(in_lora, 48)
            pe.wait_ge(l_act, 2)
            pe.wait_ge(shifted, 1)
            pe.wait_ge(a_lo, KD)
            for j in range(FT // 2):
                if j:
                    pe.wait_ge(z_ev, j)
                for i in range(2):
                    f = 2 * j + i
                    ins = pe.matmul(psum[:, 6, i * SEQ:(i + 1) * SEQ], lora[0:LORA, f * P:(f + 1) * P], wg[0:LORA, 0, :],
                                    start=True, stop=True)
                ins.then_inc(z_mm, 1)
                if j:
                    pe.wait_ge(a_ev, j)
                for i in range(2):
                    f = 2 * j + i
                    ins = pe.matmul(psum[:, 7, i * SEQ:(i + 1) * SEQ], lora[LORA:P, f * P:(f + 1) * P], wg[LORA:P, 0, :],
                                    start=True, stop=True)
                ins.then_inc(a_mm, 1)
            strip(2)
            for j in range(FT // 2):
                for i in range(2):
                    f = 2 * j + i
                    ins = pe.matmul(psum[:, j, i * SEQ:(i + 1) * SEQ], g2[:, f * P:(f + 1) * P], wg[:, 1, :], start=True, stop=True)
                ins.then_inc(g_mm, 1)
            strip(3)
            strip(4)
            pe.wait_ge(sq_ok, 1)
            pe.wait_ge(g_ev, 3)
            for j in range(FT // 2):
                for i in range(2):
                    ins = pe.matmul(psum[:, j, i * SEQ:(i + 1) * SEQ], bones[:], eP_sq[:, 2 * j + i, :], start=True, stop=True)
                ins.then_inc(ss_mm, 1)
            for q in range(5, 9):
                strip(q)
            pe.wait_ge(rk_ok, 1)
            pe.wait_ge(ss_ev, 3)
            for j in range(FT // 2):
                for i in range(2):
                    ins = pe.matmul(psum[:, j, i * SEQ:(i + 1) * SEQ], bones[:], rT[:, 2 * j + i, :], start=True, stop=True)
                ins.then_inc(bo_mm, 1)
            strip(9)
            strip(10)
            pe.wait_ge(bk_ok, 1)
            pe.wait_ge(shifted, 10)
            pe.wait_ge(bo_ev, 3)
            for f in range(FT):
                if f >= 2:
                    pe.wait_ge(tk_ev, f - 1)
                for i, src in enumerate((vT[:, f, 0:P], vT[:, f, P:SEQ], aT[:, f, 0:P], k_T[:, f, 0:P])):
                    ins = pe.transpose(psum[:, 3 * (f % 2), i * P:(i + 1) * P], src, ident[:])
                ins.then_inc(tk_mm, 1)
            pe.wait_ge(tk_ev, 6)
            pe.wait_ge(fm_out, 11)
            attention(1)

            def gemm2(s, bank, pairs):
                for kind, (lhs, rhs) in enumerate(pairs):
                    for e in range(2):
                        ins = pe.matmul(psum[:, bank, (2 * kind + e) * P:(2 * kind + e + 1) * P], lhs(e), rhs(e), start=True, stop=True)
                ins.then_inc(pm[s], 1)

            def applied(s, bank, lhs, rhs):
                for e in range(2):
                    ins = pe.matmul(psum[:, bank, e * HD:(e + 1) * HD], lhs(e), rhs(e), start=True, stop=True)
                ins.then_inc(pm[s], 1)

            pe.wait_ge(a_lo, KD + KD - FT)
            pe.wait_ge(ar_ok, 1)
            for d, s, name in in_turn(PE_AFTER):
                t = d // NPAIR

                def V(s, n, d=d):
                    pe.wait_ge(pv[s], step(DVE_STEPS, d, n))

                def A(s, n, d=d):
                    pe.wait_ge(pa[s], step(ACT_STEPS, d, n))

                b, B0 = PB[s], 4 * s
                f = 2 * (d % NPAIR) + s
                D, Arb = (lambda e: b["DA"][:, e, 0, :]), (lambda e: b["DA"][:, e, 1, :])
                Aak, Ark = (lambda e: b["KR"][:, e, 0, :]), (lambda e: b["KR"][:, e, 1, :])
                Dt, Et = (lambda e: b["T"][:, 0, e, :]), (lambda e: b["T"][:, 1, e, :])
                p2, p2t = (lambda e: b["S2"][:, 0, e, :]), (lambda e: b["S2"][:, 1, e, :])
                p4, p4t = (lambda e: b["S4"][:, 0, e, :]), (lambda e: b["S4"][:, 1, e, :])
                p8, R = (lambda e: b["S8"][:, e, :]), (lambda e: b["R"][:, e, :])
                U0, U1 = (lambda e: b["U"][0][:, e, :]), (lambda e: b["U"][1][:, e, :])
                vv = lambda e: tk[:, t, f * P + e * HD:f * P + (e + 1) * HD]
                if name == "gram":
                    if d:
                        pe.wait_ge(pv[s], step(DVE_STEPS, d - 1, "U"))
                        pe.wait_ge(pa[s], step(ACT_STEPS, d - 1, "S" if d <= NPAIR else "Y"))
                    for e in range(2):
                        r = rows_of(e)
                        tok = slice(t * P, (t + 1) * P)
                        ar = art[r, f, t, :, :].rearrange("p c n -> p (c n)")
                        pe.matmul(psum[:, B0 + e, 0:2 * P], aT[r, f, tok], ar, start=True, stop=True)
                        pe.matmul(psum[:, B0 + e, 2 * P:4 * P], k_T[r, f, tok], ar, start=True, stop=True)
                        ins = pe.matmul(psum[:, B0 + 2 + e, 0:P], art[r, f, t, 0, :], aT[r, f, tok], start=True, stop=True)
                    ins.then_inc(pm[s], 1)
                elif name == "sq2":
                    V(s, "Et")
                    gemm2(s, B0 + 2, [(Dt, D), (D, Dt)])
                elif name == "r2":
                    A(s, "S2")
                    pe.wait_ge(pp[s], d + 1)
                    gemm2(s, B0 + 3, [(p2t, R)])
                elif name == "sq4":
                    V(s, "K")
                    gemm2(s, B0, [(p2t, p2), (p2, p2t)])
                elif name == "r3":
                    A(s, "S4")
                    V(s, "R2")
                    gemm2(s, B0 + 1, [(p4t, R)])
                elif name == "sq8":
                    gemm2(s, B0 + 2, [(p4, p4t)])
                elif name == "j":
                    A(s, "S8")
                    V(s, "R3")
                    gemm2(s, B0 + 3, [(p8, R)])
                elif name == "f":
                    V(s, "J")
                    gemm2(s, B0, [(Et, R), (R, Et)])
                elif name == "z":
                    for e in range(2):
                        ins = pe.matmul(psum[:, B0 + 2 + e, 0:HD], Aak(e), vv(e), start=True, stop=t == 0)
                    if t:
                        for e in range(2):
                            ins = pe.matmul(psum[:, B0 + 2 + e, 0:HD], art[rows_of(e), f, t, 0, :], st[rows_of(e), f, :],
                                            start=False, stop=True)
                    ins.then_inc(pm[s], 1)
                elif name == "f2":
                    A(s, "F")
                    gemm2(s, B0 + 1, [(p2t, p2), (p2, p2t)])
                elif name == "uj":
                    V(s, "Z")
                    applied(s, B0 + 3, R, U0)
                elif name == "f4":
                    A(s, "F2")
                    gemm2(s, B0 + 2, [(p4t, p4)])
                elif name == "uf":
                    V(s, "U1")
                    applied(s, B0, p2, U1)
                elif name == "uf2":
                    V(s, "U2")
                    applied(s, B0 + 1, p4, U0)
                elif name == "uf4":
                    V(s, "U3")
                    A(s, "F4")
                    applied(s, B0 + 3, p8, U1)
                elif name == "y":
                    V(s, "U")
                    for e in range(2):
                        dst = psum[:, B0 + e, 0:HD]
                        pe.matmul(dst, Arb(e), U0(e), start=True, stop=False)
                        ins = pe.matmul(dst, Ark(e), vv(e), start=False, stop=t == 0)
                    if t:
                        for e in range(2):
                            ins = pe.matmul(psum[:, B0 + e, 0:HD], art[rows_of(e), f, t, 1, :], st[rows_of(e), f, :],
                                            start=False, stop=True)
                    ins.then_inc(pm[s], 1)
                else:
                    for e in range(2):
                        dst = psum[rows_of(e), B0 + 2, 0:HD]
                        c = slice(f * P + e * HD, f * P + (e + 1) * HD)
                        pe.matmul(dst, tk[:, 2, c], U0(e), start=True, stop=False)
                        ins = pe.matmul(dst, tk[:, 3, c], vv(e), start=False, stop=True)
                    ins.then_inc(pm[s], 1)
            for s in range(2):
                pe.wait_ge(pa[s], step(ACT_STEPS, ROUNDS - 1, "Y"))
            for j in range(FT // 2):
                pe.wait_ge(gn_ok, NPAIR + j + 1)
                for i in range(2):
                    for t in range(TT):
                        f = 2 * j + i
                        ins = pe.transpose(psum[:, Y_BANK[j], i * SEQ + t * P:i * SEQ + (t + 1) * P], y_tok[:, t, f * P:(f + 1) * P], ident[:])
                ins.then_inc(y_mm, 1)
            full_gemm(first["out", 1], KD, xh, xl, y_lo, 0, FT // 2)
            norm(4)
            ffn(1)

        @block.scalar
        def _(act):
            split = [0]

            def split_to(n):
                for i in range(split[0], min(n, NPIECES)):
                    act.wait_ge(landed[i % RAW], land_value[i])
                    if i >= SPL:
                        act.wait_ge(used, i - SPL + 1)
                    act.activation(w_hi[:, i % SPL, 0:size(i)], raw[:, i % RAW, 0:size(i)], ACT.Copy).then_inc(hi_done, 1)
                split[0] = max(split[0], min(n, NPIECES))

            def norm(n):
                src = hn if n == 0 else h
                dh = mh if n == 0 else xh
                if n == 0:
                    act.wait_ge(in_mem, 16)
                elif n == 1:
                    act.wait_ge(in_x, 16)
                    act.wait_ge(n_lo, 4)
                    act.wait_ge(n_tp, 4)
                else:
                    act.wait_ge(p_h, TT * (n - 2) + 1)
                act.activation(psum[:, 0:2, :], src[:, 0, :].rearrange("p (b n) -> p b n", b=2), ACT.Square,
                               accum_out=ssq[:, 0:1]).then_inc(n_sqA, 1)
                if n == 0:
                    act.wait_ge(consts, 2)
                for t in range(TT):
                    act.wait_ge((n_sqA, n_sqD)[t], n + 1)
                    act.activation(rms[:, t:t + 1], ssq[:, t:t + 1], ACT.Sqrt, bias=cst[:, 0:1], scale=1.0 / D).then_inc(n_rms, 1)
                    if t == 0:
                        act.wait_ge(n_inv, TT * n + 1)
                        act.activation(hn[:, 0, :], src[:, 0, :], ACT.Copy, scale=rin[:, 0:1]).then_inc(n_scA, 1)
                if n == 0:
                    split_to(1)
                    act.wait_ge(vec_ev, 1)
                elif n == 1:
                    split_to(3)
                for b in range(KD // 2):
                    act.wait_ge(n_tp, 4 * n + b + 1)
                    for j in range(2):
                        k = 2 * b + j
                        ins = act.activation(dh[:, k, :], psum[:, b, j * SEQ:(j + 1) * SEQ], ACT.Copy,
                                             scale=colA[:, NORM_COL[n] + k:NORM_COL[n] + k + 1])
                    ins.then_inc(n_hi, 1)

            def token_out(g):
                act.wait_ge(tok_mm, g + 1)
                dst = mkv[:, 0, :] if g == 0 else pr[:, 0, 512 * (g - 1):min(512 * g, NSA_IN)]
                act.activation(dst, psum[:, 4 + 2 * (g % 2), 0:dst.shape[1]], ACT.Copy).then_inc(tok_evA, 1)

            def turn_out(k):
                act.wait_ge(tp0, k + 1)
                src = psum[:, k % 4, :].rearrange("p (j n) -> p j n", j=2)
                kind, n = TURNS[2 * k]
                if k < 3:
                    act.activation(KC[0:HD, n:n + 2, :], src[0:HD], ACT.Copy)
                    act.activation(KC[HD:P, n:n + 2, 0:SEQ - 1], src[HD:P, :, 1:SEQ], ACT.Copy).then_inc(tp0A, 1)
                else:
                    dst = {"dup": kT, "q": qT, "mq": mqT, "mk": mkT}[kind]
                    n = n - 6 if kind == "dup" else n
                    act.activation(dst[:, n:n + 2, :], src, ACT.Copy).then_inc(tp0A, 1)

            def attention(layer):
                n = len(UNITS[layer])
                for s in range(n + LAG_V + 1):
                    if s < n:
                        u = UBASE[layer] + s
                        nbr, nk = branches(UNITS[layer][s])
                        act.wait_ge(a_max, u + 1)
                        for b in range(nbr):
                            v = SM[layer][:, u % SLOTS, b, 0:nk * P]
                            ins = act.activation(v, v, ACT.Exp, bias=nbias[:, u % SLOTS, b:b + 1], scale=SCALE,
                                                 accum_out=rsum[:, u % SLOTS, b:b + 1])
                        ins.then_inc(a_exp, 1)
                    i = s - LAG_T
                    if 0 <= i < n and (UBASE[layer] + i) % 2 == 0:
                        u = UBASE[layer] + i
                        nbr, nk = branches(UNITS[layer][i])
                        act.wait_ge(a_tp, u + 1)
                        if u >= SLOTS:
                            act.wait_ge(a_pv, u - SLOTS + 1)
                        act.activation(PT[layer][:, u % SLOTS, 0:nbr * nk, :],
                                       psum[:, PT_BANK[u % SLOTS], 0:nbr * nk * P].rearrange("p (k n) -> p k n", n=P),
                                       ACT.Copy).then_inc(a_ptA, 1)
                    i = s - LAG_V
                    if 0 <= i < n and i % 4 == 3:
                        f = UNITS[layer][i][0]
                        act.wait_ge(a_pv, UBASE[layer] + i + 1)
                        act.activation(xh[:, f, :], psum[:, 6 + f % 2, 0:SEQ], ACT.Copy).then_inc(a_hi, 1)

            def post(m, last_piece):
                for t in range(TT):
                    if t == 0:
                        act.wait_ge(p_acc, m + 1)
                    else:
                        act.wait_ge(used, last_piece)
                    act.activation(psum[:, 4 * t:4 * t + 2, :], psum[:, 4 * t + 2:4 * t + 4, :], ACT.Square,
                                   accum_out=ssq[:, 2 + t:3 + t]).then_inc(p_sq, 1)
                    act.wait_ge(p_sq, TT * m + t + 1)
                    act.activation(post_rms[:, t:t + 1], ssq[:, 2 + t:3 + t], ACT.Sqrt, bias=cst[:, 0:1],
                                   scale=1.0 / D).then_inc(p_rms, 1)

            def ffn(layer):
                u0 = NFC * layer

                def hidden_hi(c):
                    act.wait_ge(up_mul, u0 + c + 1)
                    act.activation(hh[:, 2 * c:2 * c + 2, :], hid[:], ACT.Copy).then_inc(up_hi, 1)

                for c in range(NFC):
                    i = first["up", layer] + 2 * c
                    split_to(i + 3)
                    act.wait_ge(used, i + 1)
                    if c:
                        act.wait_ge(up_mul, u0 + c)
                    act.activation(sg[:], psum[:, 2 * (c % 2), :].rearrange("p (j n) -> p j n", j=2), ACT.Silu).then_inc(up_silu, 1)
                    if c:
                        hidden_hi(c - 1)
                    split_to(i + 4)
                hidden_hi(NFC - 1)
                i0 = first["down", layer]
                for j in range(KF // 2):
                    split_to(i0 + j + 3)

            for item in LOADS_A:
                rows(act, *item)
            norm(0)
            split_to(2)
            norm(1)
            split_to(3)
            token_out(0)
            split_to(4)
            act.wait_ge(trig_r, 1)
            act.activation(trig[:], ang[:], ACT.Sin).then_inc(trig_s, 1)
            for g in range(1, 6):
                i = first["nsa"] + 2 * (g - 1)
                split_to(i + 3)
                split_to(i + 4)
                token_out(g)
                if g == 4:
                    split_to(i + 5)
                    turn_out(0)
                    turn_out(2)
                    act.wait_ge(kp_f, 1)
                    act.activation(kph[0][:], kpf[:], ACT.Copy).then_inc(kp_hi, 1)
                    act.wait_ge(kp_f, 2)
                    act.activation(kph[1][:], kpf[:], ACT.Copy).then_inc(kp_hi, 1)
            i = first["cmp"]
            split_to(i + 3)
            act.wait_ge(gl_s, 1)
            act.activation(gates[:], gates[:], ACT.Sigmoid).then_inc(gate_s, 1)
            split_to(i + 4)
            for kv in range(2):
                act.wait_ge(used, i + 2 * kv + 2)
                if kv == 0:
                    act.wait_ge(kp_lo, 2)
                act.activation(hc[:, kv, :], psum[0:GROUPS * NCMP, 4 + kv, 0:CMP_HIDDEN], ACT.Gelu_apprx_tanh).then_inc(c_gelu, 1)
            turn_out(4)
            act.wait_ge(c_tp, 1)
            act.activation(hcT[:], psum[:, 6, 0:4 * GROUPS * NCMP].rearrange("p (k n) -> p k n", k=4), ACT.Copy).then_inc(c_ht, 1)
            for k in range(6, NTURN, 2):
                turn_out(k)
            act.wait_ge(c_kt, 1)
            act.activation(kcT[:], psum[:, 7, 256:256 + GROUPS * NCMP], ACT.Copy).then_inc(c_ktv, 1)
            split_to(i + 7)
            for t in range(TT):
                act.wait_ge(b_sub, t + 1)
                v = sc[:, t].rearrange("p h n -> p (h n)")
                act.activation(v, v, ACT.Exp, scale=SCALE).then_inc(b_exp, 1)
            for t in range(TT):
                for q in range(3):
                    act.wait_ge(b_tp, 3 * t + q + 1)
                    act.activation(pcT[:, t, 4 * q:4 * q + 4, :],
                                   psum[0:NCMP, 3 * t + q, :].rearrange("p (h n) -> p h n", h=4), ACT.Copy).then_inc(b_pt, 1)
            attention(0)
            i = first["out", 0]
            for j in range(KD // 2):
                split_to(i + j + 3)
            post(0, i + KD // 2)
            norm(2)
            ffn(0)
            post(1, first["down", 0] + KF // 2)

            norm(3)

            def strip_out(q):
                act.wait_ge(used, first["rwkv"] + q + 1)
                src = psum[:, 4 + q % 2, :].rearrange("p (j n) -> p j n", j=2)
                if q == 10:
                    act.activation(mqT[:], src, ACT.Copy).then_inc(fm_out, 1)
                    return
                if q == 0:
                    act.wait_ge(shb_zero, 3)
                if q >= 2:
                    act.wait_ge(shifted, q - 1)
                act.activation(shb[q % 2][:, :, 1:SEQ + 1], src, ACT.Copy).then_inc(fm_out, 1)

            def col(base, f):
                return colB[:, base + f:base + f + 1]

            for q in range(11):
                split_to(first["rwkv"] + q + 3)
                strip_out(q)
                if q == 0:
                    act.wait_ge(shifted, 1)
                    act.activation(wg[0:LORA, 0, :], wg[0:LORA, 0, :], ACT.Tanh).then_inc(l_act, 1)
                    act.activation(wg[:, 1, :], wg[:, 1, :], ACT.Sigmoid).then_inc(l_act, 1)
                if q == 1:
                    for j in range(FT // 2):
                        act.wait_ge(z_mm, j + 1)
                        for i in range(2):
                            f = 2 * j + i
                            ins = act.activation(lwT[:, f, :], psum[:, 6, i * SEQ:(i + 1) * SEQ], ACT.Sigmoid, bias=col(B_W0, f))
                        ins.then_inc(z_ev, 1)
                        act.wait_ge(a_mm, j + 1)
                        for i in range(2):
                            f = 2 * j + i
                            ins = act.activation(aT[:, f, :], psum[:, 7, i * SEQ:(i + 1) * SEQ], ACT.Sigmoid, bias=col(B_A0, f))
                        ins.then_inc(a_ev, 1)
                if q == 2:
                    for j in range(FT // 2):
                        act.wait_ge(g_mm, j + 1)
                        act.activation(gT[:, 2 * j:2 * j + 2, :], psum[:, j, :].rearrange("p (j n) -> p j n", j=2), ACT.Copy).then_inc(g_ev, 1)
                if q == 3:
                    act.wait_ge(cs_ok, 1)
                    act.activation(eP[:], cs[:], ACT.Exp, scale=-KAPPA).then_inc(ex_ok, 1)
                    act.activation(eN[:].rearrange("p f t n -> p (f t) n"),
                                   cs[:].rearrange("p f t n -> p (f t) n")[:, :, 1:], ACT.Exp, scale=KAPPA).then_inc(ex_ok, 1)
                if q == 4:
                    act.wait_ge(ss_ev, 3)
                    act.activation(eP_sq[:], eP_sq[:], ACT.Ln).then_inc(s_act, 1)
                    act.wait_ge(s_act, 1)
                    act.activation(eP_sq[:], eP_sq[:], ACT.Exp, scale=-0.5).then_inc(ss_rt, 1)
            for f in range(FT):
                act.wait_ge(tk_mm, f + 1)
                act.activation(tk[:, :, f * P:(f + 1) * P], psum[:, 3 * (f % 2), :].rearrange("p (k n) -> p k n", k=4),
                               ACT.Copy).then_inc(tk_ev, 1)
            attention(1)
            split_to(first["rwkv"] + 11 + 3)
            act.wait_ge(sf_ok, 1)
            act.activation(sfac[:], sfac[:], ACT.Exp, scale=-KAPPA).then_inc(s_act, 1)
            act.wait_ge(s_act, 2)
            COPIES = {"S2": (2, "S2"), "S4": (0, "S4"), "S8": (2, "S8"), "F": (0, "S2"), "F2": (1, "S4"), "F4": (2, "S8")}
            def gn_root(d):
                act.wait_ge(gn_var, d + 1)
                var = normed_heads(d)[2][1]
                act.activation(var, var, ACT.Sqrt, bias=cst[:, 1:2], scale=1.0 / HD).then_inc(gn_rt, 1)

            for d, s, name in in_turn(ACT_AFTER):
                t = d // NPAIR
                f = 2 * (d % NPAIR) + s
                act.wait_ge(pm[s], step(PE_STEPS, d, ACT_AFTER[name]))
                if name == "Y":
                    src = psum[:, 4 * s:4 * s + 2, 0:HD]
                    dst = y_tok[:, t, f * P:(f + 1) * P].rearrange("p (e n) -> p e n", e=2)
                    act.activation(dst, src, ACT.Copy).then_inc(pa[s], 1)
                elif name == "S":
                    act.activation(st[:, f, :], psum[:, 4 * s + 2, 0:HD], ACT.Copy, scale=sfac[:, f:f + 1]).then_inc(pa[s], 1)
                else:
                    bank, key = COPIES[name]
                    dst = PB[s][key]
                    n = 4 if len(dst.shape) == 4 else 2
                    pat = "p a b n -> p (a b) n" if n == 4 else "p a n -> p a n"
                    act.activation(dst[:].rearrange(pat), psum[:, 4 * s + bank, 0:n * P].rearrange("p (k n) -> p k n", n=P),
                                   ACT.Copy).then_inc(pa[s], 1)
                if name == "F4" and s and d:
                    gn_root(d - 1)
            gn_root(ROUNDS - 1)
            for j in range(FT // 2):
                act.wait_ge(y_mm, j + 1)
                for i in range(2):
                    f = 2 * j + i
                    ins = act.activation(y_fin[:, f, :], psum[:, Y_BANK[j], i * SEQ:(i + 1) * SEQ], ACT.Identity,
                                         scale=col(B_LNG, f), bias=col(B_LNB, f))
                ins.then_inc(y_sc, 1)
            for j in range(FT // 2):
                act.wait_ge(y_fin_ok, j + 1)
                act.activation(xh[:, 2 * j:2 * j + 2, :], y_fin[:, 2 * j:2 * j + 2, :], ACT.Copy).then_inc(y_hi, 1)
            i = first["out", 1]
            for j in range(KD // 2):
                split_to(i + j + 3)
            post(2, i + KD // 2)
            norm(4)
            ffn(1)
            post(3, first["down", 1] + KF // 2)

        @block.vector
        def _(dve):
            chain = [0]

            def link(ins):
                chain[0] += 1
                ins.then_inc(s_dve, 1)
                dve.wait_ge(s_dve, chain[0])

            split = [0]

            def split_to(n):
                for i in range(split[0], min(n, NPIECES)):
                    dve.wait_ge(hi_done, i + 1)
                    dve.tensor_tensor(w_lo[:, i % SPL, 0:size(i)], raw[:, i % RAW, 0:size(i)], w_hi[:, i % SPL, 0:size(i)],
                                      ALU.subtract).then_inc(lo_done, 1)
                split[0] = max(split[0], min(n, NPIECES))

            def norm_start(n):
                src = hn if n == 0 else h
                if n == 0:
                    dve.wait_ge(in_mem, 16)
                elif n == 1:
                    dve.wait_ge(in_x, 16)
                    dve.wait_ge(n_tp, 4)
                if n >= 2:
                    dve.wait_ge(p_h, TT * (n - 1))
                if n:
                    dve.wait_ge(n_lo, 4 * n)
                spare = 2 if n < 2 else 6
                dve.tensor_tensor_reduce(psum[:, spare:spare + 2, :].rearrange("p b n -> p (b n)"), src[:, 1, :], src[:, 1, :], 1.0, 0.0,
                                         ALU.mult, ALU.add, ssq[:, 1:2]).then_inc(n_sqD, 1)

            def norm(n):
                src = hn if n == 0 else h
                if n < 2:
                    norm_start(n)
                for t in range(TT):
                    dve.wait_ge(n_rms, TT * n + t + 1)
                    dve.reciprocal(rin[:, t:t + 1], rms[:, t:t + 1]).then_inc(n_inv, 1)
                    if t == 0 and n >= 2:
                        norm_start(n)
                dve.wait_ge(n_inv, TT * (n + 1))
                dve.tensor_scalar(hn[:, 1, :], src[:, 1, :], rin[:, 1:2], None, ALU.mult).then_inc(n_scD, 1)

            def norm_lo(n):
                dl, dh = (ml, mh) if n == 0 else (xl, xh)
                for b in range(KD // 2):
                    dve.wait_ge(n_hi, 4 * n + b + 1)
                    for j in range(2):
                        k = 2 * b + j
                        c = NORM_COL[n] + k
                        ins = dve.scalar_tensor_tensor(dl[:, k, :], psum[:, b, j * SEQ:(j + 1) * SEQ], colA[:, c:c + 1],
                                                       dh[:, k, :], ALU.mult, ALU.subtract)
                    ins.then_inc(n_lo, 1)

            def token_out(g):
                i0 = first["mem"] if g == 0 else first["nsa"] + 2 * (g - 1)
                dve.wait_ge(used, i0 + 2)
                dst = mkv[:, 1, :] if g == 0 else pr[:, 1, 512 * (g - 1):min(512 * g, NSA_IN)]
                dve.tensor_copy(dst, psum[:, 5 + 2 * (g % 2), 0:dst.shape[1]]).then_inc(tok_evD, 1)

            def turn_out(k):
                dve.wait_ge(tp0, k + 1)
                src = psum[:, k % 4, :].rearrange("p (j n) -> p j n", j=2)
                kind, n = TURNS[2 * k]
                if k < 3:
                    dve.tensor_copy(KC[0:HD, n:n + 2, :], src[0:HD])
                    dve.tensor_copy(KC[HD:P, n:n + 2, 0:SEQ - 1], src[HD:P, :, 1:SEQ]).then_inc(tp0D, 1)
                else:
                    dst = {"dup": kT, "q": qT, "mq": mqT, "mk": mkT}[kind]
                    n = n - 6 if kind == "dup" else n
                    dve.tensor_copy(dst[:, n:n + 2, :], src).then_inc(tp0D, 1)

            def rope(a, b, cos, sin, tmp, done=None):
                dve.tensor_tensor(tmp[0], a, cos, ALU.mult)
                dve.tensor_tensor(tmp[1], b, sin, ALU.mult)
                dve.tensor_tensor(tmp[2], a, sin, ALU.mult)
                link(dve.tensor_tensor(tmp[3], b, cos, ALU.mult))
                dve.tensor_tensor(a, tmp[0], tmp[1], ALU.subtract)
                ins = dve.tensor_tensor(b, tmp[2], tmp[3], ALU.add)
                if done is None:
                    link(ins)
                else:
                    ins.then_inc(done, 1)

            def rope_heads(col, heads, tmp, done):
                v = pr[:, :, col:col + heads * HD].rearrange("p t (h d) -> p t h d", d=HD)
                tr = trig[:, 0:TT]
                cos, sin = (tr[:, :, i, :].unsqueeze(2).to_broadcast([P, TT, heads, HALF]) for i in (1, 0))
                rope(v[:, :, :, 0:HALF], v[:, :, :, HALF:ROT], cos, sin, tmp, done)

            def attention(layer):
                n = len(UNITS[layer])
                for s in range(n + LAG_V + 1):
                    if s < n:
                        u = UBASE[layer] + s
                        f, e, t, kind = UNITS[layer][s]
                        nbr, nk = branches(UNITS[layer][s])
                        dve.wait_ge(a_sc, u + 1)
                        if u >= SLOTS:
                            dve.wait_ge(a_tp, u - SLOTS + 1)
                        for b in range(nbr):
                            if kind == "nsa":
                                mask = cmask[:, (TT - 1 - t) * P:SEQ]
                            else:
                                mask = cmask[:, 0:1].to_broadcast([P, SEQ])
                            ins = dve.tensor_tensor_reduce(SM[layer][:, u % SLOTS, b, 0:nk * P], psum[:, SC_BANK[u % SLOTS], b * SEQ:b * SEQ + nk * P],
                                                           mask, 1.0, NEG, ALU.add, ALU.max, mx[:, u % SLOTS, b:b + 1])
                        link(ins)
                        dve.tensor_scalar(nbias[:, u % SLOTS, 0:nbr], mx[:, u % SLOTS, 0:nbr], -SCALE, None, ALU.mult).then_inc(a_max, 1)
                    i = s - 1
                    if 0 <= i < n:
                        u = UBASE[layer] + i
                        f, e, t, kind = UNITS[layer][i]
                        nbr, nk = branches(UNITS[layer][i])
                        dve.wait_ge(a_exp, u + 1)
                        ins = dve.reciprocal(coef[:, u % SLOTS, 0:nbr], rsum[:, u % SLOTS, 0:nbr])
                        if kind == "nsa":
                            link(ins)
                            g = 3 * (2 * f + e) + 1
                            ins = dve.tensor_tensor(coef[:, u % SLOTS, :], coef[:, u % SLOTS, :], gates[:, t, g:g + 2], ALU.mult)
                        ins.then_inc(a_coef, 1)
                    i = s - LAG_T
                    if 0 <= i < n and (UBASE[layer] + i) % 2 == 1:
                        u = UBASE[layer] + i
                        nbr, nk = branches(UNITS[layer][i])
                        dve.wait_ge(a_tp, u + 1)
                        if u >= SLOTS:
                            dve.wait_ge(a_pv, u - SLOTS + 1)
                        dve.tensor_copy(PT[layer][:, u % SLOTS, 0:nbr * nk, :],
                                        psum[:, PT_BANK[u % SLOTS], 0:nbr * nk * P].rearrange("p (k n) -> p k n", n=P)).then_inc(a_ptD, 1)
                    i = s - LAG_V
                    if 0 <= i < n and i % 4 == 3:
                        f = UNITS[layer][i][0]
                        dve.wait_ge(a_hi, f + FBASE[layer] + 1)
                        dve.tensor_tensor(xl[:, f, :], psum[:, 6 + f % 2, 0:SEQ], xh[:, f, :], ALU.subtract).then_inc(a_lo, 1)

            def post(m):
                dve.wait_ge(in_gain, 16 * (m + 1))
                for t in range(TT):
                    dve.wait_ge(p_sq, TT * m + t + 1)
                    dve.tensor_tensor(hn[:, t, :].rearrange("p (b n) -> p b n", b=2), psum[:, 4 * t + 2:4 * t + 4, :],
                                      gain[:].rearrange("p (b n) -> p b n", b=2), ALU.mult).then_inc(p_tmp, 1)
                    dve.wait_ge(p_rms, TT * m + t + 1)
                    dve.wait_ge(p_tmp, TT * m + t + 1)
                    link(dve.reciprocal(post_rin[:, t:t + 1], post_rms[:, t:t + 1]))
                    dve.scalar_tensor_tensor(h[:, t, :], hn[:, t, :], post_rin[:, t:t + 1], h[:, t, :],
                                             ALU.mult, ALU.add).then_inc(p_h, 1)

            def ffn(layer):
                u0 = NFC * layer

                def hidden_lo(c):
                    dve.wait_ge(up_hi, u0 + c + 1)
                    dve.tensor_tensor(hl[:, 2 * c:2 * c + 2, :], hid[:], hh[:, 2 * c:2 * c + 2, :],
                                      ALU.subtract).then_inc(up_lo, 1)

                for c in range(NFC):
                    i = first["up", layer] + 2 * c
                    split_to(i + 3)
                    if c:
                        hidden_lo(c - 1)
                        dve.wait_ge(up_lo, u0 + c)
                    split_to(i + 4)
                    dve.wait_ge(up_silu, u0 + c + 1)
                    dve.wait_ge(used, i + 2)
                    dve.tensor_tensor(hid[:], sg[:], psum[:, 2 * (c % 2) + 1, :].rearrange("p (j n) -> p j n", j=2),
                                      ALU.mult).then_inc(up_mul, 1)
                hidden_lo(NFC - 1)
                i0 = first["down", layer]
                for j in range(KF // 2):
                    split_to(i0 + j + 3)

            norm(0)
            dve.wait_ge(vec_tp, 1)
            dve.tensor_copy(colA[:], psum[:, 7, 0:NA])
            link(dve.tensor_copy(colB[:], psum[:, 7, P:P + NB]))
            dve.nop().then_inc(vec_ev, 1)
            split_to(1)
            norm_lo(0)
            split_to(2)
            norm(1)
            split_to(3)
            norm_lo(1)
            token_out(0)
            split_to(4)
            dve.wait_ge(in_small, 16 * 7)
            dve.wait_ge(consts, 3 + HALF)
            link(dve.tensor_copy(posf[:], posi[:]))
            shape = [P, 3, 2, HALF]
            for c in range(3):
                ins = dve.tensor_scalar(ang[:, c], invf[:], posf[:, c:c + 1], None, ALU.mult)
            link(ins)
            dve.tensor_scalar(turns[:, :, 0, :], ang[:, :, 0, :], 1.0 / (2 * np.pi), None, ALU.mult)
            link(dve.tensor_scalar(turns[:, :, 1, :], ang[:, :, 1, :], 1.0 / (2 * np.pi), 0.25, ALU.mult, ALU.add))
            link(dve.tensor_scalar(turns[:], turns[:], MAGIC, None, ALU.add))
            link(dve.tensor_scalar(turns[:], turns[:], -MAGIC, None, ALU.add))
            for part in TURN:
                link(dve.scalar_tensor_tensor(ang[:], turns[:], -float(part), ang[:], ALU.mult, ALU.add))
            link(dve.tensor_scalar(ang[:, :, 1, :], ang[:, :, 1, :], float(np.pi / 2), None, ALU.add))
            PI = float(np.nextafter(np.float32(np.pi), np.float32(0)))
            dve.tensor_scalar(ang[:], ang[:], PI, -PI, ALU.min, ALU.max).then_inc(trig_r, 1)
            for g in range(1, 6):
                i = first["nsa"] + 2 * (g - 1)
                split_to(i + 3)
                split_to(i + 4)
                token_out(g)
                if g == 4:
                    split_to(i + 5)
                    turn_out(1)
                    dve.wait_ge(tp0A, 2)
                    dve.wait_ge(tp0D, 1)
                    for kv in range(2):
                        if kv:
                            dve.wait_ge(kp_hi, 1)
                            dve.wait_ge(kp_lo, 1)
                        dst = kpf[:].rearrange("p j (g n) -> p j g n", g=GROUPS)
                        for half in range(2):
                            src = KC[:, 3 * kv:3 * kv + 3, CMP_STRIDE * half:CMP_STRIDE * (half + NCMP)].rearrange(
                                "p g (n j w) -> p j g n w", j=8, w=2)[:, :, :, :, 0]
                            col = (A_POSK, A_POSV)[kv] + 8 * half
                            ins = None
                            for gg in range(GROUPS):
                                pos = colA[:, col:col + 8].unsqueeze(2).to_broadcast([P, 8, NCMP])
                                ins = dve.tensor_tensor(dst[:, 8 * half:8 * half + 8, gg, :], src[:, :, gg, :], pos, ALU.add)
                        ins.then_inc(kp_f, 1)
                        dve.wait_ge(kp_hi, kv + 1)
                        dve.tensor_tensor(kpl[kv][:], kpf[:], kph[kv][:], ALU.subtract).then_inc(kp_lo, 1)
            i = first["cmp"]
            split_to(i + 3)
            dve.wait_ge(tok_evA, 6)
            dve.wait_ge(tok_evD, 6)
            dve.tensor_tensor(gates[:], pr[:, :, O_G:O_G + GATES], gateb[:].unsqueeze(1).to_broadcast([P, TT, GATES]),
                              ALU.add).then_inc(gl_s, 1)
            dve.wait_ge(trig_s, 1)
            small = [rt[:, 48 * k:48 * k + 48].rearrange("p (t h d) -> p t h d", t=TT, d=HALF) for k in range(4)]
            rope_heads(O_KS, GROUPS, small, roped_k)
            dve.wait_ge(roped_k, 1)
            rope_heads(O_KW, GROUPS, small, roped_k)
            split_to(i + 4)
            rope_heads(0, HEADS, [rtq[:, k] for k in range(4)], roped_q)
            turn_out(3)
            turn_out(5)
            dve.wait_ge(c_w2, 1)
            n = GROUPS * NCMP
            dve.tensor_copy(kcs[:], psum[0:n, 7, 0:HD])
            link(dve.tensor_copy(vcs[:], psum[0:NCMP, 7, HD:HD + KVW].rearrange("p (g d) -> p g d", d=HD)))
            rope(kcs[:, 0:HALF], kcs[:, HALF:ROT], trig[0:n, TT, 1, :], trig[0:n, TT, 0, :],
                 [rt[0:n, 8 * k:8 * k + 8] for k in range(4)])
            for c in range(2):
                ins = dve.tensor_copy(kcd[:, c, :], kcs[:])
            ins.then_inc(c_kd, 1)
            for k in range(7, NTURN, 2):
                turn_out(k)
            split_to(i + 7)
            for t in range(TT):
                dve.wait_ge(b_sc, t + 1)
                v = sc[:, t]
                mask = bcmask[:, t * NCMP:(t + 1) * NCMP].unsqueeze(1).to_broadcast([P, FT, NCMP])
                for e in range(2):
                    ins = dve.tensor_tensor(v.rearrange("p (f e) n -> p e f n", e=2)[:, e],
                                            psum[:, 4 + 2 * t + e, 0:FT * NCMP].rearrange("p (h n) -> p h n", n=NCMP), mask, ALU.add)
                link(ins)
                link(dve.tensor_reduce(cmx[:], v, AX.X, ALU.max))
                dve.tensor_tensor(v, v, cmx[:].unsqueeze(2).to_broadcast([P, HEADS, NCMP]), ALU.subtract).then_inc(b_sub, 1)
            dve.wait_ge(gate_s, 1)
            for t in range(TT):
                dve.wait_ge(b_exp, t + 1)
                v = sc[:, t]
                link(dve.tensor_reduce(csum[:], v, AX.X, ALU.add))
                link(dve.tensor_scalar(csum[:], csum[:], 1e-30, None, ALU.max))
                link(dve.reciprocal(csum[:], csum[:]))
                link(dve.scalar_tensor_tensor(ccf[:], csum[:], rowok[:, t:t + 1],
                                              gates[:, t, :].rearrange("p (h g) -> p h g", g=3)[:, :, 0], ALU.mult, ALU.mult))
                dve.tensor_tensor(v, v, ccf[:].unsqueeze(2).to_broadcast([P, HEADS, NCMP]), ALU.mult).then_inc(b_p, 1)
            attention(0)
            i = first["out", 0]
            for j in range(KD // 2):
                split_to(i + j + 3)
            post(0)
            norm(2)
            norm_lo(2)
            ffn(0)
            post(1)

            norm(3)
            norm_lo(3)

            def col(base, f):
                return colB[:, base + f:base + f + 1]

            def shift(q):
                dve.wait_ge(fm_out, q + 1)
                f0 = 2 * RWKV_ORDER[q]
                dst = wg if q == 0 else (rT, k_T, vT)[f0 // FT]
                j0 = 0 if q == 0 else f0 % FT
                link(dve.tensor_tensor(dst[:, j0:j0 + 2, :], shb[q % 2][:, :, 0:SEQ], shb[q % 2][:, :, 1:SEQ + 1], ALU.subtract))
                for i in range(2):
                    ins = dve.scalar_tensor_tensor(dst[:, j0 + i, :], dst[:, j0 + i, :], col(B_MU, f0 + i),
                                                   shb[q % 2][:, i, 1:SEQ + 1], ALU.mult, ALU.add)
                ins.then_inc(shifted, 1)

            flat = "p f n -> p (f n)"
            ftn = "p f (t n) -> p (f t) n"
            for q in range(10):
                split_to(first["rwkv"] + q + 3)
                shift(q)
                if q == 1:
                    dve.wait_ge(z_ev, 3)
                    for f in range(FT):
                        for t in range(TT):
                            ins = dve.tensor_tensor_scan(cs[:, f, t, 1:], cst[:, 2:3].to_broadcast([P, P]), lwT[:, f, t * P:(t + 1) * P],
                                                         0.0, ALU.mult, ALU.add)
                    link(ins)
                    link(dve.tensor_copy(mid[:], cs[:, :, :, P // 2]))
                    v = cs[:].rearrange("p f t n -> p (f t) n")
                    dve.tensor_tensor(v, v, mid[:].rearrange("p f t -> p (f t)").unsqueeze(2).to_broadcast([P, FT * TT, P + 1]),
                                      ALU.subtract).then_inc(cs_ok, 1)
                    dve.wait_ge(cs_ok, 1)
                    dve.tensor_tensor(sfac[:], cs[:, :, 0, P], mid[:, :, 1], ALU.add).then_inc(sf_ok, 1)
                if q == 3:
                    dve.wait_ge(shifted, 4)
                    for f in range(FT):
                        ins = dve.tensor_scalar(kkT[:, f, :], k_T[:, f, :], col(B_KK, f), None, ALU.mult)
                    ins.then_inc(kk_ok, 1)
                    dve.wait_ge(a_ev, 3)
                    for f in range(FT):
                        ins = dve.tensor_scalar(vT[:, f, :], aT[:, f, :], -1.0, col(B_KA, f), ALU.add, ALU.mult)
                    link(ins)
                    link(dve.scalar_tensor_tensor(k_T[:].rearrange(flat), vT[:].rearrange(flat), 1.0, k_T[:].rearrange(flat),
                                                  ALU.add, ALU.mult))
                if q == 4:
                    for j in range(FT // 2):
                        dve.wait_ge(ss_mm, j + 1)
                        dve.tensor_scalar(eP_sq[:, 2 * j:2 * j + 2, :], psum[:, j, :].rearrange("p (j n) -> p j n", j=2), 1e-24, None,
                                          ALU.max).then_inc(ss_ev, 1)
                if q == 5:
                    dve.wait_ge(ss_rt, 1)
                    link(dve.tensor_tensor(kkT[:], kkT[:], eP_sq[:], ALU.mult))
                    link(dve.tensor_tensor(aT[:], aT[:], kkT[:], ALU.mult))
                if q == 6:
                    dve.wait_ge(ex_ok, 2)
                    dve.wait_ge(shifted, 7)
                    e3 = eP[:].rearrange("p f t n -> p (f t) n")
                    for f in range(FT):
                        dve.scalar_tensor_tensor(art[:, f, :, 0, :], kkT[:, f, :].rearrange("p (t n) -> p t n", t=TT), -1.0,
                                                 eP[:, f, :, 0:P], ALU.mult, ALU.mult)
                        ins = dve.tensor_tensor(art[:, f, :, 1, :], rT[:, f, :].rearrange("p (t n) -> p t n", t=TT),
                                                eP[:, f, :, 1:], ALU.mult)
                    ins.then_inc(ar_ok, 1)
                    dve.wait_ge(ar_ok, 1)
                    for f in range(FT):
                        ins = dve.scalar_tensor_tensor(rT[:, f, :], rT[:, f, :], col(B_RK, f), k_T[:, f, :], ALU.mult, ALU.mult)
                    ins.then_inc(rk_ok, 1)
                    dve.wait_ge(rk_ok, 1)
                    en = eN[:].rearrange("p f t n -> p (f t n)")
                    dve.tensor_tensor(aT[:].rearrange(flat), aT[:].rearrange(flat), en, ALU.mult)
                    dve.tensor_tensor(k_T[:].rearrange(flat), k_T[:].rearrange(flat), en, ALU.mult).then_inc(bk_ok, 1)
            for j in range(FT // 2):
                dve.wait_ge(bo_mm, j + 1)
                dve.wait_ge(shifted, 10)
                dve.tensor_tensor(rT[:, 2 * j:2 * j + 2, :], psum[:, j, :].rearrange("p (j n) -> p j n", j=2),
                                  vT[:, 2 * j:2 * j + 2, :], ALU.mult).then_inc(bo_ev, 1)
            split_to(first["rwkv"] + 11 + 2)
            attention(1)
            split_to(first["rwkv"] + 11 + 3)
            dve.wait_ge(dm_ok, 1)

            def mask(i, n=1):
                return dmask[:, i:i + n, :].rearrange("p k n -> p (k n)").unsqueeze(1).to_broadcast([P, 2, n * P])

            def gn_mean(d):
                for s in range(2):
                    dve.wait_ge(pa[s], step(ACT_STEPS, d, "Y"))
                y3, _, st3 = normed_heads(d)
                if d >= NPAIR:
                    dve.wait_ge(gn_ok, d - NPAIR + 1)
                link(dve.tensor_reduce(st3[0], y3, AX.X, ALU.add))
                link(dve.tensor_scalar(st3[0], st3[0], 1.0 / HD, None, ALU.mult))
                dve.tensor_tensor(y3, y3, st3[0].unsqueeze(2).to_broadcast([P, 4, HD]), ALU.subtract).then_inc(gn_sub, 1)

            def gn_variance(d):
                dve.wait_ge(gn_sq, d + 1)
                _, q3, st3 = normed_heads(d)
                dve.tensor_reduce(st3[1], q3, AX.X, ALU.add).then_inc(gn_var, 1)

            def gn_scale(d):
                y3, _, st3 = normed_heads(d)
                dve.wait_ge(gn_rt, d + 1)
                link(dve.reciprocal(st3[2], st3[1]))
                dve.tensor_tensor(y3, y3, st3[2].unsqueeze(2).to_broadcast([P, 4, HD]), ALU.mult).then_inc(gn_ok, 1)

            for d, s, name in in_turn(DVE_AFTER):
                t = d // NPAIR
                b, B0 = PB[s], 4 * s

                def M(n):
                    dve.wait_ge(pm[s], step(PE_STEPS, d, n))

                def own(n):
                    dve.wait_ge(pv[s], step(DVE_STEPS, d, n))

                def uu(bank):
                    return psum[:, B0 + bank, 0:2 * HD].rearrange("p (e n) -> p e n", e=2)

                R = b["R"][:].rearrange("p e n -> p (e n)")
                if name in ("Dt", "Et"):
                    M("gram")
                    ins = dve.tensor_tensor(b["T"][:, "DE".index(name[0]), :, :], psum[:, B0 + 2:B0 + 4, 0:P],
                                            mask(4 if name == "Dt" else 5), ALU.mult)
                elif name == "D":
                    ins = dve.tensor_tensor(b["DA"][:].rearrange("p e k n -> p e (k n)"), psum[:, B0:B0 + 2, 0:2 * P], mask(0, 2), ALU.mult)
                elif name == "K":
                    ins = dve.tensor_tensor(b["KR"][:].rearrange("p e k n -> p e (k n)"), psum[:, B0:B0 + 2, 2 * P:4 * P],
                                            mask(2, 2), ALU.mult)
                elif name in ("R2", "R3", "J"):
                    M({"R2": "r2", "R3": "r3", "J": "j"}[name])
                    if name == "R2":
                        dve.wait_ge(pp[s], d + 1)
                    else:
                        own({"R3": "R2", "J": "R3"}[name])
                    bank = {"R2": 3, "R3": 1, "J": 3}[name]
                    ins = dve.tensor_tensor(R, psum[:, B0 + bank, 0:2 * P], R, ALU.add)
                elif name == "Z":
                    M("z")
                    ins = dve.tensor_copy(b["U"][0][:], psum[:, B0 + 2:B0 + 4, 0:HD])
                elif name == "U1":
                    M("uj")
                    ins = dve.tensor_copy(b["U"][1][:], uu(3))
                else:
                    after, before, bank, i, o_ = {"U2": ("uf", "U1", 0, 1, 0), "U3": ("uf2", "U2", 1, 0, 1), "U": ("uf4", "U3", 3, 1, 0)}[name]
                    M(after)
                    own(before)
                    ins = dve.tensor_tensor(b["U"][o_][:], uu(bank), b["U"][i][:], ALU.add)
                ins.then_inc(pv[s], 1)
                if s and d:
                    if name == "R2":
                        gn_mean(d - 1)
                    elif name == "Z":
                        gn_variance(d - 1)
                    elif name == "U":
                        gn_scale(d - 1)
            gn_mean(ROUNDS - 1)
            gn_variance(ROUNDS - 1)
            gn_scale(ROUNDS - 1)
            for j in range(FT // 2):
                dve.wait_ge(y_add, j + 1)
                v = y_fin[:, 2 * j:2 * j + 2, :]
                dve.tensor_tensor(v, v, gT[:, 2 * j:2 * j + 2, :], ALU.mult).then_inc(y_fin_ok, 1)
            for j in range(FT // 2):
                dve.wait_ge(y_hi, j + 1)
                dve.tensor_tensor(xl[:, 2 * j:2 * j + 2, :], y_fin[:, 2 * j:2 * j + 2, :], xh[:, 2 * j:2 * j + 2, :],
                                  ALU.subtract).then_inc(y_lo, 1)
            i = first["out", 1]
            for j in range(KD // 2):
                split_to(i + j + 3)
            post(2)
            norm(4)
            norm_lo(4)
            ffn(1)
            post(3)


_NAMES = ["x", "mem", "positions", "mem_norm_g", "w_mem_kv", "pre_mix_g", "post_mix_g", "pre_ffn_g", "post_ffn_g",
          "w_out", "w_ffn_in", "w_ffn_out", "nsa_w_in", "nsa_gate_b", "nsa_cmp_pos_k", "nsa_cmp_pos_v",
          "nsa_cmp_k_w1", "nsa_cmp_k_w2", "nsa_cmp_v_w1", "nsa_cmp_v_w2", "rwkv_w_in", "rwkv_mu", "rwkv_w0",
          "rwkv_w2", "rwkv_a0", "rwkv_a2", "rwkv_g2", "rwkv_k_k", "rwkv_k_a", "rwkv_r_k", "rwkv_ln_g", "rwkv_ln_b"]


def kernel(**inputs):
    import concourse.bacc as bacc
    from concourse.bass_utils import run_bass_kernel_spmd

    nc = bacc.Bacc("TRN2", target_bir_lowering=False, num_devices=1)
    arrays, args = {}, []
    for name in _NAMES:
        a = np.ascontiguousarray(inputs[name])
        arrays[name] = a
        args.append(nc.dram_tensor(name, a.shape, mybir.dt.from_np(a.dtype), kind="ExternalInput").ap())
    out = nc.dram_tensor("out", (1, SEQ, D), F32, kind="ExternalOutput").ap()
    trunk(nc, *args, out)
    r = run_bass_kernel_spmd(nc, [arrays], core_ids=[0])
    return r.results[0]["out"]
```
